# Optimizing a Trainium2 kernel written in Bass

```python
import jax, jax.numpy as jnp
from jax import lax
import numpy as np
import jax
import jax.numpy as jnp

D_MODEL = 1024
BATCH = 1
SEQ = 256
DEPTH = 2

POOL_WINDOWS = (2, 4, 8, 16)
POOL_GROUPS = len(POOL_WINDOWS)
POOL_GROUP_DIM = D_MODEL // POOL_GROUPS
POOL_WIDTH = POOL_GROUPS * POOL_GROUP_DIM
ATTN_GROUPS = ((128, 1), (512, 4), (2048, 16))
HEADS_PER_GROUP = 4
N_HEADS = HEADS_PER_GROUP * len(ATTN_GROUPS)
HEAD_DIM = D_MODEL // 8
ATTN_WIDTH = N_HEADS * HEAD_DIM
ATTN_OUT = HEADS_PER_GROUP * HEAD_DIM
Q_BLOCK = 64
NEG_INF = -1e30
N_BUCKETS = 32
MAX_DISTANCE = 1024
D_FF = ((8 * D_MODEL // 3 + 255) // 256) * 256
CONV_WIDTH = 3
EPS = 1e-6
SPLITS = [int(s) for s in np.cumsum([POOL_WIDTH, ATTN_WIDTH, ATTN_WIDTH, ATTN_WIDTH, D_MODEL])]
IN_WIDTH = POOL_WIDTH + 3 * ATTN_WIDTH + 2 * D_MODEL


def _rmsnorm(x, g):
    xf = x.astype(jnp.float32)
    y = xf * lax.rsqrt(jnp.mean(xf * xf, axis=-1, keepdims=True) + EPS)
    return (y * g.astype(jnp.float32)).astype(x.dtype)

def _t5_buckets(rel):
    n = -rel
    half = N_BUCKETS // 2
    ret = (n < 0).astype(np.int32) * half
    n = np.abs(n)
    max_exact = half // 2
    large = max_exact + (np.log(np.maximum(n, 1) / max_exact)
                         / np.log(MAX_DISTANCE / max_exact) * (half - max_exact)).astype(np.int32)
    large = np.minimum(large, half - 1)
    return (ret + np.where(n < max_exact, n, large)).astype(np.int32)

def _centred_mean(u, window):
    S = u.shape[1]
    c = jnp.pad(jnp.cumsum(u.astype(jnp.float32), axis=1), ((0, 0), (1, 0), (0, 0)))
    i = np.arange(S)
    lo = np.clip(i - window // 2, 0, S)
    hi = np.clip(i - window // 2 + window, 0, S)
    count = (hi - lo).astype(np.float32)
    return ((c[:, hi] - c[:, lo]) / count[None, :, None]).astype(u.dtype)

def _dilated_group(q, k, v, bias, window, dilation):
    B, S, H, Dh = q.shape
    half = window // (2 * dilation)
    offs = dilation * np.arange(-half, half + 1)
    pad = half * dilation
    k_pad = jnp.pad(k, ((0, 0), (pad, pad), (0, 0), (0, 0)))
    v_pad = jnp.pad(v, ((0, 0), (pad, pad), (0, 0), (0, 0)))
    t = np.arange(Q_BLOCK)
    scale = HEAD_DIM ** -0.5

    def block(q0):
        pos = q0 + t[:, None] + offs[None, :]
        valid = (pos >= 0) & (pos < S)
        idx = pos + pad
        kb = jnp.take(k_pad, idx, axis=1)
        vb = jnp.take(v_pad, idx, axis=1)
        qb = lax.dynamic_slice_in_dim(q, q0, Q_BLOCK, axis=1)
        logits = jnp.einsum('bqhd,bqkhd->bhqk', qb, kb,
                            preferred_element_type=jnp.float32) * scale
        logits = logits + bias.astype(jnp.float32)[None, :, None, :]
        logits = jnp.where(valid[None, None], logits, NEG_INF)
        lse = jax.nn.logsumexp(logits, axis=-1)
        p = jnp.exp(logits - lse[..., None]).astype(vb.dtype)
        o = jnp.einsum('bhqk,bqkhd->bqhd', p, vb)
        return o, lse

    starts = jnp.arange(S // Q_BLOCK, dtype=jnp.int32) * Q_BLOCK
    o, lse = lax.map(block, starts)
    o = o.transpose(1, 0, 2, 3, 4).reshape(B, S, H, Dh)
    lse = lse.transpose(1, 0, 3, 2).reshape(B, S, H)
    return o, lse

def _token_mixer(xn, w_in, w_pool, pool_scale, w_a, w_b, w_o, rel_bias):
    B, S, _ = xn.shape
    u, q, k, v, g_pool, g_attn = jnp.split(xn @ w_in, SPLITS, axis=-1)

    ug = u.reshape(B, S, POOL_GROUPS, POOL_GROUP_DIM)
    pooled = jnp.stack([_centred_mean(ug[:, :, gi], w) for gi, w in enumerate(POOL_WINDOWS)], axis=2) - ug
    pool_out = jnp.einsum('bsgc,gcd->bsgd', pooled, w_pool).reshape(B, S, POOL_WIDTH) * pool_scale

    q = q.reshape(B, S, N_HEADS, HEAD_DIM)
    k = k.reshape(B, S, N_HEADS, HEAD_DIM)
    v = v.reshape(B, S, N_HEADS, HEAD_DIM)
    outs, lses = [], []
    for gi, (window, dilation) in enumerate(ATTN_GROUPS):
        hs = slice(gi * HEADS_PER_GROUP, (gi + 1) * HEADS_PER_GROUP)
        half = window // (2 * dilation)
        buckets = _t5_buckets(dilation * np.arange(-half, half + 1))
        bias = rel_bias[buckets][:, hs].T
        o_g, lse_g = _dilated_group(q[:, :, hs], k[:, :, hs], v[:, :, hs], bias, window, dilation)
        outs.append(o_g)
        lses.append(lse_g)
    wts = jax.nn.softmax(jnp.stack(lses, axis=0), axis=0)
    attn = jnp.einsum('gbsh,gbshd->bshd', wts, jnp.stack(outs, axis=0).astype(jnp.float32))
    attn_out = attn.astype(xn.dtype).reshape(B, S, ATTN_OUT)

    merged = jax.nn.sigmoid(g_pool) * (pool_out @ w_a) + jax.nn.sigmoid(g_attn) * (attn_out @ w_b)
    return merged @ w_o

def _conv_ffn(xn, w_up, conv_w, conv_b, w_down):
    a, gval = jnp.split(xn @ w_up, 2, axis=-1)
    a = lax.conv_general_dilated(a, conv_w[:, None, :], window_strides=(1,),
                                 padding=((CONV_WIDTH // 2, CONV_WIDTH // 2),),
                                 dimension_numbers=('NWC', 'WIO', 'NWC'),
                                 feature_group_count=D_FF) + conv_b
    return (jax.nn.gelu(a) * gval) @ w_down

def first_inputs(seed: int = 0) -> dict:
    key = jax.random.key(seed)
    ks = jax.random.split(key, 16)
    f32 = jnp.float32

    def nrm(k, shape, scale):
        return jax.random.normal(k, shape, f32) * scale

    return {
        "x": nrm(ks[0], (BATCH, SEQ, D_MODEL), 1.0),
        "w_in": nrm(ks[1], (DEPTH, D_MODEL, IN_WIDTH), D_MODEL ** -0.5),
        "w_pool": nrm(ks[2], (DEPTH, POOL_GROUPS, POOL_GROUP_DIM, POOL_GROUP_DIM), POOL_GROUP_DIM ** -0.5),
        "pool_scale": 1.0 + nrm(ks[3], (DEPTH, POOL_WIDTH), 0.02),
        "w_a": nrm(ks[4], (DEPTH, POOL_WIDTH, D_MODEL), POOL_WIDTH ** -0.5),
        "w_b": nrm(ks[5], (DEPTH, ATTN_OUT, D_MODEL), ATTN_OUT ** -0.5),
        "w_o": nrm(ks[6], (DEPTH, D_MODEL, D_MODEL), D_MODEL ** -0.5),
        "norm1": 1.0 + nrm(ks[7], (DEPTH, D_MODEL), 0.02),
        "norm2": 1.0 + nrm(ks[8], (DEPTH, D_MODEL), 0.02),
        "w_up": nrm(ks[9], (DEPTH, D_MODEL, 2 * D_FF), D_MODEL ** -0.5),
        "conv_w": nrm(ks[10], (DEPTH, CONV_WIDTH, D_FF), CONV_WIDTH ** -0.5),
        "conv_b": nrm(ks[11], (DEPTH, D_FF), 0.01),
        "w_down": nrm(ks[12], (DEPTH, D_FF, D_MODEL), D_FF ** -0.5),
        "rel_bias": nrm(ks[13], (N_BUCKETS, N_HEADS), 0.2),
        "norm_f": 1.0 + nrm(ks[14], (D_MODEL,), 0.02),
    }

def first_block(x, w_in, w_pool, pool_scale, w_a, w_b, w_o, norm1, norm2,
              w_up, conv_w, conv_b, w_down, rel_bias, norm_f):
    h = x
    for layer in range(DEPTH):
        h = h + _token_mixer(_rmsnorm(h, norm1[layer]), w_in[layer], w_pool[layer], pool_scale[layer],
                             w_a[layer], w_b[layer], w_o[layer], rel_bias)
        h = h + _conv_ffn(_rmsnorm(h, norm2[layer]), w_up[layer], conv_w[layer], conv_b[layer], w_down[layer])
    return _rmsnorm(h, norm_f)


DEPTH_2 = 1

GRID_W = 64
CTX_LEN = 256
HEAD_DIM_2 = D_MODEL // 16
A_HEADS = 4
B_HEADS = 4
C_HEADS = 8
A_WIDTH = A_HEADS * HEAD_DIM_2
B_WIDTH = B_HEADS * HEAD_DIM_2
C_WIDTH = C_HEADS * HEAD_DIM_2
MIX_WIDTH = A_WIDTH + B_WIDTH + C_WIDTH
HGRN_CHUNK = 16
HGRN_F_FLOOR = 1e-20
RWKV_W_RANK = 64
RWKV_A_RANK = 64
RWKV_G_RANK = 128
RWKV_LN_EPS = 64e-5
NA_WIN_ROWS = 8
NA_WIN_COLS = 16
NA_COL_BLOCK = 16
NA_KEY_COLS = NA_COL_BLOCK + NA_WIN_COLS
ROPE_THETA = 10000.0
N_GROUPS = 4
EXPERTS_PER_GROUP = 8
TOP_K_IN_GROUP = 2
D_EXPERT = 512
NEG_INF_2 = -1e30
A_PROJ = 5 * A_WIDTH
B_PROJ = 3 * B_WIDTH + 2 * RWKV_W_RANK + 2 * RWKV_A_RANK + RWKV_G_RANK
C_PROJ = 3 * C_WIDTH
P_TOTAL = A_PROJ + B_PROJ + C_PROJ
RWKV_SPLITS = (B_WIDTH, 2 * B_WIDTH, 3 * B_WIDTH, 3 * B_WIDTH + RWKV_W_RANK, 3 * B_WIDTH + 2 * RWKV_W_RANK,
               3 * B_WIDTH + 2 * RWKV_W_RANK + RWKV_A_RANK, 3 * B_WIDTH + 2 * RWKV_W_RANK + 2 * RWKV_A_RANK)


def rms_norm(x, gain):
    xf = x.astype(jnp.float32)
    return xf * lax.rsqrt(jnp.mean(xf * xf, axis=-1, keepdims=True) + EPS) * gain.astype(jnp.float32)

def to_heads(t, n_heads):
    b, t_len, _ = t.shape
    return t.reshape(b, t_len, n_heads, HEAD_DIM_2).transpose(0, 2, 1, 3)

def chunk_gla(q, k, v, log_f, s0):
    b, h, t_len, _ = q.shape
    n = t_len // HGRN_CHUNK

    def blocks(u):
        return u.reshape(b, h, n, HGRN_CHUNK, u.shape[-1])

    q, k, v, log_f = blocks(q), blocks(k), blocks(v), blocks(log_f)
    cum = jnp.cumsum(log_f, axis=3)
    tri = jnp.tril(jnp.ones((HGRN_CHUNK, HGRN_CHUNK), dtype=bool))[:, :, None]
    diff = cum[:, :, :, :, None, :] - cum[:, :, :, None, :, :]
    decay = jnp.where(tri, jnp.exp(jnp.where(tri, diff, 0.0)), 0.0)
    scores = jnp.einsum('bhntd,bhnsd,bhntsd->bhnts', q, k, decay)
    o_intra = jnp.einsum('bhnts,bhnsv->bhntv', scores, v)
    q_in = q * jnp.exp(cum)
    k_out = k * jnp.exp(cum[:, :, :, -1:, :] - cum)
    kv = jnp.einsum('bhnsd,bhnsv->bhndv', k_out, v)
    chunk_decay = jnp.exp(cum[:, :, :, -1, :])

    def step(s, inp):
        q_c, dec_c, kv_c = inp
        o_c = jnp.einsum('bhtd,bhdv->bhtv', q_c, s)
        return s * dec_c[..., None] + kv_c, o_c

    s_fin, o_inter = lax.scan(step, s0, (jnp.moveaxis(q_in, 2, 0), jnp.moveaxis(chunk_decay, 2, 0),
                                         jnp.moveaxis(kv, 2, 0)))
    o = o_intra + jnp.moveaxis(o_inter, 0, 2)
    return o.reshape(b, h, t_len, v.shape[-1]), s_fin

def hgrn2_forget(f_pre, lb):
    f = lb + (1.0 - lb) * jax.nn.sigmoid(f_pre)
    log_f = jnp.log(jnp.maximum(f, HGRN_F_FLOOR))
    k = (1.0 - lb) * jax.nn.sigmoid(-f_pre)
    return to_heads(log_f, A_HEADS), to_heads(k, A_HEADS)

def hgrn2_mixer(p_ctx, p_lat, lb_fwd, lb_bwd, gn_gain):
    qc, ffc, fbc, ic, gc = jnp.split(p_ctx, 5, axis=-1)
    ql, ffl, fbl, il, gl = jnp.split(p_lat, 5, axis=-1)
    qc, ic, ql, il = (to_heads(t, A_HEADS) for t in (qc, ic, ql, il))
    s0 = jnp.zeros((p_lat.shape[0], A_HEADS, HEAD_DIM_2, HEAD_DIM_2), jnp.float32)

    def flip(t):
        return t[:, :, ::-1]

    lf, kf = hgrn2_forget(ffc, lb_fwd)
    oc_f, s_f = chunk_gla(qc, kf, ic, lf, s0)
    lf, kf = hgrn2_forget(ffl, lb_fwd)
    ol_f, _ = chunk_gla(ql, kf, il, lf, s_f)
    lbk, kb = hgrn2_forget(fbc, lb_bwd)
    oc_b, s_b = chunk_gla(flip(qc), flip(kb), flip(ic), flip(lbk), s0)
    lbk, kb = hgrn2_forget(fbl, lb_bwd)
    ol_b, _ = chunk_gla(flip(ql), flip(kb), flip(il), flip(lbk), s_b)

    def readout(o, g):
        o = rms_norm(o.transpose(0, 2, 1, 3), gn_gain)
        return o.reshape(g.shape) * jax.nn.silu(g)

    return readout(ol_f + flip(ol_b), gl), readout(oc_f + flip(oc_b), gc)

def centred_shift(u):
    pad = jnp.pad(u, ((0, 0), (1, 1), (0, 0)))
    return 0.5 * (pad[:, :-2] + pad[:, 2:])

def rwkv7_scan(r, w, k, v, kk, ak, s0):
    def step(s, inp):
        r_t, w_t, k_t, v_t, kk_t, ak_t = inp
        sa = jnp.einsum('bhvk,bhk->bhv', s, kk_t)
        s = s * w_t[:, :, None, :] - sa[..., None] * ak_t[:, :, None, :] + v_t[..., None] * k_t[:, :, None, :]
        return s, jnp.einsum('bhvk,bhk->bhv', s, r_t)

    xs = tuple(jnp.moveaxis(u, 1, 0) for u in (r, w, k, v, kk, ak))
    s_fin, ys = lax.scan(step, s0, xs)
    return jnp.moveaxis(ys, 0, 1), s_fin

def rwkv7_mixer(p_ctx, p_lat, mu, w0, w_up, a0, a_up, g_up, kk_scale, k_a, r_k, ln_gain, ln_bias):
    def hd(t):
        return t.reshape(t.shape[0], t.shape[1], B_HEADS, HEAD_DIM_2)

    def prep(p):
        p = p + (centred_shift(p) - p) * mu
        r, k, v, wdf, wdb, adf, adb, gd = jnp.split(p, list(RWKV_SPLITS), axis=-1)
        kk = hd(k * kk_scale)
        kk = kk / jnp.maximum(jnp.sqrt(jnp.sum(kk * kk, axis=-1, keepdims=True)), 1e-12)
        dirs = []
        for d, (wd, ad) in enumerate(((wdf, adf), (wdb, adb))):
            w = -jax.nn.softplus(-(w0[d] + jnp.tanh(wd) @ w_up[d])) - 0.5
            decay = jnp.exp(-jnp.exp(w))
            a = jax.nn.sigmoid(a0[d] + ad @ a_up[d])
            k_d = k * (1.0 + (a - 1.0) * k_a)
            dirs.append((hd(decay), hd(k_d), hd(a) * kk))
        g = jax.nn.sigmoid(gd) @ g_up
        return hd(r), hd(v), kk, dirs, g

    rc, vc, kkc, dc, gc = prep(p_ctx)
    rl, vl, kkl, dl, gl = prep(p_lat)
    s0 = jnp.zeros((p_lat.shape[0], B_HEADS, HEAD_DIM_2, HEAD_DIM_2), jnp.float32)

    def flip(t):
        return t[:, ::-1]

    (wcf, kcf, akcf), (wcb, kcb, akcb) = dc
    (wlf, klf, aklf), (wlb, klb, aklb) = dl
    yc_f, s_f = rwkv7_scan(rc, wcf, kcf, vc, kkc, akcf, s0)
    yl_f, _ = rwkv7_scan(rl, wlf, klf, vl, kkl, aklf, s_f)
    yc_b, s_b = rwkv7_scan(flip(rc), flip(wcb), flip(kcb), flip(vc), flip(kkc), flip(akcb), s0)
    yl_b, _ = rwkv7_scan(flip(rl), flip(wlb), flip(klb), flip(vl), flip(kkl), flip(aklb), s_b)

    def readout(y, r, v, k_f, k_b, g):
        mean = jnp.mean(y, axis=-1, keepdims=True)
        var = jnp.mean(jnp.square(y - mean), axis=-1, keepdims=True)
        y = ((y - mean) * lax.rsqrt(var + RWKV_LN_EPS)).reshape(g.shape) * ln_gain + ln_bias
        bonus = (jnp.sum(r * (k_f + k_b) * r_k, axis=-1, keepdims=True) * v).reshape(g.shape)
        return (y + bonus) * g

    out_lat = readout(yl_f + flip(yl_b), rl, vl, klf, klb, gl)
    out_ctx = readout(yc_f + flip(yc_b), rc, vc, kcf, kcb, gc)
    return out_lat, out_ctx

def axial_rope(t, pos_r, pos_c):
    quarter = HEAD_DIM_2 // 4
    inv = ROPE_THETA ** (-jnp.arange(quarter, dtype=jnp.float32) / quarter)
    ang = jnp.concatenate([pos_r[:, None] * inv, pos_c[:, None] * inv], axis=-1)
    cos = jnp.cos(ang)[None, :, None, :]
    sin = jnp.sin(ang)[None, :, None, :]
    t1, t2 = jnp.split(t, 2, axis=-1)
    return jnp.concatenate([t1 * cos - t2 * sin, t2 * cos + t1 * sin], axis=-1)

def neighbourhood_attention(p_ctx, p_lat, q_gain, k_gain, rpb, pos_r, pos_c, need_ctx):
    bsz, t_lat, _ = p_lat.shape
    n_ctx = p_ctx.shape[1]
    rows = t_lat // GRID_W
    win_r = min(NA_WIN_ROWS, rows)
    scale = HEAD_DIM_2 ** -0.5

    def qkv(p):
        q, k, v = jnp.split(p, 3, axis=-1)
        hd = lambda t: t.reshape(t.shape[0], t.shape[1], C_HEADS, HEAD_DIM_2)
        return rms_norm(hd(q), q_gain), rms_norm(hd(k), k_gain), hd(v)

    qc, kc, vc = qkv(p_ctx)
    ql, kl, vl = qkv(p_lat)
    ql, kl = axial_rope(ql, pos_r, pos_c), axial_rope(kl, pos_r, pos_c)
    kc_h, vc_h = kc.transpose(0, 2, 1, 3), vc.transpose(0, 2, 1, 3)

    def grid(t):
        return t.transpose(0, 2, 1, 3).reshape(bsz, C_HEADS, rows, GRID_W, HEAD_DIM_2)

    qg, kg, vg = grid(ql), grid(kl), grid(vl)
    n_cb = GRID_W // NA_COL_BLOCK
    q_col = jnp.arange(GRID_W).reshape(n_cb, NA_COL_BLOCK)
    k_start = jnp.clip(jnp.arange(n_cb) * NA_COL_BLOCK - NA_WIN_COLS // 2, 0, GRID_W - NA_KEY_COLS)
    k_col = k_start[:, None] + jnp.arange(NA_KEY_COLS)
    w_start = jnp.clip(q_col - NA_WIN_COLS // 2, 0, GRID_W - NA_WIN_COLS)
    kc3 = k_col[:, None, :]
    in_win = (kc3 >= w_start[..., None]) & (kc3 < w_start[..., None] + NA_WIN_COLS)
    col_idx = jnp.clip(kc3 - q_col[..., None] + NA_WIN_COLS - 1, 0, 2 * NA_WIN_COLS - 2)
    n_win = win_r * NA_KEY_COLS

    def one_row(r):
        r_start = jnp.clip(r - win_r // 2, 0, rows - win_r)
        k_blk = lax.dynamic_slice_in_dim(kg, r_start, win_r, axis=2)[:, :, :, k_col]
        v_blk = lax.dynamic_slice_in_dim(vg, r_start, win_r, axis=2)[:, :, :, k_col]
        q_row = lax.dynamic_index_in_dim(qg, r, axis=2, keepdims=False).reshape(
            bsz, C_HEADS, n_cb, NA_COL_BLOCK, HEAD_DIM_2)
        s_win = jnp.einsum('bhjqd,bhrjkd->bhjqrk', q_row, k_blk) * scale
        row_idx = r_start + jnp.arange(win_r) - r + NA_WIN_ROWS - 1
        bias = rpb[:, row_idx[None, None, :, None], col_idx[:, :, None, :]]
        s_win = jnp.where(in_win[:, :, None, :], s_win + bias, NEG_INF_2)
        s_ctx = jnp.einsum('bhjqd,bhld->bhjql', q_row, kc_h) * scale
        s_all = jnp.concatenate([s_win.reshape(s_win.shape[:4] + (n_win,)), s_ctx], axis=-1)
        prob = jax.nn.softmax(s_all, axis=-1)
        p_win = prob[..., :n_win].reshape(s_win.shape)
        p_ctx = prob[..., n_win:]
        o = (jnp.einsum('bhjqrk,bhrjkd->bhjqd', p_win, v_blk)
             + jnp.einsum('bhjql,bhld->bhjqd', p_ctx, vc_h))
        return o.reshape(bsz, C_HEADS, GRID_W, HEAD_DIM_2)

    o = lax.map(one_row, jnp.arange(rows))
    out_lat = o.transpose(1, 0, 3, 2, 4).reshape(bsz, t_lat, C_WIDTH)
    out_ctx = None
    if need_ctx:
        qc_h = qc.transpose(0, 2, 1, 3)
        pc = jax.nn.softmax(jnp.einsum('bhqd,bhkd->bhqk', qc_h, kc_h) * scale, axis=-1)
        out_ctx = jnp.einsum('bhqk,bhkd->bhqd', pc, vc_h).transpose(0, 2, 1, 3).reshape(bsz, n_ctx, C_WIDTH)
    return out_lat, out_ctx

def hierarchical_moe(h, w_rg, b_rg, w_re, b_re, w_gate, w_up, w_down):
    g_logits = h @ w_rg + b_rg
    g_prob = jax.nn.softmax(g_logits, axis=-1)
    g_sel = jnp.argmax(g_logits, axis=-1)
    g_w = jnp.take_along_axis(g_prob, g_sel[:, None], axis=-1)
    e_logits = (h @ w_re + b_re).reshape(-1, N_GROUPS, EXPERTS_PER_GROUP)
    e_logits = jnp.take_along_axis(e_logits, g_sel[:, None, None], axis=1)[:, 0]
    e_prob = jax.nn.softmax(e_logits, axis=-1)
    top_w, top_i = lax.top_k(e_prob, TOP_K_IN_GROUP)
    top_w = top_w / jnp.sum(top_w, axis=-1, keepdims=True) * g_w
    e_w = jnp.sum(jax.nn.one_hot(top_i, EXPERTS_PER_GROUP, dtype=jnp.float32) * top_w[..., None], axis=1)
    comb = jax.nn.one_hot(g_sel, N_GROUPS, dtype=jnp.float32)[:, :, None] * e_w[:, None, :]
    y = jnp.zeros(h.shape, jnp.float32)
    for gi in range(N_GROUPS):
        hid = jax.nn.silu(jnp.einsum('nd,edf->nef', h, w_gate[gi])) * jnp.einsum('nd,edf->nef', h, w_up[gi])
        y = y + jnp.einsum('nef,efd->nd', hid * comb[:, gi, :, None], w_down[gi])
    return y

def second_inputs(seed: int = 0) -> dict:
    key = jax.random.key(seed)
    ks = iter(jax.random.split(key, 40))
    D, G, E, F = D_MODEL, N_GROUPS, EXPERTS_PER_GROUP, D_EXPERT

    def nrm(shape, s):
        return s * jax.random.normal(next(ks), shape, jnp.float32)

    return {
        'x': nrm((BATCH, SEQ, D), 1.0),
        'c': nrm((BATCH, D), 1.0),
        'ctx': nrm((BATCH, CTX_LEN, D), 1.0),
        'c_ctx': nrm((D,), 1.0),
        'norm1_gain': 1.0 + nrm((DEPTH_2, D), 0.02),
        'norm2_gain': 1.0 + nrm((DEPTH_2, D), 0.02),
        'w_ada': nrm((DEPTH_2, D, 6 * D), 0.5 * D ** -0.5),
        'b_ada': nrm((DEPTH_2, 6 * D), 0.02),
        'w_in': nrm((DEPTH_2, D, P_TOTAL), D ** -0.5),
        'w_out': nrm((DEPTH_2, MIX_WIDTH, D), MIX_WIDTH ** -0.5),
        'hgrn_lb_logits': nrm((2, DEPTH_2, A_WIDTH), 0.5),
        'hgrn_gn_gain': 1.0 + nrm((DEPTH_2, A_HEADS, HEAD_DIM_2), 0.02),
        'rwkv_mu': jax.random.uniform(next(ks), (DEPTH_2, B_PROJ), jnp.float32, 0.0, 1.0),
        'rwkv_w0': -1.5 + nrm((DEPTH_2, 2, B_WIDTH), 0.5),
        'rwkv_w_up': nrm((DEPTH_2, 2, RWKV_W_RANK, B_WIDTH), RWKV_W_RANK ** -0.5),
        'rwkv_a0': nrm((DEPTH_2, 2, B_WIDTH), 0.1),
        'rwkv_a_up': nrm((DEPTH_2, 2, RWKV_A_RANK, B_WIDTH), RWKV_A_RANK ** -0.5),
        'rwkv_g_up': nrm((DEPTH_2, RWKV_G_RANK, B_WIDTH), RWKV_G_RANK ** -0.5),
        'rwkv_kk_scale': 0.85 + nrm((DEPTH_2, B_WIDTH), 0.02),
        'rwkv_k_a': 1.0 + nrm((DEPTH_2, B_WIDTH), 0.02),
        'rwkv_r_k': nrm((DEPTH_2, B_HEADS, HEAD_DIM_2), 0.1),
        'rwkv_ln_gain': 1.0 + nrm((DEPTH_2, B_WIDTH), 0.02),
        'rwkv_ln_bias': nrm((DEPTH_2, B_WIDTH), 0.02),
        'na_q_gain': 1.0 + nrm((DEPTH_2, HEAD_DIM_2), 0.02),
        'na_k_gain': 1.0 + nrm((DEPTH_2, HEAD_DIM_2), 0.02),
        'na_rpb': nrm((DEPTH_2, C_HEADS, 2 * NA_WIN_ROWS - 1, 2 * NA_WIN_COLS - 1), 0.1),
        'w_router_group': nrm((DEPTH_2, D, G), D ** -0.5),
        'b_router_group': nrm((DEPTH_2, G), 0.01),
        'w_router_expert': nrm((DEPTH_2, D, G * E), D ** -0.5),
        'b_router_expert': nrm((DEPTH_2, G * E), 0.01),
        'w_exp_gate': nrm((DEPTH_2, G, E, D, F), D ** -0.5),
        'w_exp_up': nrm((DEPTH_2, G, E, D, F), D ** -0.5),
        'w_exp_down': nrm((DEPTH_2, G, E, F, D), F ** -0.5),
    }

def second_block(x, c, ctx, c_ctx, norm1_gain, norm2_gain, w_ada, b_ada, w_in, w_out,
              hgrn_lb_logits, hgrn_gn_gain, rwkv_mu, rwkv_w0, rwkv_w_up, rwkv_a0, rwkv_a_up,
              rwkv_g_up, rwkv_kk_scale, rwkv_k_a, rwkv_r_k, rwkv_ln_gain, rwkv_ln_bias,
              na_q_gain, na_k_gain, na_rpb, w_router_group, b_router_group,
              w_router_expert, b_router_expert, w_exp_gate, w_exp_up, w_exp_down):
    f32 = jnp.float32
    bsz, t_lat, _ = x.shape
    n_ctx = ctx.shape[1]
    pos = jnp.arange(t_lat)
    pos_r = (pos // GRID_W).astype(f32)
    pos_c = (pos % GRID_W).astype(f32)
    lb_p = jax.nn.softmax(hgrn_lb_logits.astype(f32), axis=1)
    lower_bounds = jnp.cumsum(lb_p, axis=1) - lb_p[:, :1]
    silu_c = jax.nn.silu(c.astype(f32))
    silu_cc = jax.nn.silu(c_ctx.astype(f32))
    xl = x.astype(f32)
    xc = ctx.astype(f32)
    for layer in range(DEPTH_2):
        last = layer == DEPTH_2 - 1
        mod_l = (silu_c @ w_ada[layer] + b_ada[layer])[:, None, :]
        mod_c = (silu_cc @ w_ada[layer] + b_ada[layer])[None, None, :]
        sh1l, sc1l, g1l, sh2l, sc2l, g2l = jnp.split(mod_l, 6, axis=-1)
        sh1c, sc1c, g1c, sh2c, sc2c, g2c = jnp.split(mod_c, 6, axis=-1)
        hl = rms_norm(xl, norm1_gain[layer]) * (1.0 + sc1l) + sh1l
        hc = rms_norm(xc, norm1_gain[layer]) * (1.0 + sc1c) + sh1c
        pl = hl @ w_in[layer]
        pc = hc @ w_in[layer]
        al, bl, cl = jnp.split(pl, [A_PROJ, A_PROJ + B_PROJ], axis=-1)
        ac, bc, cc = jnp.split(pc, [A_PROJ, A_PROJ + B_PROJ], axis=-1)
        a_lat, a_ctx = hgrn2_mixer(ac, al, lower_bounds[0, layer], lower_bounds[1, layer], hgrn_gn_gain[layer])
        b_lat, b_ctx = rwkv7_mixer(bc, bl, rwkv_mu[layer], rwkv_w0[layer], rwkv_w_up[layer], rwkv_a0[layer],
                                   rwkv_a_up[layer], rwkv_g_up[layer], rwkv_kk_scale[layer], rwkv_k_a[layer],
                                   rwkv_r_k[layer], rwkv_ln_gain[layer], rwkv_ln_bias[layer])
        c_lat, c_ctxo = neighbourhood_attention(cc, cl, na_q_gain[layer], na_k_gain[layer], na_rpb[layer],
                                                pos_r, pos_c, not last)
        xl = xl + g1l * (jnp.concatenate([a_lat, b_lat, c_lat], axis=-1) @ w_out[layer])
        h2l = (rms_norm(xl, norm2_gain[layer]) * (1.0 + sc2l) + sh2l).reshape(-1, D_MODEL)
        moe_w = (w_router_group[layer], b_router_group[layer], w_router_expert[layer], b_router_expert[layer],
                 w_exp_gate[layer], w_exp_up[layer], w_exp_down[layer])
        if last:
            xl = xl + g2l * hierarchical_moe(h2l, *moe_w).reshape(xl.shape)
        else:
            xc = xc + g1c * (jnp.concatenate([a_ctx, b_ctx, c_ctxo], axis=-1) @ w_out[layer])
            h2c = (rms_norm(xc, norm2_gain[layer]) * (1.0 + sc2c) + sh2c).reshape(-1, D_MODEL)
            y = hierarchical_moe(jnp.concatenate([h2c, h2l], axis=0), *moe_w)
            xc = xc + g2c * y[:bsz * n_ctx].reshape(xc.shape)
            xl = xl + g2l * y[bsz * n_ctx:].reshape(xl.shape)
    return xl.astype(x.dtype)


def setup_inputs(seed=0):
    out = dict(first_inputs(seed))
    for name, value in second_inputs(seed + 1).items():
        if name != "x":
            out[name + "_2"] = value
    return out


def reference(
    x, w_in, w_pool, pool_scale, w_a, w_b, w_o, norm1, norm2, w_up, conv_w, conv_b, w_down,
    rel_bias, norm_f, c_2, ctx_2, c_ctx_2, norm1_gain_2, norm2_gain_2, w_ada_2, b_ada_2, w_in_2,
    w_out_2, hgrn_lb_logits_2, hgrn_gn_gain_2, rwkv_mu_2, rwkv_w0_2, rwkv_w_up_2, rwkv_a0_2,
    rwkv_a_up_2, rwkv_g_up_2, rwkv_kk_scale_2, rwkv_k_a_2, rwkv_r_k_2, rwkv_ln_gain_2,
    rwkv_ln_bias_2, na_q_gain_2, na_k_gain_2, na_rpb_2, w_router_group_2, b_router_group_2,
    w_router_expert_2, b_router_expert_2, w_exp_gate_2, w_exp_up_2, w_exp_down_2,
):
    x = first_block(
        x, w_in, w_pool, pool_scale, w_a, w_b, w_o, norm1, norm2, w_up, conv_w, conv_b, w_down,
        rel_bias, norm_f,
    )
    return second_block(
        x, c_2, ctx_2, c_ctx_2, norm1_gain_2, norm2_gain_2, w_ada_2, b_ada_2, w_in_2, w_out_2,
        hgrn_lb_logits_2, hgrn_gn_gain_2, rwkv_mu_2, rwkv_w0_2, rwkv_w_up_2, rwkv_a0_2,
        rwkv_a_up_2, rwkv_g_up_2, rwkv_kk_scale_2, rwkv_k_a_2, rwkv_r_k_2, rwkv_ln_gain_2,
        rwkv_ln_bias_2, na_q_gain_2, na_k_gain_2, na_rpb_2, w_router_group_2, b_router_group_2,
        w_router_expert_2, b_router_expert_2, w_exp_gate_2, w_exp_up_2, w_exp_down_2,
    )


_drawn_inputs = setup_inputs


def setup_inputs(seed=0):
    import zlib

    import numpy as np

    out = dict(_drawn_inputs(seed))
    spreads = {}
    factors = {'pool_scale': 3.872,
     'norm1': 3.139,
     'conv_b': 17.528,
     'rel_bias': 2.947,
     'norm1_gain_2': 7.641,
     'norm2_gain_2': 36.6,
     'b_ada_2': 2.704,
     'hgrn_gn_gain_2': 64.0,
     'rwkv_w_up_2': 32.208,
     'rwkv_a0_2': 8.0,
     'rwkv_kk_scale_2': 64.0,
     'rwkv_k_a_2': 8.0,
     'rwkv_ln_gain_2': 64.0,
     'rwkv_ln_bias_2': 64.0,
     'na_q_gain_2': 64.0,
     'na_k_gain_2': 64.0,
     'na_rpb_2': 64.0,
     'b_router_group_2': 51.848,
     'b_router_expert_2': 64.0,
     'norm2': 5.626,
     'ctx_2': 3.043,
     'c_ctx_2': 4.304,
     'rwkv_w0_2': 8.0}
    for name, (base, spread) in spreads.items():
        noise = np.random.default_rng([zlib.crc32(name.encode()), seed]).standard_normal(out[name].shape)
        drawn = base * np.exp(spread * noise) if base else spread * noise
        out[name] = jnp.asarray(drawn.astype(out[name].dtype))
    for name, factor in factors.items():
        out[name] = (out[name] * factor).astype(out[name].dtype)
    return out
```

```python
from contextlib import ExitStack

import numpy as np

import concourse.bass as bass
from concourse import mybir

F32 = mybir.dt.float32
U32 = mybir.dt.uint32
ALU = mybir.AluOpType
ACT = mybir.ActivationFunctionType
AX_X = mybir.AxisListType.X

P = 128
D = 1024
KT = D // P
S = 256
ST = S // P
DEPTH = 2
EPS = 1e-6
NEG = -1e30
SLOTS = 4
BLOCK = 4096

R_SIZE = 32584

HEADS_PER_GROUP = 4
GROUPS = ((128, 1), (512, 4), (2048, 16))
NG = len(GROUPS)
N_HEADS = HEADS_PER_GROUP * NG
HD = 128
AW = N_HEADS * HD
FF = 2816
FT = FF // P
N_BUCKETS = 32
MAX_DISTANCE = 1024
POOL_WINDOWS = (2, 4, 8, 16)
PAD = 8
UW = PAD + S + PAD
VEC_ROWS = 8 + 8 + 8 + 3 * FT + FT
V_N1, V_N2, V_PS, V_CW, V_CB = 0, 8, 16, 24, 24 + 3 * FT


def layer_plan():
    jobs = [("x1", j, "act" if j % 2 == 0 else "dve") for j in range(KT // 2)]
    jobs += [("u", j, "act") for j in range(4)]
    jobs += [("q", j, "act") for j in range(6)]
    jobs += [("k", j, "act") for j in range(6)]
    jobs += [("v", j, "act") for j in range(6)]
    for i in range(8):
        jobs.append(("gate", i, "act"))
        if i % 2 == 1 and i >= 3:
            jobs.append(("pv", (i - 3) // 2, "act"))
    jobs += [("pool", j, "act") for j in range(4)]
    jobs.append(("pv", 3, "act"))
    jobs += [("wa", j, "dve") for j in range(4)]
    jobs += [("wb", j, "dve") for j in range(4)]
    jobs += [("wo", j, "dve") for j in range(4)]
    jobs += [("x2", j, "act" if j % 2 == 0 else "dve") for j in range(KT // 2)]
    jobs += [("up", j, "dve") for j in range(FT)]
    jobs += [("down", j, "dve") for j in range(4)]
    return jobs


JOBS = layer_plan()
NJ = len(JOBS)
JOB = {(name, j): n for n, (name, j, _) in enumerate(JOBS)}
EMPTIED = {}
_count = {"act": 0, "dve": 0}
for _name, _j, _e in JOBS:
    _count[_e] += 1
    EMPTIED[(_name, _j)] = (_e, _count[_e])
N_ACT, N_DVE = _count["act"], _count["dve"]
assert NJ % 4 == 0

LAYER_BLOCKS = [("u", j, ("u", 2 * j + 1)) for j in range(2)]
LAYER_BLOCKS += [("q", j, ("q", 2 * j + 1)) for j in range(3)]
LAYER_BLOCKS += [("k", j, ("k", 2 * j + 1)) for j in range(3)]
LAYER_BLOCKS += [("v", j, ("v", 2 * j + 1)) for j in range(3)]
LAYER_BLOCKS += [("gate", j, ("gate", 2 * j + 1)) for j in range(4)]
LAYER_BLOCKS += [("pool", j, ("pool", 2 * j + 1)) for j in range(2)]
LAYER_BLOCKS += [("wa", j, ("wa", 2 * j + 1)) for j in range(2)]
LAYER_BLOCKS += [("wb", j, ("wb", 2 * j + 1)) for j in range(2)]
LAYER_BLOCKS += [("wo", j, ("wo", 2 * j + 1)) for j in range(2)]
LAYER_BLOCKS += [("up", j, ("up", 2 * j + 1)) for j in range(11)]
LAYER_BLOCKS += [("down", j, None) for j in range(6)]
NB = len(LAYER_BLOCKS)
BLK = {(name, j): n for n, (name, j, _) in enumerate(LAYER_BLOCKS)}
assert NB == 40 and NB % SLOTS == 0
QCOL, KCOL, VCOL, GCOL = D, D + AW, D + 2 * AW, D + 3 * AW


def t5_buckets(rel):
    n = -rel
    half = N_BUCKETS // 2
    ret = (n < 0).astype(np.int32) * half
    n = np.abs(n)
    exact = half // 2
    large = exact + (np.log(np.maximum(n, 1) / exact) / np.log(MAX_DISTANCE / exact) * (half - exact)).astype(np.int32)
    large = np.minimum(large, half - 1)
    return (ret + np.where(n < exact, n, large)).astype(np.int32)


def first_constants():
    hot = np.zeros((N_BUCKETS + 1, NG, 512), np.float32)
    d = np.arange(-(S - 1), S)
    for g, (window, dilation) in enumerate(GROUPS):
        half = window // (2 * dilation)
        offs = dilation * np.arange(-half, half + 1)
        bucket = dict(zip(offs.tolist(), t5_buckets(offs).tolist()))
        for i, x in enumerate(d.tolist()):
            hot[bucket.get(x, N_BUCKETS), g, i] = 1.0
        hot[N_BUCKETS, g, 2 * S - 1] = 1.0
    inv = np.zeros((len(POOL_WINDOWS), S), np.float32)
    i = np.arange(S)
    for g, w in enumerate(POOL_WINDOWS):
        inv[g] = 1.0 / (np.clip(i - w // 2 + w, 0, S) - np.clip(i - w // 2, 0, S)).astype(np.float32)
    return {
        "c_hot": hot.reshape(N_BUCKETS + 1, NG * 512),
        "c_ident": np.eye(P, dtype=np.float32),
        "c_flip": np.eye(P, dtype=np.float32)[::-1].copy(),
        "c_inv": inv,
    }


CTX = 256
T2 = S + CTX
H2 = 64
A_W = 256
B_W = 256
C_HEADS = 8
GRID_W = 64
GRID_R = S // GRID_W
WIN_COLS = 16
RPB_R, RPB_C = 15, 31
N_EXP, PER_GROUP, MG, D_EXP = 32, 8, 4, 512
QUAD = 4
SLOTS_E = P // QUAD
TURNS = N_EXP // QUAD
TURN_BLOCKS = 3 * QUAD
CH = 64
NCH = T2 // CH
LCH = S // CH
LEVELS = (1, 2, 4, 8, 16, 32, 64)
F_FLOOR = 1e-20
LN_EPS = 64e-5
DECAY = float(np.exp(-0.5))

VEC2, _r = {}, 0
for _name, _n in (("norm1_gain_2", 8), ("norm2_gain_2", 8), ("b_ada_2", 48), ("rwkv_mu_2", 9), ("rwkv_kk_scale_2", 2),
                  ("rwkv_k_a_2", 2), ("rwkv_r_k_2", 2), ("rwkv_w0_2", 4), ("rwkv_a0_2", 4), ("hgrn_lb_logits_2", 4),
                  ("c_2", 8), ("c_ctx_2", 8), ("na_q_gain_2", 1), ("na_k_gain_2", 1)):
    VEC2[_name] = (_r, _n)
    _r += _n
N_VEC2 = _r
N_VEC2_DMA = 16

BACK = (4, 7, 2, 3)
BLOCKS2 = [("w_ada_2", 512 * j, 512) for j in range(12)]
BLOCKS2 += [("w_in_2", c, n) for c, n in ((0, 512), (512, 512), (1024, 512), (1536, 512), (2048, 384),
                                          (2432, 512), (2944, 512), (3456, 512))]
N_BASE_DMA = 15
BLOCKS2 += [("w_out_2", 512 * j, 512) for j in range(2)]
ADA_ROWS = (4, 5, 10, 11)


def step_chunks(i):
    f = (4 + i) if i < 4 else i - 4
    b = (7 - i) if i < 4 else 7 - i
    return f, b


def second_plan():
    both = ("act", "dve")
    jobs = [("vec", 0, "dve")]
    jobs += [("ada", j, "dve") for j in range(12)]
    jobs += [("xl", j, both[j % 2]) for j in range(4)] + [("xc", j, both[j % 2]) for j in range(4)]
    jobs += [("aq", 0, "act")] + [("ff", j, "act") for j in range(2)] + [("fb", j, "act") for j in range(2)]
    jobs += [("ai", j, "act") for j in range(2)] + [("ag", 0, "act")]
    jobs += [("b", j, "dve") for j in range(8)]
    jobs += [("cq", j, "act") for j in range(2)] + [("ck", j, "act") for j in range(4)]
    jobs += [("cv", j, "act") for j in range(4)]
    jobs += [("kcT", j, "act") for j in range(2)] + [("hs", j, "dve") for j in range(2)]
    jobs += [("diag", t, "dve") for t in range(2)]
    for n in range(len(LEVELS)):
        jobs += [("lev", 4 * n + j, "dve") for j in range(4)]
    jobs += [("cross", j, "act") for j in range(2)] + [("ho", t, "act") for t in range(2)]
    jobs += [("nb", j, "dve") for j in range(C_HEADS)]
    jobs += [("qs", j, "dve") for j in range(6)] + [("rope", j, "dve") for j in range(4)]
    for i in range(18):
        if i < 16:
            jobs.append(("ns", i, "dve"))
        if 1 <= i < 17:
            jobs.append(("nt", i - 1, "act"))
        if i >= 2:
            jobs.append(("no", i - 2, "dve"))
    jobs += [("kn", j, "dve") for j in range(2)] + [("vt", j, "act") for j in range(2)]
    for g in range(4):
        jobs += [("wz", g, "act"), ("az", g, "act")]
        jobs += [("tk", g, "act"), ("ta", g, "act"), ("tkk", g, "act")]
        jobs += [("LT", g, "dve"), ("L1", g, "dve"), ("M2T", g, "dve"), ("NN", g, "dve")]
        for n in range(1, 6):
            jobs.append(("T1", 8 * g + n, "act"))
            if n < 5:
                jobs.append(("XU", 8 * g + n, "dve"))
            jobs.append(("XTU", 8 * g + n, "dve"))
        jobs += [("W2", g, "act"), ("G", g, "act"), ("H", g, "act"), ("PH", g, "dve"), ("PS", g, "act"), ("GT", g, "act")]
    jobs += [("st", i, "dve") for i in range(1, 7)]
    jobs += [("sa", j, "dve") for j in range(2)]
    jobs += [("y", 0, "act"), ("bon", 0, "act"), ("gg", 0, "act"), ("bT", 0, "act")]
    jobs += [("mt", j, "act") for j in range(3)]
    jobs += [("wout", j, "dve") for j in range(4)]
    jobs += [("x3", j, both[j % 2]) for j in range(4)]
    jobs += [("rt", 0, "dve"), ("pos", 0, "dve")]
    return jobs


JOBS2 = second_plan()
JOB2 = {(name, j): n for n, (name, j, _) in enumerate(JOBS2)}
assert len(JOB2) == len(JOBS2)
EMPTIED2 = {}
_count = {"act": 0, "dve": 0}
for _name, _j, _e in JOBS2:
    _count[_e] += 1
    EMPTIED2[(_name, _j)] = (_e, _count[_e])
USED2 = [("ada", j) for j in range(12)]
USED2 += [("ff", 1), ("ai", 1), ("b", 0), ("b", 4), ("b", 7), ("cq", 1), ("ck", 3), ("cv", 3), ("wout", 1), ("wout", 3)]


def second_constants():
    i = np.arange(P)
    blk = (i[:, None] // H2 == i[None, :] // H2).astype(np.float32)
    id64 = np.concatenate([np.eye(64), np.eye(64)]).astype(np.float32)
    s, t = np.arange(64)[:, None], np.arange(64)[None, :]
    masks = []
    for d in range(2):
        lt = (s < t) if d == 0 else (s > t)
        one = [lt, lt | (s == t)]
        for b in (1, 2, 4, 8, 16, 32):
            one.append(lt & (s // (2 * b) == t // (2 * b)) & (s // b != t // b))
        one.append(one[2].T)
        masks += one
    rw = np.concatenate([np.concatenate([m, m]).astype(np.float32) for m in masks], axis=1)
    base = np.concatenate([blk, id64, rw], axis=1)
    rot = np.zeros((P, P), np.float32)
    for m in range(P):
        c = m % 64
        if c < 32:
            rot[m + 32, m] = -1.0
        else:
            rot[m - 32, m] = 1.0
    pos = np.arange(S)
    inv = (np.float32(10000.0) ** (-np.arange(16, dtype=np.float32) / 16)).astype(np.float32)
    ang = np.concatenate([(pos // GRID_W).astype(np.float32)[:, None] * inv,
                          (pos % GRID_W).astype(np.float32)[:, None] * inv], axis=1)
    cos, sin = np.cos(ang).T[i % 32].astype(np.float32), np.sin(ang).T[i % 32].astype(np.float32)
    qc, kc = (i % 64)[:, None], np.arange(64)[None, :]
    w0 = np.clip(qc - WIN_COLS // 2, 0, GRID_W - WIN_COLS)
    win = np.where((kc >= w0) & (kc < w0 + WIN_COLS), 0.0, NEG).astype(np.float32)
    flip2 = np.zeros((P, P), np.float32)
    flip2[i, (i // 64) * 64 + 63 - i % 64] = 1.0
    attn = np.concatenate([rot, cos, sin, win, flip2], axis=1)
    s, t = i[:, None], i[None, :]
    hg = []
    for b in LEVELS:
        pair = (s // (2 * b) == t // (2 * b)) & (s // b != t // b)
        hg += [pair & (s < t), pair & (s > t)]
    hg = np.stack(hg, 1).astype(np.float32).reshape(P, -1)
    moe = np.zeros((P, 2 * P + SLOTS_E + S // SLOTS_E), np.float32)
    moe[:, 0:P] = i[:, None] < i[None, :]
    moe[:, P:2 * P] = 1.0
    moe[:, 2 * P:2 * P + SLOTS_E] = np.arange(SLOTS_E)
    moe[:, 2 * P + SLOTS_E:] = SLOTS_E * np.arange(S // SLOTS_E)
    return {"c2_base": base, "c2_attn": attn, "c2_levels": hg, "c2_moe": moe}


class Chain:

    def __init__(self, eng, sem):
        self.eng, self.sem, self.base, self.n = eng, sem, 0, 0

    def __call__(self, ins):
        self.n += 1
        ins.then_inc(self.sem, 1)
        self.eng.wait_ge(self.sem, self.base + self.n)


DVE_CHAIN, POOL_CHAIN, MOE_CHAIN = 36, 17, 4


def build(nc, d, out):
    ctx = ExitStack()
    with ctx:
        def sb(name, shape, dt=F32):
            return ctx.enter_context(nc.sbuf_tensor(name, shape, dt))

        def sem(name):
            return ctx.enter_context(nc.semaphore(name))

        wring = sb("wring", [P, SLOTS, BLOCK])
        h = sb("h", [P, ST, D])
        xs = sb("xs", [P, ST, D])
        ident = sb("ident", [P, P])
        stats = sb("stats", [P, 16])
        R = sb("R", [P, R_SIZE])

        at = [0]

        def part(*shape):
            n = int(np.prod(shape))
            v = R[:, at[0]:at[0] + n]
            at[0] += n
            if len(shape) == 1:
                return v
            names = "abcd"[:len(shape)]
            return v.rearrange(f"p ({' '.join(names)}) -> p {' '.join(names)}", **dict(zip(names, shape)))

        xT = part(KT, S)
        bias = part(N_HEADS, 384)
        upad = part(KT, UW)
        poolT = part(KT, S)
        mark = at[0]
        qT = part(N_HEADS, S)
        kT = part(N_HEADS, S)
        vtok = part(ST, AW)
        gate = part(2 * KT, S)
        attnT = part(HEADS_PER_GROUP, S)
        logit = part(2, NG * S)
        probT = part(2, NG * ST, S)
        poolA = part(2, UW)
        poolB = part(2, UW)
        inv = part(len(POOL_WINDOWS), S)
        cols = part(VEC_ROWS)
        rows = part(P)
        assert at[0] <= R_SIZE, at[0]
        mT = poolT
        poT = xs[:, :, :].rearrange("p t (a s) -> p (t a) s", s=S)
        act = R[:, mark:mark + FT * S].rearrange("p (f s) -> p f s", s=S)
        junk = vtok[:, 0, 0:D]
        hankel = R[:, mark:mark + N_HEADS * 384].rearrange("p (h j) -> p h j", j=384)
        hot = R[0:N_BUCKETS + 1, mark + 4608:mark + 4608 + NG * 512].rearrange("p (g j) -> p g j", j=512)
        relb = R[0:N_BUCKETS + 1, mark + 6144:mark + 6144 + N_HEADS]
        flip = R[:, mark + 6200:mark + 6328]
        tab = R[0:HEADS_PER_GROUP, mark + 6400:mark + 6400 + NG * 512].rearrange("p (g j) -> p g j", j=512)

        bank = [ctx.enter_context(nc.psum_tensor(f"bank{i}", [P, 512], F32)) for i in range(4)]
        ps_s = ctx.enter_context(nc.psum_tensor("ps_s", [P, 1024], F32))
        ps_t = ctx.enter_context(nc.psum_tensor("ps_t", [P, 1024], F32))

        tab_dram = nc.dram_tensor("bias_table", (N_HEADS, 512), F32, kind="Internal").ap()

        loaded = [sem(f"block_loaded{i}") for i in range(SLOTS)]
        const_in = sem("const_in")
        h_in = sem("h_in")
        tab_out = sem("tab_out")
        hankel_in = sem("hankel_in")
        rows_in = sem("rows_in")
        bank_full = sem("bank_full")
        down_used = sem("down_used")
        scores_full = sem("scores_full")
        probT_full = sem("probT_full")
        tab_full = sem("tab_full")
        bias_full = sem("bias_full")
        cols_full = sem("cols_full")
        act_emptied = sem("act_emptied")
        sumsq = sem("sumsq")
        rms_ready = sem("rms_ready")
        probs_ready = sem("probs_ready")
        exp_done = sem("exp_done")
        conv_mid = sem("conv_mid")
        gelu_ready = sem("gelu_ready")
        cols_ready = sem("cols_ready")
        bias_ready = sem("bias_ready")
        dve_emptied = sem("dve_emptied")
        ms_ready = sem("ms_ready")
        xs_ready = sem("xs_ready")
        neg_max = sem("neg_max")
        rsum_ready = sem("rsum_ready")
        logits_taken = sem("logits_taken")
        probT_ready = sem("probT_ready")
        layer_done = sem("layer_done")
        tab_ready = sem("tab_ready")
        relb_set = sem("relb_set")
        dve_chain = sem("dve_chain")
        pads_zero = sem("pads_zero")
        pooled = sem("pooled")
        pool_chain = sem("pool_chain")

        def slot_of(name, j):
            return BLK[(name, j)] % SLOTS

        def wait_block(eng, l, name, j):
            n = BLK[(name, j)]
            eng.wait_ge(loaded[n % SLOTS], l * (16 * NB // SLOTS) + 16 * (n // SLOTS + 1))

        def wait_full(eng, l, job):
            eng.wait_ge(bank_full, l * NJ + JOB[job] + 1)

        def wait_emptied(eng, l, job):
            who, n = EMPTIED[job]
            if who == "act":
                eng.wait_ge(act_emptied, l * N_ACT + n)
            else:
                eng.wait_ge(dve_emptied, l * N_DVE + n)

        at[0] = 0
        base = part(P + 64 + 18 * 64)
        ones_blk, id64 = base[:, 0:P], base[:, P:P + 64]
        rw_mask = base[:, P + 64:P + 64 + 18 * 64].rearrange("p (m t) -> p m t", t=64)
        cols2 = part(N_VEC2)
        gmul = part(2, D)
        lng = part(2, 64)
        lnb = part(2, 64)
        hgain = part(A_W)
        rbias = part(40)
        modT = part(32, 2)
        mulT = part(3, KT)
        csil = part(KT, 2)
        wr = part(KT, 36)
        wup = part(B_W)
        aup = part(B_W)
        gup = part(B_W)
        mixtok = part(ST, 768)
        st = part(64)
        lb = part(6, 4)
        mu2 = part(2, 9)
        kam = part(2)
        pB_r, pB_k, pB_v = part(2, S), part(2, T2), part(2, T2)
        pB_w, pB_a, pB_g = part(T2), part(T2), part(S)
        rstage = R[0:C_HEADS, at[0] - 896:at[0]].rearrange("p (r c) -> p r c", c=P)
        x_area = at[0]
        cq, ck, cv = part(4, S), part(4, T2), part(4, 512)
        attn_c = part(P + 2 * S + 64 + P)
        rot, cos, sin = attn_c[:, 0:P], attn_c[:, P:P + S], attn_c[:, P + S:P + 2 * S]
        win, flip2 = attn_c[:, P + 2 * S:P + 2 * S + 64], attn_c[:, P + 2 * S + 64:]
        a_area = at[0]
        aq = part(2, S)
        fF, fB, kF, kB = part(2, T2), part(2, T2), part(2, T2), part(2, T2)
        ai, ag = part(4, A_W), part(2, A_W)
        hg_mask = part(len(LEVELS) * 2 * P // 4).bitcast(mybir.dt.uint8).rearrange("p (m t) -> p m t", t=P)
        n = len(LEVELS) * 2 * P
        mask_stage = R[:, a_area + 2 * S:a_area + 2 * S + n]
        w_area = at[0]
        hT = part(KT, T2)
        ctxb, csb, normf, vrows = part(ST, D), part(KT, P), part(D), part(P)
        assert at[0] <= R_SIZE, at[0]
        mixT = xs[:, :, :].rearrange("p t (a s) -> p (t a) s", s=S)
        at[0] = w_area
        XS, XP = part(2, S), part(2, S)
        Qd, Kd = part(2, 2, S), part(2, 2, S)
        Ksum = part(2, S)
        AT, ATx = part(2, ST, 2, P), part(2, 2, 2, P)
        kcT, hst = part(2, ST, A_W), part(2, 2, P)
        zeros = part(S)
        ho, hsq = part(ST, A_W), part(ST, A_W)
        assert at[0] <= R_SIZE, at[0]
        IP, IS = fF[:, :, 0:S], fB[:, :, 0:S]
        at[0] = a_area
        nbias = part(C_HEADS, 6, 64)
        nhank = part(C_HEADS, 6, 64)
        nsq = part(4, T2)
        nrs = part(4, T2)
        nrot = part(4, S)
        nL, nPT = part(2, T2), part(2, 4, P)
        assert at[0] <= R_SIZE, at[0]
        at[0] = x_area
        reset = xs[:, 0, :].rearrange("p (d t) -> p d t", d=2)
        PhiT, Psi = part(4, NCH, 64), part(4, NCH, 64)
        NN = part(4, 2, LCH, 64)
        GT, Hn = part(4, LCH, 64), part(4, LCH, 64)
        rh = part(4, S)
        states = part(NCH, 4, 64)
        vtk = part(2, NCH, 64)
        kunit = part(2, T2)
        ksum = part(2, S)
        sw, aa, cc, tmp1, tmp2 = part(T2), part(T2), part(T2), part(T2), part(T2)
        kap, alp, kh = part(T2), part(T2), part(T2)
        LT = part(NCH, 64)
        X, XT, T1 = (x.rearrange("p (c t) -> p c t", t=64) for x in (aa, tmp1, tmp2))
        MT = part(NCH, 64)
        kapt, alpt, kht = part(NCH, 64), part(NCH, 64), part(NCH, 64)
        assert at[0] <= R_SIZE, (at[0], "delta")
        G, W2 = T1, MT
        M2T = sw.rearrange("p (c t) -> p c t", t=64)
        Hfull = cc.rearrange("p (c t) -> p c t", t=64)
        dend = st[:, 40:48]
        at[0] = x_area
        yb, ysq, nSA, bo, gg = part(8, 64), part(8, 64), part(4, LCH, 64), part(8), part(8, 64)
        at[0] = x_area
        h2T = part(KT, S)
        rl = part(ST, 36)
        comb = part(ST, N_EXP)
        gsel, ge, gmx = part(ST, MG), part(ST, MG), part(ST)
        esel, eg, ee, emx = part(ST, MG, PER_GROUP), part(ST, PER_GROUP), part(ST, PER_GROUP), part(ST)
        sel1, sel2, m2, order = part(ST, PER_GROUP), part(ST, PER_GROUP), part(ST), part(PER_GROUP)
        sel, posm = part(ST, N_EXP), part(ST, N_EXP)
        counts, over = part(N_EXP), part(S // SLOTS_E)
        most, sweeps_f = part(1), part(1)
        sweeps_i = part(1).bitcast(mybir.dt.int32)
        moe_c = part(2 * P + SLOTS_E + S // SLOTS_E)
        earlier, all_ones, slot_no = moe_c[:, 0:P], moe_c[:, P:2 * P], moe_c[:, 2 * P:2 * P + SLOTS_E]
        sweep_from = moe_c[:, 2 * P + SLOTS_E:]
        pcol, ccol = part(ST, QUAD), part(ST, QUAD)
        pick, put = part(ST, P), part(ST, P)
        putT = part(ST, P)
        xg = part(KT, P)
        sg, hid = part(D_EXP), part(D_EXP)
        hidT = part(D_EXP // P, P)
        yg = part(D)
        y = part(ST, D)
        ob = part(ST, D)
        assert at[0] <= R_SIZE, (at[0], "experts")

        rpb_dram = nc.dram_tensor("window_bias", (C_HEADS, 7, P), F32, kind="Internal").ap()
        banks8 = [b[:, :] for b in bank] + [ps_s[:, 0:512], ps_s[:, 512:1024], ps_t[:, 0:512], ps_t[:, 512:1024]]
        vec_in, early_in, base_in = sem("vec_in"), sem("early_in"), sem("base_in")
        rpb_in, rpb_out, nhank_in, moe_c_in, stored = sem("rpb_in"), sem("rpb_out"), sem("nhank_in"), sem("moe_c_in"), sem("stored")
        full2, moe_full, moe_used = sem("full2"), sem("moe_full"), sem("moe_used")
        act_emptied2 = sem("act_emptied2")
        csil_ready, sumsq2, rms2, shift_mid = sem("csil_ready"), sem("sumsq2"), sem("rms2"), sem("shift_mid")
        hsq_ready, hroot_ready, nsq_ready = sem("hsq_ready"), sem("hroot_ready"), sem("nsq_ready")
        nroot_ready, nprob_ready, th_ready = sem("nroot_ready"), sem("nprob_ready"), sem("th_ready")
        kroot_ready, exp_out, ysq_ready, yroot_ready = sem("kroot_ready"), sem("exp_out"), sem("ysq_ready"), sem("yroot_ready")
        gexp_out, moe_sg = sem("gexp_out"), sem("moe_sg")
        xg_act, hidT_ready, yg_act = sem("xg_act"), sem("hidT_ready"), sem("yg_act")
        dve_emptied2 = sem("dve_emptied2")
        csb_ready, lb_ready, ms2, xl_ready = sem("csb_ready"), sem("lb_ready"), sem("ms2"), sem("xl_ready")
        ctx_ready, xs2_ready, mul_ready = sem("ctx_ready"), sem("xs2_ready"), sem("mul_ready")
        kc_ready, ksum_ready, xp_ready, lev_f = sem("kc_ready"), sem("ksum_ready"), sem("xp_ready"), sem("lev_f")
        hms_ready, mixa_ready, nms_ready = sem("hms_ready"), sem("mixa_ready"), sem("nms_ready")
        qk_normed, qk_turned, nneg_ready = sem("qk_normed"), sem("qk_turned"), sem("nneg_ready")
        reset_ready, kksq_ready, kn_ready, exp_in, group_ready = sem("reset_ready"), sem("kksq_ready"), sem("kn_ready"), sem("exp_in"), sem("group_ready")
        m0_done, mt_ready, mt_next, state_ready = sem("m0_done"), sem("mt_ready"), sem("mt_next"), sem("state_ready")
        bonus_in, ycent_ready, yms_ready, yb_ready = sem("bonus_in"), sem("ycent_ready"), sem("yms_ready"), sem("yb_ready")
        h2_ready, xs3_ready, gexp_in, rt_done = sem("h2_ready"), sem("xs3_ready"), sem("gexp_in"), sem("rt_done")
        moe_hid, out_ready, sel_ready = sem("moe_hid"), sem("out_ready"), sem("sel_ready")
        disp_ready, xg_dve, yg_dve = sem("disp_ready"), sem("xg_dve"), sem("yg_dve")
        rstage_zero, fk_ready, lev_b, mask_ready = sem("rstage_zero"), sem("fk_ready"), sem("lev_b"), sem("mask_ready")

        def bank2(name, j):
            return banks8[JOB2[(name, j)] % 8]

        def wait_full2(eng, job):
            eng.wait_ge(full2, JOB2[job] + 1)

        def wait_emptied2(eng, job):
            who, n = EMPTIED2[job]
            eng.wait_ge(act_emptied2 if who == "act" else dve_emptied2, n)

        def wait_block2(eng, n):
            eng.wait_ge(loaded[n % SLOTS], 16 * (DEPTH * NB // SLOTS + n // SLOTS + 1))

        def expert_loads(sw_, tn, m):
            each = 16 * TURN_BLOCKS // SLOTS
            return sw_ * (TURNS * each) + tn * each + 16 * (DEPTH * NB // SLOTS + (len(BLOCKS2) + m) // SLOTS + 1)

        def used_by(sw_, tn, m):
            return sw_ * (TURNS * TURN_BLOCKS) + tn * TURN_BLOCKS + (SLOTS + m)

        def turn(sw_, tn, n, of):
            return sw_ * (TURNS * of) + tn * of + n

        def shift_parts(j):
            if j == 0:
                return [(pB_r[:, 0, :], 0, S, 0), (pB_r[:, 1, :], S, S, 1)]
            if j < 5:
                return [((pB_k, pB_v)[(j - 1) // 2][:, (j - 1) % 2, :], 0, T2, 1 + j)]
            return [((pB_w, pB_a, pB_g)[j - 5], 0, (T2, T2, S)[j - 5], 1 + j)]

        block = ctx.enter_context(nc.Block())

        @block.sync
        def _(sp):
            def source(l, name, j):
                w_in = d["w_in"][l].rearrange("(k p) n -> p k n", p=P)
                col = {"u": 0, "q": QCOL, "k": KCOL, "v": VCOL, "gate": GCOL}
                if name in col:
                    c = col[name] + 512 * j
                    return w_in[:, :, c:c + 512], KT
                if name == "pool":
                    return d["w_pool"][l, 2 * j:2 * j + 2].rearrange("g (k p) n -> p (g k) n", p=P), 4
                if name == "wb":
                    return d["w_b"][l].rearrange("(k p) n -> p k n", p=P)[:, :, 512 * j:512 * j + 512], 4
                if name == "down":
                    k = 4 if j < 5 else 2
                    return d["w_down"][l, 4 * j * P:(4 * j + k) * P].rearrange("(k p) n -> p k n", p=P), k
                w = {"wa": "w_a", "wo": "w_o", "up": "w_up"}[name]
                return d[w][l].rearrange("(k p) n -> p k n", p=P)[:, :, 512 * j:512 * j + 512], KT

            sp.dma_start(h[:, :, :], d["x"][0].rearrange("(t p) n -> p t n", p=P)).then_inc(h_in, 16)
            with sp.Fori(0, DEPTH) as l:
                for n, (name, j, _) in enumerate(LAYER_BLOCKS):
                    if n < 3:
                        sp.wait_ge(down_used, l * 5 + 3 + n)
                    elif n == 3:
                        sp.wait_ge(layer_done, l + 1)
                    else:
                        job = LAYER_BLOCKS[n - SLOTS][2]
                        if job is None:
                            sp.wait_ge(down_used, l * 5 + 5 + LAYER_BLOCKS[n - SLOTS][1] + 1)
                        else:
                            wait_full(sp, l, job)
                    src, k = source(l, name, j)
                    size = src.shape[2] * k
                    dst = wring[:, n % SLOTS, 0:size].rearrange("p (k n) -> p k n", k=k)
                    sp.dma_start(dst, src).then_inc(loaded[n % SLOTS], 16)


            def load2(n):
                name, c, width = BLOCKS2[n]
                dst = wring[:, n % SLOTS, 0:KT * width].rearrange("p (k n) -> p k n", k=KT)
                sp.dma_start(dst, d[name][0].rearrange("(k p) n -> p k n", p=P)[:, :, c:c + width])\
                    .then_inc(loaded[n % SLOTS], 16)

            for n in range(len(BLOCKS2)):
                if n < 3:
                    sp.wait_ge(down_used, DEPTH * 5 + 3 + n)
                elif n == 3:
                    sp.wait_ge(layer_done, DEPTH + 1)
                else:
                    wait_full2(sp, USED2[n - SLOTS])
                load2(n)

            gates_d = [d[x].rearrange("a g e k n -> (a g e) k n") for x in ("w_exp_gate_2", "w_exp_up_2", "w_exp_down_2")]

            for n in range(len(BLOCKS2) - SLOTS, len(BLOCKS2)):
                wait_full2(sp, USED2[n])

            def load_turn(sw_, tn):
                for m in range(TURN_BLOCKS):
                    u, which = (m // 2, m % 2) if m < 2 * QUAD else (m - 2 * QUAD, 2)
                    s = (len(BLOCKS2) + m) % SLOTS
                    sp.wait_ge(moe_used, used_by(sw_, tn, m - SLOTS + 1))
                    sp.dma_start(wring[:, s, :].rearrange("p (k n) -> p k n", k=(KT, KT, D_EXP // P)[which]),
                                 gates_d[which][tn * QUAD + u].rearrange("(k p) n -> p k n", p=P)).then_inc(loaded[s], 16)

            with sp.Fori(0, TURNS) as tn:
                load_turn(0, tn)
            sp.wait_ge(rt_done, 1)
            n = sp.value_load(sweeps_i[0:1, 0:1], min_val=1, max_val=S // SLOTS_E)
            with sp.If(n > 1):
                with sp.Fori(1, n) as sw_:
                    with sp.Fori(0, TURNS) as tn:
                        load_turn(sw_, tn)
            for t in range(ST):
                sp.wait_ge(out_ready, t + 1)
                sp.dma_start(out[0, t * P:(t + 1) * P, :], ob[:, t, :]).then_inc(stored, 16)
            sp.wait_ge(stored, 16 * ST)

        @block.tensor
        def _(pe):
            def w(name, j, k, n):
                return wring[:, slot_of(name, j), 0:k * n].rearrange("p (k n) -> p k n", k=k)

            pe.wait_ge(const_in, 80)
            pe.wait_ge(relb_set, 2)
            for g in range(NG):
                mm = pe.matmul(bank[g][0:HEADS_PER_GROUP, :], relb[:, 4 * g:4 * g + 4], hot[:, g, :],
                               start=True, stop=True)
            mm.then_inc(tab_full, 1)
            pe.wait_ge(hankel_in, 16)
            pe.wait_ge(tab_ready, 1)
            for i in range(N_HEADS):
                if i >= 4:
                    pe.wait_ge(bias_ready, i - 3)
                pe.matmul(bank[i % 4][:, 0:384], flip, hankel[:, i, :], start=True, stop=True).then_inc(bias_full, 1)
            pe.wait_ge(bias_ready, N_HEADS)
            pe.nop().then_inc(down_used, 5)

            with pe.Fori(0, DEPTH) as l:
                def begin(name, j):
                    n = JOB[(name, j)]
                    if n >= 4:
                        wait_emptied(pe, l, JOBS[n - 4][:2])
                    return bank[n % 4]

                def x_job(name, j):
                    b = begin(name, j)
                    for kk in range(2):
                        for t in range(ST):
                            mm = pe.transpose(b[:, kk * S + t * P:kk * S + t * P + P],
                                              xs[:, t, (2 * j + kk) * P:(2 * j + kk + 1) * P], ident[:, :])
                    mm.then_inc(bank_full, 1)

                def rows_of(name, j, c0, c1, blk, k, n, rhs, rk0=0, wk0=0):
                    b = begin(name, j)
                    ww = w(blk[0], blk[1], k, n)
                    for i, c in enumerate((c0, c1)):
                        for kk in range(rhs[1]):
                            mm = pe.matmul(b[:, i * S:(i + 1) * S], ww[:, wk0 + kk, c:c + P],
                                           rhs[0][:, rk0 + kk, :], start=kk == 0, stop=kk == rhs[1] - 1)
                    mm.then_inc(bank_full, 1)

                def scores(i):
                    hh, t = i // 2, i % 2
                    if i:
                        pe.wait_ge(logits_taken, l * 8 + i)
                    for g in range(NG):
                        hd = g * HEADS_PER_GROUP + hh
                        mm = pe.matmul(ps_s[:, g * S:(g + 1) * S], qT[:, hd, t * P:(t + 1) * P], kT[:, hd, :],
                                       start=True, stop=True)
                    mm.then_inc(scores_full, 1)

                def turn_probs(i):
                    pe.wait_ge(probs_ready, l * 8 + i + 1)
                    if i:
                        pe.wait_ge(probT_ready, l * 8 + i)
                    for k in range(NG * ST):
                        mm = pe.transpose(ps_t[:, k * P:(k + 1) * P], logit[:, i % 2, k * P:(k + 1) * P], ident[:, :])
                    mm.then_inc(probT_full, 1)

                def pv(hh):
                    pe.wait_ge(probT_ready, l * 8 + 2 * hh + 2)
                    b = begin("pv", hh)
                    for g in range(NG):
                        hd = g * HEADS_PER_GROUP + hh
                        for t in range(ST):
                            mm = pe.matmul(b[:, 0:S], vtok[:, t, hd * HD:(hd + 1) * HD], probT[:, hh % 2, g * ST + t, :],
                                           start=g == 0 and t == 0, stop=g == NG - 1 and t == ST - 1)
                    mm.then_inc(bank_full, 1)

                pe.wait_ge(rows_in, l * 80 + 80)
                pe.transpose(ps_t[:, 0:VEC_ROWS], rows[0:VEC_ROWS, :], ident[0:VEC_ROWS, 0:VEC_ROWS]).then_inc(cols_full, 1)

                pe.wait_ge(xs_ready, l * 4 + 2)
                for j in range(4):
                    x_job("x1", j)
                wait_emptied(pe, l, ("x1", 2))
                wait_emptied(pe, l, ("x1", 3))
                for name, nb in (("u", 2), ("q", 3), ("k", 3)):
                    for bl in range(nb):
                        wait_block(pe, l, name, bl)
                        for i in range(2):
                            rows_of(name, 2 * bl + i, i * S, i * S + P, (name, bl), KT, 512, (xT, KT))
                for bl in range(3):
                    wait_block(pe, l, "v", bl)
                    for t in range(ST):
                        b = begin("v", 2 * bl + t)
                        for k in range(KT):
                            mm = pe.matmul(b[:, :], xT[:, k, t * P:(t + 1) * P], w("v", bl, KT, 512)[:, k, :],
                                           start=k == 0, stop=k == KT - 1)
                        mm.then_inc(bank_full, 1)
                wait_emptied(pe, l, ("v", 5))
                for i in range(8):
                    scores(i)
                    if i % 2 == 0:
                        wait_block(pe, l, "gate", i // 2)
                    rows_of("gate", i, (i % 2) * S, (i % 2) * S + P, ("gate", i // 2), KT, 512, (xT, KT))
                    if i:
                        turn_probs(i - 1)
                    if i % 2 == 1 and i >= 3:
                        pv((i - 3) // 2)
                turn_probs(7)
                pe.wait_ge(pooled, l + 1)
                for g in range(4):
                    if g % 2 == 0:
                        wait_block(pe, l, "pool", g // 2)
                    rows_of("pool", g, 0, P, ("pool", g // 2), 4, S, (poolT, 2), rk0=2 * g, wk0=2 * (g % 2))
                pv(3)
                wait_emptied(pe, l, ("pool", 3))
                for j in range(4):
                    if j % 2 == 0:
                        wait_block(pe, l, "wa", j // 2)
                    rows_of("wa", j, (j % 2) * S, (j % 2) * S + P, ("wa", j // 2), KT, 512, (poT, KT))
                wait_emptied(pe, l, ("pv", 3))
                for j in range(4):
                    if j % 2 == 0:
                        wait_block(pe, l, "wb", j // 2)
                    rows_of("wb", j, (j % 2) * S, (j % 2) * S + P, ("wb", j // 2), 4, 512, (attnT, HEADS_PER_GROUP))
                wait_emptied(pe, l, ("wb", 3))
                for j in range(4):
                    half, t = j // 2, j % 2
                    if t == 0:
                        wait_block(pe, l, "wo", half)
                    b = begin("wo", j)
                    for k in range(KT):
                        mm = pe.matmul(b[:, :], mT[:, k, t * P:(t + 1) * P], w("wo", half, KT, 512)[:, k, :],
                                       start=k == 0, stop=k == KT - 1)
                    mm.then_inc(bank_full, 1)
                pe.wait_ge(xs_ready, l * 4 + 4)
                for j in range(4):
                    x_job("x2", j)
                wait_emptied(pe, l, ("x2", 2))
                wait_emptied(pe, l, ("x2", 3))
                for j in range(FT):
                    if j % 2 == 0:
                        wait_block(pe, l, "up", j // 2)
                    rows_of("up", j, (j % 2) * S, (j % 2) * S + P, ("up", j // 2), KT, 512, (xT, KT))
                wait_emptied(pe, l, ("up", FT - 1))
                for bl in range(6):
                    wait_block(pe, l, "down", bl)
                    nk = 4 if bl < 5 else 2
                    for j in range(4):
                        half, t = j // 2, j % 2
                        for kk in range(nk):
                            k = 4 * bl + kk
                            mm = pe.matmul(bank[JOB[("down", j)] % 4][:, :], act[:, k, t * P:(t + 1) * P],
                                           w("down", bl, nk, D)[:, kk, half * 512:(half + 1) * 512],
                                           start=k == 0, stop=k == FT - 1)
                        if bl == 5:
                            mm.then_inc(bank_full, 1)
                        elif j == 3:
                            mm.then_inc(down_used, 1)


            def fill(name, j):
                n = JOB2[(name, j)]
                assert n == done2[0], (name, j, JOBS2[done2[0]])
                done2[0] += 1
                if n >= 8:
                    wait_emptied2(pe, JOBS2[n - 8][:2])
                return bank2(name, j)

            done2 = [0]

            def w2(n, c0=0, c1=512):
                cols_n = BLOCKS2[n][2]
                return wring[:, n % SLOTS, 0:KT * cols_n].rearrange("p (k n) -> p k n", k=KT)[:, :, c0:c1]

            def channels(name, j, n, tiles, width, o=0):
                b = fill(name, j)
                for i, c in enumerate(tiles):
                    for k in range(KT):
                        mm = pe.matmul(b[:, i * width:(i + 1) * width], w2(n)[:, k, c:c + P] if BLOCKS2[n][2] == 512 else
                                       w2(n, 0, 384)[:, k, c:c + P], hT[:, k, o:o + width], start=k == 0, stop=k == KT - 1)
                mm.then_inc(full2, 1)

            def tokens(name, j, n, toks, c0, c1):
                b = fill(name, j)
                width = c1 - c0
                for i, t in enumerate(toks):
                    for k in range(KT):
                        mm = pe.matmul(b[:, i * width:(i + 1) * width], hT[:, k, t * P:(t + 1) * P],
                                       w2(n)[:, k, c0:c1], start=k == 0, stop=k == KT - 1)
                mm.then_inc(full2, 1)

            def turn4(name, j, src):
                b = fill(name, j)
                for kk_ in range(2):
                    for t in range(ST):
                        mm = pe.transpose(b[:, kk_ * S + t * P:kk_ * S + t * P + P], src(2 * j + kk_, t), ident[:, :])
                mm.then_inc(full2, 1)

            def heads64(b, chunks, lhs, rhs, start=True, stop=True, out=None, skip=False):
                for c in chunks:
                    for hd in range(2):
                        q = slice(64 * hd, 64 * hd + 64)
                        o = c if out is None else out(c)
                        mm = pe.matmul(b[q, 64 * o:64 * o + 64], lhs(q, c), rhs(q, c), start=start, stop=stop,
                                       skip_group_check=skip)
                return mm

            pe.wait_ge(vec_in, 16 * N_VEC2_DMA)
            b = fill("vec", 0)
            pe.transpose(b[:, 0:N_VEC2], vrows[0:N_VEC2, :], ident[0:N_VEC2, 0:N_VEC2]).then_inc(full2, 1)
            pe.wait_ge(csb_ready, 1)
            for n in range(12):
                wait_block2(pe, n)
                b = fill("ada", n)
                if n in ADA_ROWS:
                    for k in range(KT):
                        mm = pe.matmul(b[:, :], csb[:, k, :], w2(n)[:, k, :], start=k == 0, stop=k == KT - 1)
                else:
                    for i in range(4):
                        for k in range(KT):
                            mm = pe.matmul(b[:, 2 * i:2 * i + 2], w2(n)[:, k, i * P:(i + 1) * P], csil[:, k, :],
                                           start=k == 0, stop=k == KT - 1)
                mm.then_inc(full2, 1)
            pe.wait_ge(xs2_ready, 2)
            for j in range(4):
                turn4("xl", j, lambda k, t: xs[:, t, k * P:(k + 1) * P])
            pe.wait_ge(ctx_ready, 2)
            for j in range(4):
                turn4("xc", j, lambda k, t: ctxb[:, t, k * P:(k + 1) * P])
            wait_emptied2(pe, ("xc", 2))
            wait_emptied2(pe, ("xc", 3))
            wait_block2(pe, 12)
            channels("aq", 0, 12, (0, P), S)
            channels("ff", 0, 12, (2 * P,), T2)
            channels("ff", 1, 12, (3 * P,), T2)
            wait_block2(pe, 13)
            channels("fb", 0, 13, (0,), T2)
            channels("fb", 1, 13, (P,), T2)
            for j in range(2):
                tokens("ai", j, 13, (2 * j, 2 * j + 1), 2 * P, 4 * P)
            wait_block2(pe, 14)
            tokens("ag", 0, 14, (0, 1), 0, 2 * P)
            channels("b", 0, 14, (2 * P, 3 * P), S)
            wait_block2(pe, 15)
            for j in range(4):
                channels("b", 1 + j, 15, (j * P,), T2)
            wait_block2(pe, 16)
            channels("b", 5, 16, (0,), T2)
            channels("b", 6, 16, (P,), T2)
            channels("b", 7, 16, (2 * P,), S)
            wait_block2(pe, 17)
            channels("cq", 0, 17, (0, P), S)
            channels("cq", 1, 17, (2 * P, 3 * P), S)
            wait_block2(pe, 18)
            for j in range(4):
                channels("ck", j, 18, (j * P,), T2)
            wait_block2(pe, 19)
            for j in range(4):
                tokens("cv", j, 19, (j,), 0, 512)

            pe.wait_ge(kc_ready, 2)
            for dr in range(2):
                b = fill("kcT", dr)
                for t in range(ST):
                    for pr in range(2):
                        mm = pe.transpose(b[:, t * A_W + pr * P:t * A_W + (pr + 1) * P], Kd[:, dr, pr, t * P:(t + 1) * P],
                                          ident[:, :])
                mm.then_inc(full2, 1)
            for dr in range(2):
                wait_emptied2(pe, ("kcT", dr))
                b = fill("hs", dr)
                for pr in range(2):
                    for t in range(ST):
                        mm = pe.matmul(b[:, pr * P:(pr + 1) * P], kcT[:, dr, t, pr * P:(pr + 1) * P],
                                       ai[:, 2 + t, pr * P:(pr + 1) * P], start=t == 0, stop=t == ST - 1)
                mm.then_inc(full2, 1)

            def level(name, j, par, parts):
                b = fill(name, j)
                q = slice(64 * par, 64 * par + 64)
                for i, (q_of, k_of, pr, ts, tq) in enumerate(parts):
                    mm = pe.matmul(b[:, i * P:(i + 1) * P], k_of[q, pr, ts * P:(ts + 1) * P],
                                   q_of[q, pr, tq * P:(tq + 1) * P], start=True, stop=True)
                mm.then_inc(full2, 1)

            pe.wait_ge(ksum_ready, 1)
            for par in range(2):
                level("diag", par, par, [(aq, Ksum, pr, t, t) for t in range(ST) for pr in range(2)])
            for n in range(len(LEVELS)):
                for dr in range(2):
                    pe.wait_ge((lev_f, lev_b)[dr], n + 1)
                    for par in range(2):
                        level("lev", 4 * n + 2 * dr + par, par,
                              [(Qd[:, dr, :, :], Kd[:, dr, :, :], pr, t, t) for t in range(ST) for pr in range(2)])
            for dr in range(2):
                pe.wait_ge((lev_f, lev_b)[dr], len(LEVELS) + 1)
            for par in range(2):
                level("cross", par, par, [(Qd[:, dr, :, :], Kd[:, dr, :, :], pr, dr, 1 - dr)
                                          for dr in range(2) for pr in range(2)])
            for dr in range(2):
                pe.wait_ge((lev_f, lev_b)[dr], len(LEVELS) + 2)
            wait_emptied2(pe, ("hs", 1))
            wait_emptied2(pe, ("lev", 4 * len(LEVELS) - 1))
            wait_emptied2(pe, ("cross", 1))
            for t in range(ST):
                b = fill("ho", t)
                for pr in range(2):
                    for dr in range(2):
                        pe.matmul(b[:, pr * P:(pr + 1) * P], Qd[:, dr, pr, t * P:(t + 1) * P], hst[:, dr, pr, :],
                                  start=dr == 0, stop=False, skip_group_check=True)
                    for hd in (2 * pr, 2 * pr + 1):
                        o = b[:, hd * 64:hd * 64 + 64]
                        pe.matmul(o, AT[:, hd % 2, t, pr, :], ai[:, t, hd * 64:hd * 64 + 64], start=False, stop=False,
                                  skip_group_check=True)
                        mm = pe.matmul(o, ATx[:, hd % 2, 1 - t, pr, :], ai[:, 1 - t, hd * 64:hd * 64 + 64], start=False,
                                       stop=True, skip_group_check=True)
                mm.then_inc(full2, 1)

            pe.wait_ge(nhank_in, 16 * 12)
            for j in range(C_HEADS):
                b = fill("nb", j)
                pe.matmul(b[:, 0:384], flip2, nhank[:, j, :, :].rearrange("p r c -> p (r c)"), start=True, stop=True)\
                    .then_inc(full2, 1)
            pe.wait_ge(nsq_ready, 1)
            for j in range(2):
                b = fill("qs", j)
                pe.matmul(b[:, :], ones_blk, nrot[:, 2 * j:2 * j + 2, :], start=True, stop=True).then_inc(full2, 1)
            wait_emptied2(pe, ("qs", 1))
            pe.wait_ge(nsq_ready, 2)
            for j in range(4):
                b = fill("qs", 2 + j)
                pe.matmul(b[:, :], ones_blk, nsq[:, j, :], start=True, stop=True).then_inc(full2, 1)
            pe.wait_ge(qk_normed, 2)
            for j in range(4):
                src = (cq, cq, ck, ck)[j]
                b = fill("rope", j)
                for i in range(2):
                    mm = pe.matmul(b[:, i * S:(i + 1) * S], rot, src[:, 2 * (j % 2) + i, 0:S], start=True, stop=True)
                mm.then_inc(full2, 1)
            pe.wait_ge(qk_turned, 1)
            for i in range(18):
                if i < 16:
                    hd, t = i // 2, i % 2
                    q = slice(64 * (hd % 2), 64 * (hd % 2) + 64)
                    b = fill("ns", i)
                    pe.matmul(b[:, :], cq[q, hd // 2, t * P:(t + 1) * P], ck[q, hd // 2, :], start=True, stop=True)\
                        .then_inc(full2, 1)
                if 1 <= i < 17:
                    b = fill("nt", i - 1)
                    pe.wait_ge(nprob_ready, i)
                    for k in range(4):
                        mm = pe.transpose(b[:, k * P:(k + 1) * P], nL[:, (i - 1) % 2, k * P:(k + 1) * P], ident[:, :])
                    mm.then_inc(full2, 1)
                if i >= 2:
                    hd = (i - 2) // 2
                    b = fill("no", i - 2)
                    wait_emptied2(pe, ("nt", i - 2))
                    for k in range(4):
                        mm = pe.matmul(b[:, 0:64], nPT[:, i % 2, k, :], cv[:, k, hd * 64:hd * 64 + 64],
                                       start=k == 0, stop=k == 3)
                    mm.then_inc(full2, 1)

            idn = lambda q, c: ident[q, q]
            ck_ = lambda v: lambda q, c: v[q, 64 * c:64 * c + 64]
            cc_ = lambda v: lambda q, c: v[q, c, :]
            every, lat = range(NCH), range(LCH)
            pe.wait_ge(kksq_ready, 1)
            for pr in range(2):
                b = fill("kn", pr)
                pe.matmul(b[:, :], ones_blk, (tmp1, tmp2)[pr], start=True, stop=True).then_inc(full2, 1)
            for pr in range(2):
                b = fill("vt", pr)
                heads64(b, every, lambda q, c: pB_v[q, pr, 64 * c:64 * c + 64], idn).then_inc(full2, 1)
            pe.wait_ge(th_ready, 1)
            for g in range(4):
                dr, pr = g // 2, g % 2
                q = slice(64 * dr, 64 * dr + 64)
                b = fill("wz", g)
                pe.matmul(b[:, :], wup[q, pr * P:(pr + 1) * P], pB_w[q, :], start=True, stop=True).then_inc(full2, 1)
                b = fill("az", g)
                pe.matmul(b[:, :], aup[q, pr * P:(pr + 1) * P], pB_a[q, :], start=True, stop=True).then_inc(full2, 1)
                pe.wait_ge(group_ready, g + 1)
                for name, src in (("tk", kap), ("ta", aa), ("tkk", tmp1)):
                    b = fill(name, g)
                    heads64(b, every, ck_(src), idn).then_inc(full2, 1)
                b = fill("LT", g)
                heads64(b, every, ck_(alp), ck_(kap)).then_inc(full2, 1)
                b = fill("L1", g)
                heads64(b, every, ck_(kap), ck_(alp)).then_inc(full2, 1)
                b = fill("M2T", g)
                heads64(b, every, ck_(kh), ck_(kap)).then_inc(full2, 1)
                b = fill("NN", g)
                rg = rh[:, g, :]
                heads64(b, lat, ck_(alp), ck_(rg))
                heads64(b, lat, ck_(kh), ck_(rg), out=lambda c: c + LCH).then_inc(full2, 1)
                for n in range(1, 6):
                    pe.wait_ge(mt_ready, 5 * g + n)
                    b = fill("T1", 8 * g + n)
                    heads64(b, every, cc_(MT), cc_(X)).then_inc(full2, 1)
                    wait_emptied2(pe, ("T1", 8 * g + n))
                    if n < 5:
                        b = fill("XU", 8 * g + n)
                        heads64(b, every, cc_(XT), cc_(T1)).then_inc(full2, 1)
                    b = fill("XTU", 8 * g + n)
                    heads64(b, every, cc_(T1), cc_(XT)).then_inc(full2, 1)
                wait_emptied2(pe, ("M2T", g))
                b = fill("W2", g)
                heads64(b, every, cc_(M2T), cc_(vtk[:, pr, :, :])).then_inc(full2, 1)
                wait_emptied2(pe, ("XTU", 8 * g + 5))
                b = fill("G", g)
                heads64(b, every, cc_(XT), cc_(kapt)).then_inc(full2, 1)
                wait_emptied2(pe, ("W2", g))
                b = fill("H", g)
                heads64(b, every, cc_(XT), cc_(W2)).then_inc(full2, 1)
                wait_emptied2(pe, ("G", g))
                b = fill("PH", g)
                heads64(b, every, cc_(G), cc_(alpt)).then_inc(full2, 1)
                wait_emptied2(pe, ("H", g))
                b = fill("PS", g)
                for c in every:
                    for hd in range(2):
                        q = slice(64 * hd, 64 * hd + 64)
                        pe.matmul(b[q, 64 * c:64 * c + 64], kht[q, c, :], vtk[q, pr, c, :], start=True, stop=False)
                        mm = pe.matmul(b[q, 64 * c:64 * c + 64], alpt[q, c, :], Hfull[q, c, :], start=False, stop=True)
                mm.then_inc(full2, 1)
                b = fill("GT", g)
                heads64(b, lat, cc_(kapt), cc_(XT)).then_inc(full2, 1)
            wait_emptied2(pe, ("GT", 3))
            pe.wait_ge(state_ready, 1)
            for i in range(1, 7):
                b = fill("st", i)
                for g in range(4):
                    c = step_chunks(i)[g // 2]
                    for hd in range(2):
                        q = slice(64 * hd, 64 * hd + 64)
                        mm = pe.matmul(b[q, 64 * g:64 * g + 64], PhiT[q, g, c, :], states[q, i, g, :], start=True, stop=True)
                mm.then_inc(full2, 1)
                wait_emptied2(pe, ("st", i))
            for dr in range(2):
                b = fill("sa", dr)
                for pr in range(2):
                    g = 2 * dr + pr
                    for c in lat:
                        i = 4 + (c if dr == 0 else 3 - c)
                        for hd in range(2):
                            q = slice(64 * hd, 64 * hd + 64)
                            o = 64 * (LCH * pr + c)
                            mm = pe.matmul(b[q, o:o + 64], GT[q, g, c, :], states[q, i, g, :], start=True, stop=True)
                mm.then_inc(full2, 1)
            wait_emptied2(pe, ("sa", 1))
            b = fill("y", 0)
            for pr in range(2):
                for c in lat:
                    for hd in range(2):
                        q = slice(64 * hd, 64 * hd + 64)
                        o = b[q, 64 * (LCH * pr + c):64 * (LCH * pr + c) + 64]
                        for dr in range(2):
                            g = 2 * dr + pr
                            i = 4 + (c if dr == 0 else 3 - c)
                            pe.matmul(o, rh[q, g, 64 * c:64 * c + 64], states[q, i, g, :], start=dr == 0, stop=False)
                            pe.matmul(o, NN[q, g, 1, c, :], vtk[q, pr, c, :], start=False, stop=False)
                            mm = pe.matmul(o, NN[q, g, 0, c, :], nSA[q, g, c, :], start=False, stop=dr == 1)
            mm.then_inc(full2, 1)
            pe.wait_ge(bonus_in, 1)
            b = fill("bon", 0)
            for pr in range(2):
                for c in lat:
                    for hd in range(2):
                        q = slice(64 * hd, 64 * hd + 64)
                        o = LCH * pr + c
                        mm = pe.matmul(b[q, o:o + 1], ksum[q, pr, 64 * c:64 * c + 64], ones_blk[q, 64 * hd:64 * hd + 1],
                                       start=True, stop=True)
            mm.then_inc(full2, 1)
            b = fill("gg", 0)
            for pr in range(2):
                for c in lat:
                    for hd in range(2):
                        q = slice(64 * hd, 64 * hd + 64)
                        o = 64 * (LCH * pr + c)
                        mm = pe.matmul(b[q, o:o + 64], pB_g[:, 64 * c:64 * c + 64],
                                       gup[:, (2 * pr + hd) * 64:(2 * pr + hd) * 64 + 64], start=True, stop=True)
            mm.then_inc(full2, 1)
            pe.wait_ge(yb_ready, 1)
            b = fill("bT", 0)
            heads64(b, range(2 * LCH), lambda q, c: yb[q, c, :], idn).then_inc(full2, 1)

            pe.wait_ge(mixa_ready, 1)
            wait_emptied2(pe, ("no", 15))
            for j in range(3):
                turn4("mt", j, lambda k, t: mixtok[:, t, k * P:(k + 1) * P])
            wait_emptied2(pe, ("mt", 2))
            for j in range(4):
                half, t = j // 2, j % 2
                if t == 0:
                    wait_block2(pe, 20 + half)
                b = fill("wout", j)
                for k in range(KT):
                    mm = pe.matmul(b[:, :], mixT[:, k, t * P:(t + 1) * P], w2(20 + half)[:, k, :],
                                   start=k == 0, stop=k == KT - 1)
                mm.then_inc(full2, 1)
            pe.wait_ge(xs3_ready, 2)
            for j in range(4):
                turn4("x3", j, lambda k, t: xs[:, t, k * P:(k + 1) * P])
            wait_emptied2(pe, ("x3", 2))
            wait_emptied2(pe, ("x3", 3))
            b = fill("rt", 0)
            for t in range(ST):
                for k in range(KT):
                    mm = pe.matmul(b[:, t * 36:(t + 1) * 36], h2T[:, k, t * P:(t + 1) * P], wr[:, k, :],
                                   start=k == 0, stop=k == KT - 1)
            mm.then_inc(full2, 1)
            pe.wait_ge(sel_ready, 1)
            pe.wait_ge(moe_c_in, 16)
            b = fill("pos", 0)
            pe.matmul(b[:, 0:N_EXP], earlier, sel[:, 0, :], start=True, stop=True)
            pe.matmul(b[:, N_EXP:2 * N_EXP], all_ones, sel[:, 0, :], start=True, stop=False)
            pe.matmul(b[:, N_EXP:2 * N_EXP], earlier, sel[:, 1, :], start=False, stop=True)
            pe.matmul(b[:, 2 * N_EXP:3 * N_EXP], all_ones, sel[:, 0, :], start=True, stop=False)
            pe.matmul(b[:, 2 * N_EXP:3 * N_EXP], all_ones, sel[:, 1, :], start=False, stop=True).then_inc(full2, 1)
            assert done2[0] == len(JOBS2)
            pe.wait_ge(rt_done, 1)
            sweeps = pe.value_load(sweeps_i[0:1, 0:1], min_val=1, max_val=S // SLOTS_E)

            with pe.Fori(0, sweeps) as sw_:
                with pe.Fori(0, TURNS) as tn:
                    pe.wait_ge(disp_ready, turn(sw_, tn, 1, 1))
                    for j in range(2):
                        for i in range(4):
                            k = 4 * j + i
                            for t in range(ST):
                                mm = pe.matmul(banks8[j][:, i * P:(i + 1) * P], xs[:, t, k * P:(k + 1) * P], pick[:, t, :],
                                               start=t == 0, stop=t == ST - 1)
                        mm.then_inc(moe_full, 1)
                    for t in range(ST):
                        mm = pe.transpose(banks8[7][:, t * P:(t + 1) * P], put[:, t, :], ident[:, :])
                    mm.then_inc(moe_full, 1)
                    pe.wait_ge(xg_act, turn(sw_, tn, 1, 1))
                    pe.wait_ge(xg_dve, turn(sw_, tn, 1, 1))
                    for m in range(2 * QUAD):
                        u, which = m // 2, m % 2
                        s = (len(BLOCKS2) + m) % SLOTS
                        pe.wait_ge(loaded[s], expert_loads(sw_, tn, m))
                        ww = wring[:, s, :].rearrange("p (k n) -> p k n", k=KT)
                        q = slice(SLOTS_E * u, SLOTS_E * (u + 1))
                        for k in range(KT):
                            mm = pe.matmul(banks8[2 + which][q, :], xg[:, k, q], ww[:, k, :], start=k == 0, stop=k == KT - 1)
                        mm.then_inc(moe_used, 1)
                    pe.wait_ge(moe_hid, turn(sw_, tn, 1, 1))
                    for k in range(D_EXP // P):
                        mm = pe.transpose(banks8[4][:, k * P:(k + 1) * P], hid[:, k * P:(k + 1) * P], ident[:, :])
                    mm.then_inc(moe_full, 1)
                    pe.wait_ge(hidT_ready, turn(sw_, tn, 1, 1))
                    for u in range(QUAD):
                        m = 2 * QUAD + u
                        s = (len(BLOCKS2) + m) % SLOTS
                        pe.wait_ge(loaded[s], expert_loads(sw_, tn, m))
                        ww = wring[:, s, :].rearrange("p (k n) -> p k n", k=D_EXP // P)
                        q = slice(SLOTS_E * u, SLOTS_E * (u + 1))
                        for half in range(2):
                            for k in range(D_EXP // P):
                                mm = pe.matmul(banks8[5 + half][q, :], hidT[:, k, q], ww[:, k, half * 512:(half + 1) * 512],
                                               start=k == 0, stop=k == D_EXP // P - 1)
                        mm.then_inc(moe_used, 1)
                    pe.wait_ge(yg_act, turn(sw_, tn, 1, 1))
                    pe.wait_ge(yg_dve, turn(sw_, tn, 1, 1))
                    for j in range(4):
                        half, t = j // 2, j % 2
                        pe.matmul(banks8[BACK[j]], putT[:, t, :], yg[:, half * 512:(half + 1) * 512], start=True, stop=True)\
                            .then_inc(moe_full, 1)

        @block.scalar
        def _(act_eng):
            a = act_eng
            a.dma_start(hot[:, :, :], d["c_hot"].rearrange("b (g j) -> b g j", g=NG)).then_inc(const_in, 16)
            a.dma_start(ident[:, :], d["c_ident"]).then_inc(const_in, 16)
            a.dma_start(flip, d["c_flip"]).then_inc(const_in, 16)
            a.dma_start(inv[:, :, :], d["c_inv"].unsqueeze(0).broadcast_to([P, 4, S])).then_inc(const_in, 16)
            a.wait_ge(relb_set, 1)
            a.dma_start(relb[0:N_BUCKETS, :], d["rel_bias"]).then_inc(const_in, 16)
            a.wait_ge(tab_ready, 1)
            a.dma_start(tab_dram.rearrange("(g h) j -> h g j", h=4), tab[:, :, :]).then_inc(tab_out, 16)
            a.wait_ge(tab_out, 16)
            a.dma_start(hankel[:, :, :], bass.AP(tensor=tab_dram.tensor, offset=0,
                                                 ap=[[1, P], [512, N_HEADS], [1, 384]])).then_inc(hankel_in, 16)
            for i in range(N_HEADS):
                a.wait_ge(bias_full, i + 1)
                a.activation(bias[:, i, :], bank[i % 4][:, 0:384], ACT.Copy).then_inc(bias_ready, 1)

            with a.Fori(0, DEPTH) as l:
                a.wait_ge(layer_done, l + 1)
                for name, row, n in (("norm1", V_N1, 8), ("norm2", V_N2, 8), ("pool_scale", V_PS, 8),
                                     ("conv_b", V_CB, FT)):
                    a.dma_start(rows[row:row + n, :], d[name][l].rearrange("(r p) -> r p", p=P)).then_inc(rows_in, 16)
                a.dma_start(rows[V_CW:V_CW + 3 * FT, :],
                            d["conv_w"][l].rearrange("c (r p) -> (c r) p", p=P)).then_inc(rows_in, 16)

                def squares(n):
                    for t in range(ST):
                        a.activation(junk, h[:, t, :], ACT.Square, accum_out=stats[:, t:t + 1]).then_inc(sumsq, 1)
                        a.wait_ge(sumsq, l * 4 + 2 * n + t + 1)
                    a.wait_ge(ms_ready, l * 2 + n + 1)
                    a.activation(stats[:, 4:6], stats[:, 2:4], ACT.Sqrt).then_inc(rms_ready, 1)

                def x_evac(name, vec):
                    for j in (0, 2):
                        b = bank[JOB[(name, j)] % 4]
                        wait_full(a, l, (name, j))
                        for kk in range(2):
                            k = 2 * j + kk
                            ins = a.activation(xT[:, k, :], b[:, kk * S:(kk + 1) * S], ACT.Copy,
                                               scale=cols[:, vec + k:vec + k + 1])
                        ins.then_inc(act_emptied, 1)

                def evac(name, j, dst, func=ACT.Copy, scale=1.0, n=512):
                    wait_full(a, l, (name, j))
                    b = bank[JOB[(name, j)] % 4]
                    a.activation(dst, b[:, 0:n] if len(dst.shape) == 2 else
                                 b[:, 0:n].rearrange("p (c s) -> p c s", s=S), func, scale=scale).then_inc(act_emptied, 1)

                squares(0)
                a.wait_ge(cols_full, l + 1)
                a.activation(cols, ps_t[:, 0:VEC_ROWS], ACT.Copy).then_inc(cols_ready, 1)
                a.wait_ge(cols_ready, l + 1)
                x_evac("x1", V_N1)
                a.wait_ge(pads_zero, 1)
                for j in range(4):
                    evac("u", j, upad[:, 2 * j:2 * j + 2, PAD:PAD + S])
                for j in range(6):
                    evac("q", j, qT[:, 2 * j:2 * j + 2, :])
                for j in range(6):
                    evac("k", j, kT[:, 2 * j:2 * j + 2, :])
                for j in range(6):
                    evac("v", j, vtok[:, j % 2, (j // 2) * 512:(j // 2 + 1) * 512])

                def softmax(i):
                    a.wait_ge(neg_max, l * 8 + i + 1)
                    L = logit[:, i % 2, :]
                    o = 6 + 3 * (i % 2)
                    a.activation(L, L, ACT.Exp, bias=stats[:, o:o + 1], accum_out=stats[:, o + 1:o + 2])\
                        .then_inc(exp_done, 1)
                    a.wait_ge(exp_done, l * 8 + i + 1)
                    a.wait_ge(rsum_ready, l * 8 + i + 1)
                    a.activation(L, L, ACT.Copy, scale=stats[:, o + 2:o + 3]).then_inc(probs_ready, 1)

                for i in range(8):
                    softmax(i)
                    evac("gate", i, gate[:, 2 * i:2 * i + 2, :], ACT.Tanh, 0.5)
                    if i % 2 == 1 and i >= 3:
                        evac("pv", (i - 3) // 2, attnT[:, (i - 3) // 2, :], n=S)
                for g in range(4):
                    b = bank[JOB[("pool", g)] % 4]
                    wait_full(a, l, ("pool", g))
                    for kk in range(2):
                        k = 2 * g + kk
                        ins = a.activation(poT[:, k, :], b[:, kk * S:(kk + 1) * S], ACT.Copy,
                                           scale=cols[:, V_PS + k:V_PS + k + 1])
                    ins.then_inc(act_emptied, 1)
                evac("pv", 3, attnT[:, 3, :], n=S)

                wait_emptied(a, l, ("wo", 3))
                squares(1)
                x_evac("x2", V_N2)
                for j in range(11):
                    wait_full(a, l, ("up", j))
                    b = bank[JOB[("up", j)] % 4]
                    for kk in range(2):
                        f = 2 * j + kk
                        a.activation(act[:, f, :], b[:, kk * S:(kk + 1) * S], ACT.Identity,
                                     scale=cols[:, V_CW + FT + f:V_CW + FT + f + 1],
                                     bias=cols[:, V_CB + f:V_CB + f + 1]).then_inc(conv_mid, 1)
                    if j:
                        wait_emptied(a, l, ("up", j - 1))
                        a.activation(act[:, 2 * j - 2:2 * j, :], act[:, 2 * j - 2:2 * j, :],
                                     ACT.Gelu_apprx_tanh).then_inc(gelu_ready, 1)
                wait_emptied(a, l, ("up", 10))
                a.activation(act[:, 20:22, :], act[:, 20:22, :], ACT.Gelu_apprx_tanh).then_inc(gelu_ready, 1)


            a.wait_ge(layer_done, DEPTH + 1)

            def flat(name, off, n, m):
                return bass.AP(tensor=d[name].tensor, offset=off, ap=[[m, n], [1, m]])

            for name, (row, n) in VEC2.items():
                if n == 1:
                    for q in range(2):
                        a.dma_start(vrows[row:row + 1, 64 * q:64 * q + 64], flat(name, 0, 1, 64)).then_inc(vec_in, 16)
                else:
                    a.dma_start(vrows[row:row + n, :], flat(name, 0, n, P)).then_inc(vec_in, 16)

            def spread(name, off, n, parts=P):
                return bass.AP(tensor=d[name].tensor, offset=off, ap=[[0, parts], [1, n]])

            a.dma_start(ctxb[:, :, :], d["ctx_2"][0].rearrange("(t p) n -> p t n", p=P)).then_inc(early_in, 16)
            a.dma_start(normf, spread("norm_f", 0, D)).then_inc(early_in, 16)
            for i in range(2):
                a.dma_start(gmul[:, i, :], spread("b_ada_2", (2 + 3 * i) * D, D)).then_inc(early_in, 16)
            a.dma_start(base, d["c2_base"]).then_inc(base_in, 16)
            a.dma_start(attn_c, d["c2_attn"]).then_inc(base_in, 16)
            a.dma_start(mask_stage, d["c2_levels"]).then_inc(base_in, 16)
            for hd in range(2):
                for dst, name in ((lng, "rwkv_ln_gain_2"), (lnb, "rwkv_ln_bias_2")):
                    a.dma_start(dst[64 * hd:64 * hd + 64, :, :],
                                bass.AP(tensor=d[name].tensor, offset=64 * hd, ap=[[0, 64], [P, 2], [1, 64]]))\
                        .then_inc(base_in, 16)
            a.dma_start(hgain, spread("hgrn_gn_gain_2", 0, A_W)).then_inc(base_in, 16)
            a.dma_start(rbias[:, 0:4], spread("b_router_group_2", 0, 4)).then_inc(base_in, 16)
            a.dma_start(rbias[:, 4:36], spread("b_router_expert_2", 0, 32)).then_inc(base_in, 16)
            a.dma_start(wr[:, :, 0:4], d["w_router_group_2"][0].rearrange("(k p) n -> p k n", p=P)).then_inc(base_in, 16)
            a.dma_start(wr[:, :, 4:36], d["w_router_expert_2"][0].rearrange("(k p) n -> p k n", p=P)).then_inc(base_in, 16)
            a.dma_start(wup, d["rwkv_w_up_2"][0].rearrange("e r n -> (e r) n")).then_inc(base_in, 16)
            a.dma_start(aup, d["rwkv_a_up_2"][0].rearrange("e r n -> (e r) n")).then_inc(base_in, 16)
            a.dma_start(gup, d["rwkv_g_up_2"][0]).then_inc(base_in, 16)
            a.wait_ge(rstage_zero, 1)
            a.dma_start(rstage[:, :, 48:48 + RPB_C], d["na_rpb_2"][0, :, 4:11, :]).then_inc(rpb_in, 16)
            a.wait_ge(rpb_in, 16)
            a.dma_start(rpb_dram, rstage[:, :, :]).then_inc(rpb_out, 16)

            wait_emptied2(a, ("vec", 0))
            rc = VEC2["c_2"][0]
            a.activation(csil[:, :, :].rearrange("p k c -> p c k"), cols2[:, rc:rc + 16].rearrange("p (c k) -> p c k", c=2),
                         ACT.Silu).then_inc(csil_ready, 1)

            def squares2(n, src):
                for t in range(ST):
                    a.activation(mixtok[:, :, :].rearrange("p t n -> p (t n)")[:, 0:D], src[:, t, :], ACT.Square,
                                 accum_out=st[:, 4 * n + t:4 * n + t + 1]).then_inc(sumsq2, 1)
                    a.wait_ge(sumsq2, 2 * n + t + 1)

            def root2(n):
                a.wait_ge(ms2, n + 1)
                a.activation(st[:, 16 + 2 * n:18 + 2 * n], st[:, 4 * n + 2:4 * n + 4], ACT.Sqrt).then_inc(rms2, 1)

            squares2(0, h)
            a.wait_ge(early_in, 64)
            squares2(1, ctxb)
            root2(0)
            root2(1)
            a.wait_ge(xl_ready, 2)
            squares2(2, h)
            root2(2)

            def full_bank(job):
                wait_full2(a, job)
                return bank2(*job)

            def x2_evac(name, dst, w, mul, add):
                for j in (0, 2):
                    b = full_bank((name, j))
                    for kk_ in range(2):
                        k = 2 * j + kk_
                        ins = a.activation(dst(k), b[:, kk_ * S:(kk_ + 1) * S], ACT.Identity,
                                           scale=mul(k), bias=add(k))
                    ins.then_inc(act_emptied2, 1)

            def take(job, dst, func=ACT.Copy, scale=1.0, n=512, split=None):
                b = full_bank(job)[:, 0:n]
                if split:
                    b = b.rearrange("p (c s) -> p c s", c=split)
                a.activation(dst, b, func, scale=scale).then_inc(act_emptied2, 1)

            a.wait_ge(mul_ready, 1)
            x2_evac("xl", lambda k: hT[:, k, 0:S], S, lambda k: mulT[:, 0, k:k + 1], lambda k: modT[:, k, 0:1])
            x2_evac("xc", lambda k: hT[:, k, S:T2], S, lambda k: mulT[:, 1, k:k + 1], lambda k: modT[:, k, 1:2])
            take(("aq", 0), aq[:, :, :], split=2)
            a.wait_ge(mask_ready, 1)
            for name, f, kx in (("ff", fF, kF), ("fb", fB, kB)):
                for j in range(2):
                    b = full_bank((name, j))
                    a.activation(kx[:, j, :], b, ACT.Sigmoid, scale=-1.0)
                    a.activation(f[:, j, :], b, ACT.Sigmoid).then_inc(act_emptied2, 1)
            for j in range(2):
                take(("ai", j), ai[:, 2 * j:2 * j + 2, :], split=2)
            take(("ag", 0), ag[:, :, :], ACT.Silu, split=2)
            a.wait_ge(base_in, 16 * N_BASE_DMA)
            a.wait_ge(rpb_out, 16)
            for j in range(8):
                b = full_bank(("b", j))
                for dst, o, n, m in shift_parts(j):
                    ins = a.activation(dst, b[:, o:o + n], ACT.Copy, scale=mu2[:, 0, m:m + 1])
                ins.then_inc(shift_mid, 1)
            for j in range(2):
                take(("cq", j), cq[:, 2 * j:2 * j + 2, :], split=2)
            for j in range(4):
                take(("ck", j), ck[:, j, :])
            for j in range(4):
                take(("cv", j), cv[:, j, :])
            for j in range(2):
                take(("kcT", j), kcT[:, j, :, :], split=2)
            for j in range(2):
                take(("cross", j), ATx[:, j, :, :, :].rearrange("p d r s -> p (d r) s"), split=4)
            for t in range(2):
                take(("ho", t), ho[:, t, :], n=A_W)
                wait_emptied2(a, ("ho", t))
            a.activation(hsq[:, :, :], ho[:, :, :], ACT.Square).then_inc(hsq_ready, 1)
            a.wait_ge(hms_ready, 1)
            a.activation(st[:, 32:40], st[:, 32:40], ACT.Sqrt).then_inc(hroot_ready, 1)
            a.wait_ge(mixa_ready, 1)
            for q in range(2):
                for r in range(6):
                    src = bass.AP(tensor=rpb_dram.tensor, offset=(1 - q + r) * P, ap=[[1, 64], [7 * P, C_HEADS], [1, 64]])
                    a.dma_start(nhank[64 * q:64 * q + 64, :, r, :], src).then_inc(nhank_in, 16)
            a.activation(nrot[:, :, :], cq[:, :, :], ACT.Square).then_inc(nsq_ready, 1)
            a.activation(nsq[:, :, :], ck[:, :, :], ACT.Square).then_inc(nsq_ready, 1)
            a.wait_ge(nms_ready, 1)
            a.activation(nL[:, :, :], nL[:, :, :], ACT.Sqrt).then_inc(nroot_ready, 1)
            a.activation(nrs[:, :, :], nrs[:, :, :], ACT.Sqrt).then_inc(nroot_ready, 1)
            for i in range(18):
                if i < 16:
                    o = 48 + 3 * (i % 4)
                    L = nL[:, i % 2, :]
                    a.wait_ge(nneg_ready, i + 1)
                    a.activation(L, L, ACT.Exp, bias=st[:, o:o + 1], accum_out=st[:, o + 1:o + 2]).then_inc(nprob_ready, 1)
                if 1 <= i < 17:
                    if i >= 3:
                        wait_full2(a, ("no", i - 3))
                    take(("nt", i - 1), nPT[:, (i - 1) % 2, :, :], split=4)
            a.activation(pB_w, pB_w, ACT.Tanh)
            a.activation(pB_g, pB_g, ACT.Sigmoid).then_inc(th_ready, 1)
            a.wait_ge(kn_ready, 1)
            a.activation(tmp1, tmp1, ACT.Sqrt)
            a.activation(tmp2, tmp2, ACT.Sqrt).then_inc(kroot_ready, 1)
            for pr in range(2):
                take(("vt", pr), vtk[:, pr, :, :], split=NCH)
            for g in range(4):
                dr, pr = g // 2, g % 2
                for name, dst, vec in (("wz", sw, "rwkv_w0_2"), ("az", aa, "rwkv_a0_2")):
                    c = VEC2[vec][0] + g
                    b = full_bank((name, g))
                    a.activation(dst, b, ACT.Sigmoid, bias=cols2[:, c:c + 1]).then_inc(act_emptied2, 1)
                a.wait_ge(exp_in, 2 * g + 1)
                a.activation(tmp2[:, 0:S], cc[:, 0:S], ACT.Exp, scale=-DECAY)
                a.activation(alp, cc, ACT.Exp, scale=DECAY)
                a.activation(dend, cc[:, (CH - 1 if dr == 0 else 0)::CH], ACT.Exp, scale=-DECAY).then_inc(exp_out, 1)
                a.wait_ge(exp_in, 2 * g + 2)
                a.activation(kap, kap, ACT.Exp, scale=-DECAY)
                kx = kapt[:, :, :].rearrange("p c t -> p (c t)")
                a.activation(kx, kx, ACT.Exp, scale=DECAY).then_inc(exp_out, 1)
                take(("tk", g), kapt[:, :, :], split=NCH)
                take(("ta", g), alpt[:, :, :], split=NCH)
                take(("tkk", g), kht[:, :, :], split=NCH)
                for n in range(1, 6):
                    take(("T1", 8 * g + n), T1[:, :, :], split=NCH)
                take(("W2", g), W2[:, :, :], split=NCH)
                take(("G", g), G[:, :, :], split=NCH)
                b = full_bank(("H", g))
                a.activation(Hn[:, g, :, :], b[:, 0:S].rearrange("p (c s) -> p c s", c=LCH), ACT.Copy, scale=-1.0)
                take(("H", g), Hfull[:, :, :], scale=-1.0, split=NCH)
                take(("PS", g), Psi[:, g, :, :], split=NCH)
                take(("GT", g), GT[:, g, :, :], n=S, split=LCH)
            take(("y", 0), yb[:, :, :], split=8)
            take(("bon", 0), bo, n=8)
            take(("gg", 0), gg[:, :, :], split=8)
            wait_emptied2(a, ("y", 0))
            a.wait_ge(ycent_ready, 1)
            a.activation(ysq[:, :, :], yb[:, :, :], ACT.Square).then_inc(ysq_ready, 1)
            a.wait_ge(yms_ready, 1)
            a.activation(st[:, 32:40], st[:, 32:40], ACT.Sqrt).then_inc(yroot_ready, 1)
            take(("bT", 0), mixT[:, 2:4, :], split=2)
            for j in range(3):
                c = (0, 4, 6)[j]
                take(("mt", j), mixT[:, c:c + 2, :], split=2)
            a.wait_ge(h2_ready, 1)
            a.dma_start(moe_c, d["c2_moe"]).then_inc(moe_c_in, 16)
            squares2(3, h)
            root2(3)
            x2_evac("x3", lambda k: h2T[:, k, :], S, lambda k: mulT[:, 2, k:k + 1], lambda k: modT[:, 16 + k, 0:1])
            a.wait_ge(gexp_in, 1)
            a.activation(ge, ge, ACT.Exp)
            a.activation(ee, ee, ACT.Exp).then_inc(gexp_out, 1)
            a.wait_ge(rt_done, 1)
            sweeps = a.value_load(sweeps_i[0:1, 0:1], min_val=1, max_val=S // SLOTS_E)
            with a.Fori(0, sweeps) as sw_:
                with a.Fori(0, TURNS) as tn:
                    a.wait_ge(moe_full, turn(sw_, tn, 1, 8))
                    for i in range(4):
                        ins = a.activation(xg[:, i, :], banks8[0][:, i * P:(i + 1) * P], ACT.Identity,
                                           scale=mulT[:, 2, i:i + 1], bias=modT[:, 16 + i, 0:1])
                    ins.then_inc(xg_act, 1)
                    a.wait_ge(moe_full, turn(sw_, tn, 3, 8))
                    a.activation(putT[:, :, :].rearrange("p t s -> p (t s)"), banks8[7][:, 0:ST * P], ACT.Copy)
                    a.wait_ge(moe_used, used_by(sw_, tn, 2 * QUAD - 1))
                    a.activation(sg, banks8[2], ACT.Silu).then_inc(moe_sg, 1)
                    a.wait_ge(moe_full, turn(sw_, tn, 4, 8))
                    a.activation(hidT[:, :, :].rearrange("p k s -> p (k s)"), banks8[4], ACT.Copy).then_inc(hidT_ready, 1)
                    a.wait_ge(moe_used, used_by(sw_, tn, TURN_BLOCKS))
                    a.activation(yg[:, 0:512], banks8[5], ACT.Copy).then_inc(yg_act, 1)

        @block.vector
        def _(v):
            chain = Chain(v, dve_chain)
            v.memset(relb, NEG).then_inc(relb_set, 1)
            v.wait_ge(const_in, 80)
            v.memset(stats[:, :], 0.0).then_inc(relb_set, 1)
            v.wait_ge(tab_full, 1)
            for g in range(NG):
                ins = v.tensor_copy(tab[:, g, :], bank[g][0:HEADS_PER_GROUP, :])
                if g < NG - 1:
                    chain(ins)
            ins.then_inc(tab_ready, 1)
            v.wait_ge(h_in, 16)
            v.wait_ge(bias_ready, N_HEADS)
            v.memset(stats[:, 15:16], 0.0).then_inc(layer_done, 1)
            first = chain.n

            with v.Fori(0, DEPTH) as l:
                chain.base, chain.n = l * DVE_CHAIN + first, 0

                def norm(n):
                    v.wait_ge(sumsq, l * 4 + 2 * n + 2)
                    v.tensor_scalar(stats[:, 2:4], stats[:, 0:2], 1.0 / D, EPS, ALU.mult, ALU.add).then_inc(ms_ready, 1)
                    v.wait_ge(rms_ready, l * 2 + n + 1)
                    chain(v.reciprocal(stats[:, 12:14], stats[:, 4:6]))
                    for t in range(ST):
                        v.tensor_scalar(xs[:, t, :], h[:, t, :], stats[:, 12 + t:13 + t], None, ALU.mult)\
                            .then_inc(xs_ready, 1)

                def x_evac(name, vec):
                    for j in (1, 3):
                        b = bank[JOB[(name, j)] % 4]
                        wait_full(v, l, (name, j))
                        for kk in range(2):
                            k = 2 * j + kk
                            ins = v.tensor_scalar(xT[:, k, :], b[:, kk * S:(kk + 1) * S],
                                                  cols[:, vec + k:vec + k + 1], None, ALU.mult)
                        ins.then_inc(dve_emptied, 1)

                norm(0)
                v.wait_ge(cols_ready, l + 1)
                x_evac("x1", V_N1)

                def logits(i):
                    hh, t = i // 2, i % 2
                    L = logit[:, i % 2, :]
                    o = 6 + 3 * (i % 2)
                    v.wait_ge(scores_full, l * 8 + i + 1)
                    if i >= 2:
                        v.wait_ge(probT_full, l * 8 + i - 1)
                    v.scalar_tensor_tensor(
                        L.rearrange("p (g s) -> p g s", s=S), ps_s[:, 0:NG * S].rearrange("p (g s) -> p g s", s=S),
                        HD ** -0.5, bias[:, hh::HEADS_PER_GROUP, P * (1 - t):P * (1 - t) + S],
                        ALU.mult, ALU.add).then_inc(logits_taken, 1)
                    v.wait_ge(logits_taken, l * 8 + i + 1)
                    chain(v.tensor_reduce(stats[:, 14:15], L, AX_X, ALU.max))
                    v.tensor_scalar(stats[:, o:o + 1], stats[:, 14:15], -1.0, None, ALU.mult).then_inc(neg_max, 1)
                    v.wait_ge(exp_done, l * 8 + i + 1)
                    v.reciprocal(stats[:, o + 2:o + 3], stats[:, o + 1:o + 2]).then_inc(rsum_ready, 1)

                def take_probT(i):
                    hh, t = i // 2, i % 2
                    v.wait_ge(probT_full, l * 8 + i + 1)
                    if hh >= 2 and t == 0:
                        wait_full(v, l, ("pv", hh - 2))
                    v.tensor_copy(probT[:, hh % 2, :, t * P:(t + 1) * P],
                                  ps_t[:, 0:NG * S].rearrange("p (k q) -> p k q", q=P)).then_inc(probT_ready, 1)

                for i in range(8):
                    logits(i)
                    if i:
                        take_probT(i - 1)
                take_probT(7)
                for j in range(4):
                    wait_full(v, l, ("wa", j))
                    v.scalar_tensor_tensor(mT[:, 2 * j:2 * j + 2, :].rearrange("p c s -> p (c s)"),
                                           gate[:, 2 * j:2 * j + 2, :].rearrange("p c s -> p (c s)"), 1.0,
                                           bank[JOB[("wa", j)] % 4][:, :], ALU.add, ALU.mult).then_inc(dve_emptied, 1)
                for j in range(4):
                    wait_full(v, l, ("wb", j))
                    tmp = logit[:, 0, 0:512]
                    chain(v.scalar_tensor_tensor(tmp, gate[:, KT + 2 * j:KT + 2 * j + 2, :].rearrange("p c s -> p (c s)"),
                                                 1.0, bank[JOB[("wb", j)] % 4][:, :], ALU.add, ALU.mult))
                    m = mT[:, 2 * j:2 * j + 2, :].rearrange("p c s -> p (c s)")
                    wait_emptied(v, l, ("wa", j))
                    v.tensor_tensor(m, m, tmp, ALU.add).then_inc(dve_emptied, 1)
                    wait_emptied(v, l, ("wb", j))
                for j in range(4):
                    half, t = j // 2, j % 2
                    wait_full(v, l, ("wo", j))
                    hv = h[:, t, half * 512:(half + 1) * 512]
                    v.scalar_tensor_tensor(hv, bank[JOB[("wo", j)] % 4][:, :], 0.5, hv, ALU.mult, ALU.add)\
                        .then_inc(dve_emptied, 1)
                norm(1)
                x_evac("x2", V_N2)
                for j in range(11):
                    wait_full(v, l, ("up", j))
                    b = bank[JOB[("up", j)] % 4]
                    v.wait_ge(conv_mid, l * FT + 2 * j + 2)
                    for kk in range(2):
                        f = 2 * j + kk
                        c = V_CW + f
                        o = kk * S
                        chain(v.scalar_tensor_tensor(act[:, f, 1:S], b[:, o:o + S - 1], cols[:, c:c + 1],
                                                     act[:, f, 1:S], ALU.mult, ALU.add))
                        ins = v.scalar_tensor_tensor(act[:, f, 0:S - 1], b[:, o + 1:o + S],
                                                     cols[:, c + 2 * FT:c + 2 * FT + 1],
                                                     act[:, f, 0:S - 1], ALU.mult, ALU.add)
                    ins.then_inc(dve_emptied, 1)
                for j in range(11, FT):
                    wait_full(v, l, ("up", j))
                    v.wait_ge(gelu_ready, l * 11 + j - 10)
                    f = 2 * (j - 11)
                    av = act[:, f:f + 2, :].rearrange("p c s -> p (c s)")
                    v.tensor_tensor(av, bank[JOB[("up", j)] % 4][:, :], av, ALU.mult).then_inc(dve_emptied, 1)
                for j in range(4):
                    half, t = j // 2, j % 2
                    wait_full(v, l, ("down", j))
                    hv = h[:, t, half * 512:(half + 1) * 512]
                    v.tensor_tensor(hv, bank[JOB[("down", j)] % 4][:, :], hv, ALU.add).then_inc(dve_emptied, 1)
                wait_emptied(v, l, ("down", 3))
                v.memset(stats[:, 15:16], 0.0).then_inc(layer_done, 1)
                assert chain.n == DVE_CHAIN, chain.n


            chain.base, chain.n = first + DEPTH * DVE_CHAIN, 0

            def full_bank(job):
                wait_full2(v, job)
                return bank2(*job)

            def col(name, i, n=1):
                c = VEC2[name][0] + i
                return cols2[:, c:c + n]

            v.tensor_copy(cols2, full_bank(("vec", 0))[:, 0:N_VEC2]).then_inc(dve_emptied2, 1)
            wait_emptied2(v, ("vec", 0))
            v.wait_ge(csil_ready, 1)
            v.tensor_copy(csb[:, :, :], csil[:, :, 0:1].broadcast_to([P, KT, P])).then_inc(csb_ready, 1)
            chain(v.tensor_scalar(mu2[:, 0, :], col("rwkv_mu_2", 0, 9), -1.0, 1.0, ALU.mult, ALU.add))
            chain(v.tensor_scalar(mu2[:, 1, :], col("rwkv_mu_2", 0, 9), 0.5, None, ALU.mult))
            lg = col("hgrn_lb_logits_2", 0, 4)
            chain(v.tensor_tensor(lb[:, 0, :], lg, lg, ALU.subtract))
            v.wait_ge(base_in, 16 * N_BASE_DMA)
            chain(v.tensor_tensor(lb[:, 1, :], lb[:, 0, :], lb[:, 0, :], ALU.is_equal))
            chain(v.reciprocal(lb[:, 2, :], lb[:, 1, :]))
            chain(v.tensor_tensor(lb[:, 3, :], lb[:, 1, :], lb[:, 2, :], ALU.mult))
            chain(v.tensor_tensor(lb[:, 4, :], lb[:, 3, :], lb[:, 3, :], ALU.subtract))
            v.tensor_scalar(lb[:, 5, :], lb[:, 4, :], -1.0, 1.0, ALU.mult, ALU.add).then_inc(lb_ready, 1)
            chain(v.tensor_scalar(kam[:, 0:2], col("rwkv_k_a_2", 0, 2), -1.0, 1.0, ALU.mult, ALU.add))

            def inverse_rms(n, width=D):
                v.wait_ge(sumsq2, 2 * n + 2)
                v.tensor_scalar(st[:, 4 * n + 2:4 * n + 4], st[:, 4 * n:4 * n + 2], 1.0 / width, EPS, ALU.mult, ALU.add)\
                    .then_inc(ms2, 1)
                v.wait_ge(rms2, n + 1)
                chain(v.reciprocal(st[:, 24 + 2 * n:26 + 2 * n], st[:, 16 + 2 * n:18 + 2 * n]))

            def rs(n, t):
                return st[:, 24 + 2 * n + t:25 + 2 * n + t]

            inverse_rms(0)
            v.wait_ge(early_in, 64)
            for t in range(ST):
                v.scalar_tensor_tensor(h[:, t, :], h[:, t, :], rs(0, t), normf, ALU.mult, ALU.mult).then_inc(xl_ready, 1)
            inverse_rms(1)
            for t in range(ST):
                v.tensor_scalar(ctxb[:, t, :], ctxb[:, t, :], rs(1, t), None, ALU.mult).then_inc(ctx_ready, 1)
            inverse_rms(2)
            for t in range(ST):
                v.tensor_scalar(xs[:, t, :], h[:, t, :], rs(2, t), None, ALU.mult).then_inc(xs2_ready, 1)
            for n in range(12):
                b = full_bank(("ada", n))
                if n in ADA_ROWS:
                    g = gmul[:, n // 6, (n % 2) * 512:(n % 2) * 512 + 512]
                    v.tensor_tensor(g, b, g, ALU.add).then_inc(dve_emptied2, 1)
                else:
                    m = 4 * n if n < 4 else 4 * n - 8
                    v.tensor_tensor(modT[:, m:m + 4, :], b[:, 0:8].rearrange("p (i c) -> p i c", c=2),
                                    col("b_ada_2", 4 * n, 4).unsqueeze(2).broadcast_to([P, 4, 2]), ALU.add)\
                        .then_inc(dve_emptied2, 1)
            wait_emptied2(v, ("ada", 11))
            for i, (m, c, name) in enumerate(((8, 0, "norm1_gain_2"), (8, 1, "norm1_gain_2"), (24, 0, "norm2_gain_2"))):
                ins = v.scalar_tensor_tensor(mulT[:, i, :], modT[:, m:m + 8, c], 1.0, col(name, 0, 8), ALU.add, ALU.mult)
                if i < 2:
                    chain(ins)
            ins.then_inc(mul_ready, 1)
            v.wait_ge(mul_ready, 1)

            def x2_evac(name, dst, mul, add):
                for j in (1, 3):
                    b = full_bank((name, j))
                    for kk_ in range(2):
                        k = 2 * j + kk_
                        ins = v.tensor_scalar(dst(k), b[:, kk_ * S:(kk_ + 1) * S], mul(k), add(k), ALU.mult, ALU.add)
                    ins.then_inc(dve_emptied2, 1)

            x2_evac("xl", lambda k: hT[:, k, 0:S], lambda k: mulT[:, 0, k:k + 1], lambda k: modT[:, k, 0:1])
            x2_evac("xc", lambda k: hT[:, k, S:T2], lambda k: mulT[:, 1, k:k + 1], lambda k: modT[:, k, 1:2])
            for j in range(8):
                b = full_bank(("b", j))
                v.wait_ge(shift_mid, j + 1)
                parts = shift_parts(j)
                for i, (dst, o, n, m) in enumerate(parts):
                    segs = n // S
                    dv = dst.rearrange("p (s t) -> p s t", t=S)
                    bv = b[:, o:o + n].rearrange("p (s t) -> p s t", t=S)
                    hm = mu2[:, 1, m:m + 1]
                    chain(v.scalar_tensor_tensor(dv[:, :, 1:S], bv[:, :, 0:S - 1], hm, dv[:, :, 1:S], ALU.mult, ALU.add))
                    ins = v.scalar_tensor_tensor(dv[:, :, 0:S - 1], bv[:, :, 1:S], hm, dv[:, :, 0:S - 1],
                                                 ALU.mult, ALU.add)
                    if i < len(parts) - 1:
                        chain(ins)
                ins.then_inc(dve_emptied2, 1)

            wait_full2(v, ("cv", 3))
            chain(v.memset(zeros, 0.0))
            v.memset(XS[:, :, CTX - 1:CTX], 1.0)
            chain(v.memset(XP[:, :, 0:1], 1.0))
            v.wait_ge(fk_ready, 1)
            for pr in range(2):
                chain(v.tensor_tensor_scan(XS[:, pr, 0:CTX - 1][:, ::-1], fF[:, pr, S + 1:T2][:, ::-1],
                                           zeros[:, 0:CTX - 1], 1.0, ALU.mult, ALU.add))
                chain(v.tensor_tensor_scan(XP[:, pr, 1:CTX], fB[:, pr, S:T2 - 1], zeros[:, 0:CTX - 1], 1.0,
                                           ALU.mult, ALU.add))
            v.tensor_tensor(Kd[:, 0, :, :], kF[:, :, S:T2], XS[:, :, :], ALU.mult).then_inc(kc_ready, 1)
            v.tensor_tensor(Kd[:, 1, :, :], kB[:, :, S:T2], XP[:, :, :], ALU.mult).then_inc(kc_ready, 1)
            v.tensor_tensor(Ksum[:, :, :], kF[:, :, 0:S], kB[:, :, 0:S], ALU.add).then_inc(ksum_ready, 1)
            v.wait_ge(kc_ready, 2)
            v.memset(XS[:, :, :], 1.0)
            v.memset(XP[:, :, :], 1.0).then_inc(xp_ready, 1)
            v.wait_ge(xp_ready, 1)
            wait_full2(v, ("kcT", 1))

            def level_f(n):
                if n:
                    wait_full2(v, ("lev", 4 * (n - 1) + 1) if n <= len(LEVELS) else ("cross", 1))
                if n <= len(LEVELS):
                    chain(v.tensor_tensor(Kd[:, 0, :, :], kF[:, :, 0:S], XS[:, :, :], ALU.mult))
                v.tensor_tensor(Qd[:, 0, :, :], aq[:, :, :], IP, ALU.mult).then_inc(lev_f, 1)
                v.wait_ge(lev_f, n + 1)
                if n <= len(LEVELS):
                    bw = 1 << n
                    x = XS[:, :, :].rearrange("p r (n h b) -> p r n h b", h=2, b=bw)
                    ip = IP.rearrange("p r (n h b) -> p r n h b", h=2, b=bw)
                    for r in range(2):
                        shape = [P, S // (2 * bw), bw]
                        chain(v.tensor_tensor(x[:, r, :, 0, :], x[:, r, :, 0, :],
                                              ip[:, r, :, 1, bw - 1:bw].broadcast_to(shape), ALU.mult))
                        chain(v.tensor_tensor(ip[:, r, :, 1, :], ip[:, r, :, 1, :],
                                              ip[:, r, :, 0, bw - 1:bw].broadcast_to(shape), ALU.mult))

            level_f(0)
            for j in range(2):
                b = full_bank(("hs", j))
                v.tensor_tensor(hst[:, j, :, :], b[:, 0:A_W].rearrange("p (r m) -> p r m", r=2),
                                ones_blk.unsqueeze(1).broadcast_to([P, 2, P]), ALU.mult).then_inc(dve_emptied2, 1)
            at3 = [AT[:, par, :, :, :].rearrange("p t r s -> p (t r) s") for par in range(2)]
            for par in range(2):
                b = full_bank(("diag", par))
                v.tensor_copy(at3[par], b.rearrange("p (h s) -> p h s", h=4)).then_inc(dve_emptied2, 1)
            wait_emptied2(v, ("diag", 1))
            for n in range(len(LEVELS)):
                level_f(n + 1)
                for j in range(4):
                    dr, par = j // 2, j % 2
                    job = ("lev", 4 * n + j)
                    if j >= 2 or n:
                        wait_emptied2(v, ("lev", 4 * n + j - 2) if j >= 2 else ("lev", 4 * (n - 1) + j + 2))
                    b = full_bank(job)
                    v.copy_predicated(at3[par], hg_mask[:, 2 * n + dr:2 * n + dr + 1, :].broadcast_to([P, 4, P]),
                                      b.rearrange("p (h s) -> p h s", h=4)).then_inc(dve_emptied2, 1)
            level_f(len(LEVELS) + 1)
            v.wait_ge(hsq_ready, 1)
            chain(v.tensor_reduce(st[:, 32:40], hsq[:, :, :].rearrange("p t (h d) -> p (t h) d", d=64), AX_X, ALU.add))
            v.tensor_scalar(st[:, 32:40], st[:, 32:40], 1.0 / 64, EPS, ALU.mult, ALU.add).then_inc(hms_ready, 1)
            v.wait_ge(hroot_ready, 1)
            chain(v.reciprocal(st[:, 32:40], st[:, 32:40]))
            hv = ho[:, :, :].rearrange("p t (h d) -> p (t h) d", d=64)
            chain(v.tensor_tensor(hv, hv, st[:, 32:40].unsqueeze(2).broadcast_to([P, 8, 64]), ALU.mult))
            chain(v.tensor_tensor(ho[:, :, :], ho[:, :, :], hgain.unsqueeze(1).broadcast_to([P, ST, A_W]), ALU.mult))
            v.tensor_tensor(mixtok[:, :, 0:A_W], ho[:, :, :], ag[:, :, :], ALU.mult).then_inc(mixa_ready, 1)
            v.wait_ge(mixa_ready, 1)

            for j in range(C_HEADS):
                b = full_bank(("nb", j))
                v.tensor_tensor(nbias[:, j, :, :], b[:, 0:384].rearrange("p (r c) -> p r c", r=6),
                                win.unsqueeze(1).broadcast_to([P, 6, 64]), ALU.add).then_inc(dve_emptied2, 1)
            for j in range(6):
                b = full_bank(("qs", j))
                dst = nL[:, j, :] if j < 2 else nrs[:, j - 2, :]
                v.tensor_scalar(dst, b, 1.0 / 64, EPS, ALU.mult, ALU.add).then_inc(dve_emptied2, 1)
            wait_emptied2(v, ("qs", 5))
            v.memset(st[:, 63:64], 0.0).then_inc(nms_ready, 1)
            for i, (x, r, name, n) in enumerate(((cq, nL, "na_q_gain_2", 1024), (ck, nrs, "na_k_gain_2", 2048))):
                v.wait_ge(nroot_ready, i + 1)
                rf = r[:, :, :].rearrange("p a b -> p (a b)")
                xf = x[:, :, :].rearrange("p a b -> p (a b)")
                chain(v.reciprocal(rf, rf))
                v.scalar_tensor_tensor(xf, xf, col(name, 0), rf, ALU.mult, ALU.mult).then_inc(qk_normed, 1)
            v.wait_ge(qk_normed, 2)
            for j in range(4):
                x = (cq, cq, ck, ck)[j][:, 2 * (j % 2):2 * (j % 2) + 2, 0:S]
                tr = nrot[:, 0:2, :]
                b = full_bank(("rope", j)).rearrange("p (i s) -> p i s", i=2)
                chain(v.tensor_tensor(tr, b, sin.unsqueeze(1).broadcast_to([P, 2, S]), ALU.mult))
                chain(v.tensor_tensor(x, x, cos.unsqueeze(1).broadcast_to([P, 2, S]), ALU.mult))
                v.tensor_tensor(x, x, tr, ALU.add).then_inc(dve_emptied2, 1)
                wait_emptied2(v, ("rope", j))
            v.memset(st[:, 63:64], 0.0).then_inc(qk_turned, 1)
            for i in range(18):
                if i < 16:
                    hd, t = i // 2, i % 2
                    o = 48 + 3 * (i % 4)
                    b = full_bank(("ns", i))
                    if i >= 2:
                        wait_full2(v, ("nt", i - 2))
                    L = nL[:, i % 2, :]
                    r0 = 2 * (1 - t)
                    chain(v.scalar_tensor_tensor(L[:, 0:S], b[:, 0:S], H2 ** -0.5,
                                                 nbias[:, hd, r0:r0 + 4, :].rearrange("p r c -> p (r c)"),
                                                 ALU.mult, ALU.add))
                    v.tensor_scalar(L[:, S:T2], b[:, S:T2], H2 ** -0.5, None, ALU.mult).then_inc(dve_emptied2, 1)
                    wait_emptied2(v, ("ns", i))
                    chain(v.tensor_reduce(st[:, o + 2:o + 3], L, AX_X, ALU.max))
                    v.tensor_scalar(st[:, o:o + 1], st[:, o + 2:o + 3], -1.0, None, ALU.mult).then_inc(nneg_ready, 1)
                if i >= 2:
                    hd, t = (i - 2) // 2, i % 2
                    o = 48 + 3 * ((i - 2) % 4)
                    v.wait_ge(nprob_ready, i - 1)
                    chain(v.reciprocal(st[:, o + 2:o + 3], st[:, o + 1:o + 2]))
                    b = full_bank(("no", i - 2))
                    v.tensor_scalar(mixtok[:, t, A_W + 64 * hd:A_W + 64 * hd + 64], b[:, 0:64], st[:, o + 2:o + 3], None,
                                    ALU.mult).then_inc(dve_emptied2, 1)
            for pr in range(2):
                chain(v.tensor_scalar(kunit[:, pr, :], pB_k[:, pr, :], col("rwkv_kk_scale_2", pr), None, ALU.mult))
                chain(v.tensor_tensor((tmp1, tmp2)[pr], kunit[:, pr, :], kunit[:, pr, :], ALU.mult))
            v.memset(st[:, 63:64], 0.0).then_inc(kksq_ready, 1)
            for pr in range(2):
                v.tensor_scalar((tmp1, tmp2)[pr], full_bank(("kn", pr)), 1e-24, None, ALU.max).then_inc(dve_emptied2, 1)
            wait_emptied2(v, ("kn", 1))
            v.memset(st[:, 63:64], 0.0).then_inc(kn_ready, 1)
            v.memset(reset[:, :, :], 1.0)
            chain(v.memset(states[:, 0, :, :], 0.0))
            v.memset(st[:, 63:64], 0.0).then_inc(reset_ready, 1)
            v.wait_ge(reset_ready, 1)
            rv = reset.rearrange("p d (c t) -> p d c t", t=CH)
            chain(v.memset(rv[:, 0, :, 0:1], 0.0))
            chain(v.memset(rv[:, 1, :, CH - 1:CH], 0.0))
            v.wait_ge(kroot_ready, 1)
            for pr in range(2):
                t_ = (tmp1, tmp2)[pr]
                chain(v.reciprocal(t_, t_))
                chain(v.tensor_tensor(kunit[:, pr, :], kunit[:, pr, :], t_, ALU.mult))
            for g in range(4):
                dr, pr = g // 2, g % 2
                wait_emptied2(v, ("az", g))
                rm, cc3 = reset[:, dr, :], cc.rearrange("p (c t) -> p c t", t=CH)
                if dr == 0:
                    v.tensor_tensor_scan(cc, rm, sw, 0.0, ALU.mult, ALU.add).then_inc(exp_in, 1)
                else:
                    v.tensor_tensor_scan(cc[:, ::-1], rm[:, ::-1], sw[:, ::-1], 0.0, ALU.mult, ALU.add).then_inc(exp_in, 1)
                v.wait_ge(exp_in, 2 * g + 1)
                chain(v.tensor_tensor(kap, cc, sw, ALU.subtract))
                e = CH - 1 if dr == 0 else 0
                v.tensor_tensor(kapt[:, :, :], cc3, cc3[:, :, e:e + 1].broadcast_to([P, NCH, CH]), ALU.subtract)\
                    .then_inc(exp_in, 1)
                chain(v.tensor_scalar(tmp1, aa, col("rwkv_k_a_2", pr), kam[:, pr:pr + 1], ALU.mult, ALU.add))
                chain(v.tensor_tensor(tmp1, tmp1, pB_k[:, pr, :], ALU.mult))
                if dr == 0:
                    chain(v.tensor_copy(ksum[:, pr, :], tmp1[:, 0:S]))
                else:
                    chain(v.tensor_tensor(ksum[:, pr, :], ksum[:, pr, :], tmp1[:, 0:S], ALU.add))
                chain(v.tensor_tensor(aa, aa, kunit[:, pr, :], ALU.mult))
                v.wait_ge(exp_out, 2 * g + 1)
                chain(v.tensor_tensor(rh[:, g, :], pB_r[:, pr, :], tmp2[:, 0:S], ALU.mult))
                chain(v.tensor_tensor(kh, tmp1, alp, ALU.mult))
                chain(v.tensor_tensor(alp, aa, alp, ALU.mult))
                v.wait_ge(exp_out, 2 * g + 2)
                chain(v.tensor_tensor(kap, kap, kunit[:, pr, :], ALU.mult))
                kx = kapt[:, :, :].rearrange("p c t -> p (c t)")
                chain(v.tensor_tensor(aa, aa, kx, ALU.mult))
                v.tensor_tensor(tmp1, tmp1, kx, ALU.mult).then_inc(group_ready, 1)
                mask = lambda m, n=NCH: rw_mask[:, 9 * dr + m:9 * dr + m + 1, :].broadcast_to([P, n, 64])
                idb = id64.unsqueeze(1).broadcast_to([P, NCH, 64])
                b3 = lambda job: full_bank(job).rearrange("p (c t) -> p c t", t=64)
                v.tensor_tensor(LT[:, :, :], b3(("LT", g)), mask(0), ALU.mult).then_inc(dve_emptied2, 1)
                wait_emptied2(v, ("LT", g))
                v.tensor_tensor(MT[:, :, :], LT[:, :, :], mask(2), ALU.mult).then_inc(m0_done, 1)
                chain(v.tensor_tensor(X[:, :, :], b3(("L1", g)), mask(8), ALU.mult))
                v.wait_ge(m0_done, g + 1)
                chain(v.tensor_tensor(XT[:, :, :], idb, MT[:, :, :], ALU.subtract))
                v.tensor_tensor(X[:, :, :], idb, X[:, :, :], ALU.subtract).then_inc(dve_emptied2, 1)
                wait_emptied2(v, ("L1", g))
                v.tensor_tensor(MT[:, :, :], LT[:, :, :], mask(3), ALU.mult).then_inc(mt_ready, 1)
                v.tensor_tensor(M2T[:, :, :], b3(("M2T", g)), mask(0), ALU.mult).then_inc(dve_emptied2, 1)
                v.tensor_tensor(NN[:, g, :, :, :].rearrange("p a c t -> p (a c) t"), b3(("NN", g)), mask(1), ALU.mult)\
                    .then_inc(dve_emptied2, 1)
                for n in range(1, 6):
                    if n < 5:
                        wait_full2(v, ("T1", 8 * g + n))
                        v.tensor_tensor(MT[:, :, :], LT[:, :, :], mask(3 + n), ALU.mult).then_inc(mt_next, 1)
                        v.tensor_tensor(X[:, :, :], X[:, :, :], b3(("XU", 8 * g + n)), ALU.subtract)\
                            .then_inc(dve_emptied2, 1)
                    v.tensor_tensor(XT[:, :, :], XT[:, :, :], b3(("XTU", 8 * g + n)), ALU.subtract)\
                        .then_inc(dve_emptied2, 1)
                    wait_emptied2(v, ("XTU", 8 * g + n))
                    if n < 5:
                        v.memset(st[:, 63:64], 0.0).then_inc(mt_ready, 1)
                chain(v.tensor_tensor(PhiT[:, g, :, :], idb, dend.unsqueeze(2).broadcast_to([P, NCH, 64]), ALU.mult))
                v.tensor_tensor(PhiT[:, g, :, :], PhiT[:, g, :, :], b3(("PH", g)), ALU.subtract).then_inc(dve_emptied2, 1)
                wait_emptied2(v, ("PH", g))
            wait_emptied2(v, ("GT", 3))
            for dr in range(2):
                c = step_chunks(0)[dr]
                ins = v.tensor_copy(states[:, 1, 2 * dr:2 * dr + 2, :], Psi[:, 2 * dr:2 * dr + 2, c, :])
                if dr == 0:
                    chain(ins)
            ins.then_inc(state_ready, 1)
            for i in range(1, 7):
                b = full_bank(("st", i))[:, 0:256].rearrange("p (g t) -> p g t", g=4)
                for dr in range(2):
                    c = step_chunks(i)[dr]
                    ins = v.tensor_tensor(states[:, i + 1, 2 * dr:2 * dr + 2, :], b[:, 2 * dr:2 * dr + 2, :],
                                          Psi[:, 2 * dr:2 * dr + 2, c, :], ALU.add)
                    if dr == 0:
                        chain(ins)
                ins.then_inc(dve_emptied2, 1)
            for dr in range(2):
                v.tensor_tensor(nSA[:, 2 * dr:2 * dr + 2, :, :], Hn[:, 2 * dr:2 * dr + 2, :, :],
                                full_bank(("sa", dr)).rearrange("p (g c t) -> p g c t", g=2, c=LCH), ALU.subtract)\
                    .then_inc(dve_emptied2, 1)
            for pr in range(2):
                chain(v.scalar_tensor_tensor(ksum[:, pr, :], ksum[:, pr, :], col("rwkv_r_k_2", pr), pB_r[:, pr, :],
                                             ALU.mult, ALU.mult))
            v.memset(st[:, 63:64], 0.0).then_inc(bonus_in, 1)
            yv = yb[:, :, :]
            s8 = lambda x: x.unsqueeze(2).broadcast_to([P, 8, 64])
            g4 = lambda x: x.unsqueeze(2).broadcast_to([P, 2, LCH, 64])
            y4 = yv.rearrange("p (r c) t -> p r c t", r=2)
            wait_emptied2(v, ("gg", 0))
            chain(v.tensor_reduce(st[:, 48:56], yv, AX_X, ALU.add))
            chain(v.tensor_scalar(st[:, 48:56], st[:, 48:56], 1.0 / 64, None, ALU.mult))
            v.tensor_tensor(yv, yv, s8(st[:, 48:56]), ALU.subtract).then_inc(ycent_ready, 1)
            v.wait_ge(ysq_ready, 1)
            chain(v.tensor_reduce(st[:, 32:40], ysq[:, :, :], AX_X, ALU.add))
            v.tensor_scalar(st[:, 32:40], st[:, 32:40], 1.0 / 64, LN_EPS, ALU.mult, ALU.add).then_inc(yms_ready, 1)
            v.wait_ge(yroot_ready, 1)
            chain(v.reciprocal(st[:, 32:40], st[:, 32:40]))
            chain(v.tensor_tensor(yv, yv, s8(st[:, 32:40]), ALU.mult))
            for r in range(2):
                chain(v.tensor_tensor(y4[:, r, :, :], y4[:, r, :, :], lng[:, r:r + 1, :].broadcast_to([P, LCH, 64]), ALU.mult))
                chain(v.tensor_tensor(y4[:, r, :, :], y4[:, r, :, :], lnb[:, r:r + 1, :].broadcast_to([P, LCH, 64]), ALU.add))
                chain(v.tensor_tensor(ysq[:, 4 * r:4 * r + 4, :], vtk[:, r, 0:LCH, :],
                                      bo[:, 4 * r:4 * r + 4].unsqueeze(2).broadcast_to([P, LCH, 64]), ALU.mult))
            chain(v.tensor_tensor(yv, yv, ysq[:, :, :], ALU.add))
            v.tensor_tensor(yv, yv, gg[:, :, :], ALU.mult).then_inc(yb_ready, 1)

            for j in range(4):
                half, t = j // 2, j % 2
                tm = mixtok[:, :, :].rearrange("p t n -> p (t n)")[:, 0:512]
                c = slice(half * 512, half * 512 + 512)
                chain(v.tensor_tensor(tm, full_bank(("wout", j)), gmul[:, 0, c], ALU.mult))
                v.tensor_tensor(h[:, t, c], h[:, t, c], tm, ALU.add).then_inc(dve_emptied2, 1)
                wait_emptied2(v, ("wout", j))
            v.memset(st[:, 63:64], 0.0).then_inc(h2_ready, 1)
            inverse_rms(3)
            for t in range(ST):
                v.tensor_scalar(xs[:, t, :], h[:, t, :], rs(3, t), None, ALU.mult).then_inc(xs3_ready, 1)
            x2_evac("x3", lambda k: h2T[:, k, :], lambda k: mulT[:, 2, k:k + 1], lambda k: modT[:, 16 + k, 0:1])
            v.tensor_tensor(rl[:, :, :], full_bank(("rt", 0))[:, 0:72].rearrange("p (t n) -> p t n", t=2),
                            rbias[:, 0:36].unsqueeze(1).broadcast_to([P, ST, 36]), ALU.add).then_inc(dve_emptied2, 1)
            wait_emptied2(v, ("rt", 0))
            gl, el = rl[:, :, 0:MG], rl[:, :, MG:36].rearrange("p t (g e) -> p t g e", g=MG)

            def b2(x, n):
                return x.unsqueeze(2).broadcast_to([P, ST, n])

            def first_max(dst, src, mx, n):
                chain(v.tensor_reduce(mx, src, AX_X, ALU.max))
                chain(v.tensor_tensor(dst, src, b2(mx, n), ALU.is_equal))
                chain(v.tensor_tensor(dst, dst, order[:, 8 - n:8].unsqueeze(1).broadcast_to([P, ST, n]), ALU.mult))
                chain(v.tensor_reduce(m2, dst, AX_X, ALU.max))
                chain(v.tensor_tensor(dst, dst, b2(m2, n), ALU.is_equal))

            for i in range(8):
                chain(v.memset(order[:, i:i + 1], float(8 - i)))
            first_max(gsel, gl, gmx, MG)
            chain(v.tensor_tensor(ge, gl, b2(gmx, MG), ALU.subtract))
            for t in range(ST):
                chain(v.tensor_tensor(esel[:, t, :, :], el[:, t, :, :],
                                      gsel[:, t, :].unsqueeze(2).broadcast_to([P, MG, PER_GROUP]), ALU.mult))
            chain(v.tensor_reduce(eg, esel[:, :, :, :].rearrange("p t g e -> p t e g"), AX_X, ALU.add))
            first_max(sel1, eg, emx, PER_GROUP)
            chain(v.tensor_tensor(ee, eg, b2(emx, PER_GROUP), ALU.subtract))
            v.scalar_tensor_tensor(eg, sel1, NEG, eg, ALU.mult, ALU.add).then_inc(gexp_in, 1)
            v.wait_ge(gexp_in, 1)
            first_max(sel2, eg, emx, PER_GROUP)
            chain(v.tensor_tensor(sel1, sel1, sel2, ALU.add))
            v.wait_ge(gexp_out, 1)
            chain(v.tensor_reduce(gmx, ge, AX_X, ALU.add))
            chain(v.reciprocal(gmx, gmx))
            chain(v.tensor_reduce(emx, ee, AX_X, ALU.add))
            chain(v.reciprocal(emx, emx))
            chain(v.tensor_tensor(ee, ee, b2(emx, PER_GROUP), ALU.mult))
            chain(v.tensor_tensor(ee, ee, sel1, ALU.mult))
            chain(v.tensor_reduce(emx, ee, AX_X, ALU.add))
            chain(v.reciprocal(emx, emx))
            chain(v.tensor_tensor(emx, emx, gmx, ALU.mult))
            chain(v.tensor_tensor(ee, ee, b2(emx, PER_GROUP), ALU.mult))
            for t in range(ST):
                chain(v.tensor_tensor(comb[:, t, :].rearrange("p (g e) -> p g e", g=MG),
                                      gsel[:, t, :].unsqueeze(2).broadcast_to([P, MG, PER_GROUP]),
                                      ee[:, t, :].unsqueeze(1).broadcast_to([P, MG, PER_GROUP]), ALU.mult))
            v.tensor_scalar(sel[:, :, :], comb[:, :, :], 0.0, None, ALU.is_gt).then_inc(sel_ready, 1)
            v.wait_ge(sel_ready, 1)
            b = full_bank(("pos", 0))
            chain(v.scalar_tensor_tensor(posm[:, :, :], b[:, 0:2 * N_EXP].rearrange("p (t e) -> p t e", t=ST), 1.0,
                                         sel[:, :, :], ALU.add, ALU.mult))
            chain(v.tensor_scalar(posm[:, :, :], posm[:, :, :], -1.0, None, ALU.add))
            v.tensor_copy(counts, b[:, 2 * N_EXP:3 * N_EXP]).then_inc(dve_emptied2, 1)
            wait_emptied2(v, ("pos", 0))
            chain(v.tensor_reduce(most, counts, AX_X, ALU.max))
            chain(v.tensor_scalar(over, sweep_from, most, None, ALU.is_lt))
            chain(v.tensor_reduce(sweeps_f, over, AX_X, ALU.add))
            chain(v.tensor_copy(sweeps_i, sweeps_f))
            v.memset(y[:, :, :], 0.0).then_inc(rt_done, 1)
            v.wait_ge(rt_done, 1)
            second = chain.base + chain.n
            sweeps = v.value_load(sweeps_i[0:1, 0:1], min_val=1, max_val=S // SLOTS_E)
            per_sweep = TURNS * MOE_CHAIN + 1

            def of_quad(x):
                return x.unsqueeze(2).broadcast_to([P, QUAD, SLOTS_E])

            slots = slot_no.unsqueeze(1).broadcast_to([P, QUAD, SLOTS_E])
            with v.Fori(0, sweeps) as sw_:
                with v.Fori(0, TURNS) as tn:
                    chain.base, chain.n = sw_ * per_sweep + tn * MOE_CHAIN + second, 0
                    chain(v.tensor_copy(ccol[:, :, :], comb[:, :, bass.ds(tn * QUAD, QUAD)]))
                    chain(v.tensor_copy(pcol[:, :, :], posm[:, :, bass.ds(tn * QUAD, QUAD)]))
                    for t in range(ST):
                        ins = v.tensor_tensor(pick[:, t, :].rearrange("p (u s) -> p u s", u=QUAD), slots,
                                              of_quad(pcol[:, t, :]), ALU.is_equal)
                    chain(ins)
                    for t in range(ST):
                        ins = v.tensor_tensor(put[:, t, :].rearrange("p (u s) -> p u s", u=QUAD),
                                              pick[:, t, :].rearrange("p (u s) -> p u s", u=QUAD),
                                              of_quad(ccol[:, t, :]), ALU.mult)
                    ins.then_inc(disp_ready, 1)
                    v.wait_ge(moe_full, turn(sw_, tn, 2, 8))
                    for i in range(4):
                        ins = v.tensor_scalar(xg[:, 4 + i, :], banks8[1][:, i * P:(i + 1) * P], mulT[:, 2, 4 + i:5 + i],
                                              modT[:, 20 + i, 0:1], ALU.mult, ALU.add)
                    ins.then_inc(xg_dve, 1)
                    v.wait_ge(moe_used, used_by(sw_, tn, 2 * QUAD))
                    v.wait_ge(moe_sg, turn(sw_, tn, 1, 1))
                    v.tensor_tensor(hid, banks8[3], sg, ALU.mult).then_inc(moe_hid, 1)
                    v.wait_ge(moe_used, used_by(sw_, tn, TURN_BLOCKS))
                    v.tensor_copy(yg[:, 512:1024], banks8[6]).then_inc(yg_dve, 1)
                    for j in range(4):
                        half, t = j // 2, j % 2
                        yv = y[:, t, half * 512:half * 512 + 512]
                        v.wait_ge(moe_full, turn(sw_, tn, 5 + j, 8))
                        ins = v.tensor_tensor(yv, yv, banks8[BACK[j]], ALU.add)
                    chain(ins)
                    assert chain.n == MOE_CHAIN
                chain.base, chain.n = sw_ * per_sweep + TURNS * MOE_CHAIN + second, 0
                chain(v.tensor_scalar(posm[:, :, :], posm[:, :, :], -float(SLOTS_E), None, ALU.add))
            for t in range(ST):
                chain.base, chain.n = sweeps * per_sweep + second, t
                chain(v.tensor_tensor(ob[:, t, :], y[:, t, :], gmul[:, 1, :], ALU.mult))
                v.tensor_tensor(ob[:, t, :], ob[:, t, :], h[:, t, :], ALU.add).then_inc(out_ready, 1)

        @block.gpsimd
        def _(g_eng):
            g_eng.memset(upad[:, :, :], 0.0).then_inc(pads_zero, 1)
            chain = Chain(g_eng, pool_chain)
            g_eng.wait_ge(const_in, 80)
            with g_eng.Fori(0, DEPTH) as l:
                chain.base, chain.n = l * POOL_CHAIN, 0
                wait_emptied(g_eng, l, ("u", 3))
                for g, window in enumerate(POOL_WINDOWS):
                    u = upad[:, 2 * g:2 * g + 2, :]
                    src, w, n = u, 1, 0
                    while w < window:
                        dst = (poolA, poolB)[n % 2]
                        m = UW - 2 * w + 1
                        chain(g_eng.tensor_tensor(dst[:, :, 0:m], src[:, :, 0:m], src[:, :, w:w + m], ALU.add))
                        src, w, n = dst, 2 * w, n + 1
                    o = PAD - window // 2
                    dst = (poolA, poolB)[n % 2]
                    chain(g_eng.tensor_tensor(dst[:, :, 0:S], src[:, :, o:o + S],
                                              inv[:, g:g + 1, :].broadcast_to([P, 2, S]), ALU.mult))
                    ins = g_eng.tensor_tensor(poolT[:, 2 * g:2 * g + 2, :], dst[:, :, 0:S], u[:, :, PAD:PAD + S],
                                              ALU.subtract)
                    if g < 3:
                        chain(ins)
                ins.then_inc(pooled, 1)
                assert chain.n == POOL_CHAIN, chain.n

            g_eng.wait_ge(layer_done, DEPTH + 1)
            g_eng.memset(rstage[:, :, :], 0.0).then_inc(rstage_zero, 1)
            g_eng.memset(st[:, 61:62], 0.0).then_inc(moe_used, SLOTS)
            chain.base, chain.n = DEPTH * POOL_CHAIN, 0
            g_eng.wait_ge(base_in, 16 * N_BASE_DMA)
            g_eng.tensor_copy(hg_mask.rearrange("p m t -> p (m t)"), mask_stage).then_inc(mask_ready, 1)
            g_eng.wait_ge(lb_ready, 1)
            for dr, (name, f, kx) in enumerate((("ff", fF, kF), ("fb", fB, kB))):
                for j in range(2):
                    wait_emptied2(g_eng, (name, j))
                    low, rest = lb[:, 4, 2 * dr + j:2 * dr + j + 1], lb[:, 5, 2 * dr + j:2 * dr + j + 1]
                    chain(g_eng.tensor_scalar(f[:, j, :], f[:, j, :], rest, low, ALU.mult, ALU.add))
                    chain(g_eng.tensor_scalar(f[:, j, :], f[:, j, :], F_FLOOR, None, ALU.max))
                    ins = g_eng.tensor_scalar(kx[:, j, :], kx[:, j, :], rest, None, ALU.mult)
                    if (dr, j) != (1, 1):
                        chain(ins)
            ins.then_inc(fk_ready, 1)
            g_eng.wait_ge(fk_ready, 1)
            g_eng.wait_ge(xp_ready, 1)
            wait_full2(g_eng, ("kcT", 1))
            for n in range(len(LEVELS) + 2):
                if n:
                    wait_full2(g_eng, ("lev", 4 * (n - 1) + 3) if n <= len(LEVELS) else ("cross", 1))
                if n <= len(LEVELS):
                    chain(g_eng.tensor_tensor(Kd[:, 1, :, :], kB[:, :, 0:S], XP[:, :, :], ALU.mult))
                g_eng.tensor_tensor(Qd[:, 1, :, :], aq[:, :, :], IS, ALU.mult).then_inc(lev_b, 1)
                g_eng.wait_ge(lev_b, n + 1)
                if n <= len(LEVELS):
                    bw = 1 << n
                    x = XP[:, :, :].rearrange("p r (n h b) -> p r n h b", h=2, b=bw)
                    ip = IS.rearrange("p r (n h b) -> p r n h b", h=2, b=bw)
                    for r in range(2):
                        shape = [P, S // (2 * bw), bw]
                        chain(g_eng.tensor_tensor(x[:, r, :, 1, :], x[:, r, :, 1, :],
                                                  ip[:, r, :, 0, 0:1].broadcast_to(shape), ALU.mult))
                        chain(g_eng.tensor_tensor(ip[:, r, :, 0, :], ip[:, r, :, 0, :],
                                                  ip[:, r, :, 1, 0:1].broadcast_to(shape), ALU.mult))


INPUTS = ["x", "w_in", "w_pool", "pool_scale", "w_a", "w_b", "w_o", "norm1", "norm2", "w_up", "conv_w", "conv_b", "w_down",
          "rel_bias", "norm_f", "c_2", "ctx_2", "c_ctx_2", "norm1_gain_2", "norm2_gain_2", "w_ada_2", "b_ada_2", "w_in_2",
          "w_out_2", "hgrn_lb_logits_2", "hgrn_gn_gain_2", "rwkv_mu_2", "rwkv_w0_2", "rwkv_w_up_2", "rwkv_a0_2",
          "rwkv_a_up_2", "rwkv_g_up_2", "rwkv_kk_scale_2", "rwkv_k_a_2", "rwkv_r_k_2", "rwkv_ln_gain_2",
          "rwkv_ln_bias_2", "na_q_gain_2", "na_k_gain_2", "na_rpb_2", "w_router_group_2", "b_router_group_2",
          "w_router_expert_2", "b_router_expert_2", "w_exp_gate_2", "w_exp_up_2", "w_exp_down_2"]


def kernel(**inputs):
    import concourse.bacc as bacc
    from concourse.bass_utils import run_bass_kernel_spmd

    nc = bacc.Bacc("TRN2", target_bir_lowering=False, num_devices=1)
    arrays = {name: np.ascontiguousarray(inputs[name]) for name in INPUTS}
    arrays.update(first_constants())
    arrays.update(second_constants())
    views = {name: nc.dram_tensor(name, a.shape, mybir.dt.from_np(a.dtype), kind="ExternalInput").ap()
             for name, a in arrays.items()}
    out = nc.dram_tensor("out", (1, S, D), F32, kind="ExternalOutput").ap()
    build(nc, views, out)
    result = run_bass_kernel_spmd(nc, [arrays], core_ids=[0])
    return result.results[0]["out"]
```

```python
from contextlib import ExitStack

import numpy as np

import concourse.bass as bass
from concourse import mybir

F32 = mybir.dt.float32
U32 = mybir.dt.uint32
ALU = mybir.AluOpType
ACT = mybir.ActivationFunctionType
AX_X = mybir.AxisListType.X

P = 128
D = 1024
KT = D // P
S = 256
ST = S // P
DEPTH = 2
EPS = 1e-6
NEG = -1e30
SLOTS = 4
BLOCK = 4096

R_SIZE = 32584

HEADS_PER_GROUP = 4
GROUPS = ((128, 1), (512, 4), (2048, 16))
NG = len(GROUPS)
N_HEADS = HEADS_PER_GROUP * NG
HD = 128
AW = N_HEADS * HD
FF = 2816
FT = FF // P
N_BUCKETS = 32
MAX_DISTANCE = 1024
POOL_WINDOWS = (2, 4, 8, 16)
PAD = 8
UW = PAD + S + PAD
VEC_ROWS = 8 + 8 + 8 + 3 * FT + FT
V_N1, V_N2, V_PS, V_CW, V_CB = 0, 8, 16, 24, 24 + 3 * FT


def layer_plan():
    jobs = [("x1", j, "act" if j % 2 == 0 else "dve") for j in range(KT // 2)]
    jobs += [("u", j, "act") for j in range(4)]
    jobs += [("q", j, "act") for j in range(6)]
    jobs += [("k", j, "act") for j in range(6)]
    jobs += [("v", j, "act") for j in range(6)]
    for i in range(8):
        jobs.append(("gate", i, "act"))
        if i % 2 == 1 and i >= 3:
            jobs.append(("pv", (i - 3) // 2, "act"))
    jobs += [("pool", j, "act") for j in range(4)]
    jobs.append(("pv", 3, "act"))
    jobs += [("wa", j, "dve") for j in range(4)]
    jobs += [("wb", j, "dve") for j in range(4)]
    jobs += [("wo", j, "dve") for j in range(4)]
    jobs += [("x2", j, "act" if j % 2 == 0 else "dve") for j in range(KT // 2)]
    jobs += [("up", j, "dve") for j in range(FT)]
    jobs += [("down", j, "dve") for j in range(4)]
    return jobs


JOBS = layer_plan()
NJ = len(JOBS)
JOB = {(name, j): n for n, (name, j, _) in enumerate(JOBS)}
EMPTIED = {}
_count = {"act": 0, "dve": 0}
for _name, _j, _e in JOBS:
    _count[_e] += 1
    EMPTIED[(_name, _j)] = (_e, _count[_e])
N_ACT, N_DVE = _count["act"], _count["dve"]
assert NJ % 4 == 0

LAYER_BLOCKS = [("u", j, ("u", 2 * j + 1)) for j in range(2)]
LAYER_BLOCKS += [("q", j, ("q", 2 * j + 1)) for j in range(3)]
LAYER_BLOCKS += [("k", j, ("k", 2 * j + 1)) for j in range(3)]
LAYER_BLOCKS += [("v", j, ("v", 2 * j + 1)) for j in range(3)]
LAYER_BLOCKS += [("gate", j, ("gate", 2 * j + 1)) for j in range(4)]
LAYER_BLOCKS += [("pool", j, ("pool", 2 * j + 1)) for j in range(2)]
LAYER_BLOCKS += [("wa", j, ("wa", 2 * j + 1)) for j in range(2)]
LAYER_BLOCKS += [("wb", j, ("wb", 2 * j + 1)) for j in range(2)]
LAYER_BLOCKS += [("wo", j, ("wo", 2 * j + 1)) for j in range(2)]
LAYER_BLOCKS += [("up", j, ("up", 2 * j + 1)) for j in range(11)]
LAYER_BLOCKS += [("down", j, None) for j in range(6)]
NB = len(LAYER_BLOCKS)
SPLIT_IN = [(name, j) for name, n in (("u", 4), ("q", 6), ("k", 6), ("v", 6)) for j in range(n)]
SPLIT_UP = [("up", j) for j in range(FT)]
SPLIT_DOWN = [("down", i) for i in range(FT // 2)]
SPLIT = {job: n for n, job in enumerate(SPLIT_IN + SPLIT_UP + SPLIT_DOWN)}
N_DOWN = len(SPLIT_DOWN)
HALF = 256
GATE_AT = KT * S + N_HEADS * 384 + KT * UW + KT * S + 2 * N_HEADS * S + ST * AW
Q_AT = GATE_AT - ST * AW - 2 * N_HEADS * S
assert (FT - N_HEADS) * S == HEADS_PER_GROUP * S + 2 * NG * S and ST * AW == N_HEADS * S
PROB_AT = GATE_AT + 2 * KT * S + HEADS_PER_GROUP * S + 2 * NG * S
BLK = {(name, j): n for n, (name, j, _) in enumerate(LAYER_BLOCKS)}
assert NB == 40 and NB % SLOTS == 0
QCOL, KCOL, VCOL, GCOL = D, D + AW, D + 2 * AW, D + 3 * AW


def t5_buckets(rel):
    n = -rel
    half = N_BUCKETS // 2
    ret = (n < 0).astype(np.int32) * half
    n = np.abs(n)
    exact = half // 2
    large = exact + (np.log(np.maximum(n, 1) / exact) / np.log(MAX_DISTANCE / exact) * (half - exact)).astype(np.int32)
    large = np.minimum(large, half - 1)
    return (ret + np.where(n < exact, n, large)).astype(np.int32)


def first_constants():
    hot = np.zeros((N_BUCKETS + 1, NG, 512), np.float32)
    d = np.arange(-(S - 1), S)
    for g, (window, dilation) in enumerate(GROUPS):
        half = window // (2 * dilation)
        offs = dilation * np.arange(-half, half + 1)
        bucket = dict(zip(offs.tolist(), t5_buckets(offs).tolist()))
        for i, x in enumerate(d.tolist()):
            hot[bucket.get(x, N_BUCKETS), g, i] = 1.0
        hot[N_BUCKETS, g, 2 * S - 1] = 1.0
    inv = np.zeros((len(POOL_WINDOWS), S), np.float32)
    i = np.arange(S)
    for g, w in enumerate(POOL_WINDOWS):
        inv[g] = 1.0 / (np.clip(i - w // 2 + w, 0, S) - np.clip(i - w // 2, 0, S)).astype(np.float32)
    return {
        "c_hot": hot.reshape(N_BUCKETS + 1, NG * 512),
        "c_ident": np.eye(P, dtype=np.float32),
        "c_flip": np.eye(P, dtype=np.float32)[::-1].copy(),
        "c_inv": inv,
    }


CTX = 256
T2 = S + CTX
H2 = 64
A_W = 256
B_W = 256
C_HEADS = 8
GRID_W = 64
GRID_R = S // GRID_W
WIN_COLS = 16
RPB_R, RPB_C = 15, 31
N_EXP, PER_GROUP, MG, D_EXP = 32, 8, 4, 512
QUAD = 4
SLOTS_E = P // QUAD
TURNS = N_EXP // QUAD
TURN_BLOCKS = 3 * QUAD
CH = 64
NCH = T2 // CH
LCH = S // CH
LEVELS = (1, 2, 4, 8, 16, 32, 64)
F_FLOOR = 1e-20
LN_EPS = 64e-5
DECAY = float(np.exp(-0.5))

VEC2, _r = {}, 0
for _name, _n in (("norm1_gain_2", 8), ("norm2_gain_2", 8), ("b_ada_2", 48), ("rwkv_mu_2", 9), ("rwkv_kk_scale_2", 2),
                  ("rwkv_k_a_2", 2), ("rwkv_r_k_2", 2), ("rwkv_w0_2", 4), ("rwkv_a0_2", 4), ("hgrn_lb_logits_2", 4),
                  ("c_2", 8), ("c_ctx_2", 8), ("na_q_gain_2", 1), ("na_k_gain_2", 1)):
    VEC2[_name] = (_r, _n)
    _r += _n
N_VEC2 = _r
N_VEC2_DMA = 16

BACK = (4, 7, 2, 3)
BLOCKS2 = [("w_ada_2", 512 * j, 512) for j in range(12)]
BLOCKS2 += [("w_in_2", c, n) for c, n in ((0, 512), (512, 512), (1024, 512), (1536, 512), (2048, 384),
                                          (2432, 512), (2944, 512), (3456, 512))]
N_BASE_DMA = 15
BLOCKS2 += [("w_out_2", 512 * j, 512) for j in range(2)]
ADA_ROWS = (4, 5, 10, 11)


def step_chunks(i):
    f = (4 + i) if i < 4 else i - 4
    b = (7 - i) if i < 4 else 7 - i
    return f, b


GROUP_STAGES = ("gates", "products", "MX1", "XMX1", "MX2", "XMX2", "MX3", "XMX3", "MX4", "XMX4", "MX5", "XMX5",
                "G", "H", "Psi")
GROUP_STEPS = [(stage, 2 * dr + pr) for dr in range(2) for stage in GROUP_STAGES for pr in range(2)]


def inverse_inputs(g, n):
    return 10 * (g // 2) + 2 * (n - 1) + g % 2 + 1


def second_plan():
    both = ("act", "dve")
    jobs = [("vec", 0, "dve")]
    jobs += [("ada", j, "dve") for j in range(12)] + [("adaT", 0, "dve")]
    jobs += [("xl", j, both[j % 2]) for j in range(4)] + [("xc", j, both[j % 2]) for j in range(4)]
    jobs += [("aq", 0, "act")] + [("ff", j, "act") for j in range(2)] + [("fb", j, "act") for j in range(2)]
    jobs += [("ai", j, "act") for j in range(2)] + [("ag", 0, "act")]
    jobs += [("b", j, "dve") for j in range(8)]
    jobs += [("cq", j, "act") for j in range(2)] + [("ck", j, "act") for j in range(4)]
    jobs += [("cv", j, "act") for j in range(4)]
    jobs += [("kcT", j, "act") for j in range(2)] + [("hs", j, "dve") for j in range(2)]
    jobs += [("diag", t, "dve") for t in range(2)]
    for n in range(len(LEVELS)):
        jobs += [("lev", 4 * n + j, "dve") for j in range(4)]
    jobs += [("nb", j, "dve") for j in range(C_HEADS)]
    jobs += [("cross", j, "act") for j in range(2)] + [("ho", t, "act") for t in range(2)]
    jobs += [("qs", j, "dve") for j in range(6)] + [("rope", j, "dve") for j in range(4)]
    for i in range(18):
        if i < 16:
            jobs.append(("ns", i, "dve"))
        if 1 <= i < 17:
            jobs.append(("nt", i - 1, "act"))
        if i >= 2:
            jobs.append(("no", i - 2, "dve"))
    jobs += [("kn", j, "dve") for j in range(2)] + [("vt", j, "act") for j in range(2)]
    for stage, g in GROUP_STEPS:
        if stage == "gates":
            jobs += [("wz", g, "act"), ("az", g, "act")]
        elif stage == "products":
            jobs += [("tk", g, "act"), ("ta", g, "act"), ("tkk", g, "act")]
            jobs += [("LT", g, "dve"), ("L1", g, "dve"), ("M2T", g, "dve"), ("NN", g, "dve")]
        elif stage == "G":
            jobs += [("W2", g, "act"), ("G", g, "act")]
        elif stage == "H":
            jobs += [("H", g, "act"), ("PH", g, "dve")]
        elif stage == "Psi":
            jobs += [("PS", g, "act"), ("GT", g, "act")]
        elif stage[0] == "M":
            jobs.append(("T1", 8 * g + int(stage[-1]), "act"))
        else:
            n = int(stage[-1])
            if n < 5:
                jobs.append(("XU", 8 * g + n, "dve"))
            jobs.append(("XTU", 8 * g + n, "dve"))
    jobs += [("st", i, "dve") for i in range(1, 7)]
    jobs += [("sa", j, "dve") for j in range(2)]
    jobs += [("y", 0, "act"), ("bon", 0, "act"), ("gg", 0, "act"), ("bT", 0, "act")]
    jobs += [("mt", j, "act") for j in range(3)]
    jobs += [("wout", j, "dve") for j in range(4)]
    jobs += [("x3", j, both[j % 2]) for j in range(4)]
    jobs += [("rt", 0, "dve"), ("pos", 0, "dve")]
    return jobs


JOBS2 = second_plan()
JOB2 = {(name, j): n for n, (name, j, _) in enumerate(JOBS2)}
assert len(JOB2) == len(JOBS2)
EMPTIED2 = {}
_count = {"act": 0, "dve": 0}
for _name, _j, _e in JOBS2:
    _count[_e] += 1
    EMPTIED2[(_name, _j)] = (_e, _count[_e])
USED2 = [("ada", j) for j in range(12)]
USED2 += [("ff", 1), ("ai", 1), ("b", 0), ("b", 4), ("b", 7), ("cq", 1), ("ck", 3), ("cv", 3), ("wout", 1), ("wout", 3)]


def second_constants():
    i = np.arange(P)
    blk = (i[:, None] // H2 == i[None, :] // H2).astype(np.float32)
    id64 = np.concatenate([np.eye(64), np.eye(64)]).astype(np.float32)
    s, t = np.arange(64)[:, None], np.arange(64)[None, :]
    masks = []
    for d in range(2):
        lt = (s < t) if d == 0 else (s > t)
        one = [lt, lt | (s == t)]
        for b in (1, 2, 4, 8, 16, 32):
            one.append(lt & (s // (2 * b) == t // (2 * b)) & (s // b != t // b))
        one.append(one[2].T)
        masks += one
    rw = np.concatenate([np.concatenate([m, m]).astype(np.float32) for m in masks], axis=1)
    base = np.concatenate([blk, id64, rw], axis=1)
    rot = np.zeros((P, P), np.float32)
    for m in range(P):
        c = m % 64
        if c < 32:
            rot[m + 32, m] = -1.0
        else:
            rot[m - 32, m] = 1.0
    pos = np.arange(S)
    inv = (np.float32(10000.0) ** (-np.arange(16, dtype=np.float32) / 16)).astype(np.float32)
    ang = np.concatenate([(pos // GRID_W).astype(np.float32)[:, None] * inv,
                          (pos % GRID_W).astype(np.float32)[:, None] * inv], axis=1)
    cos, sin = np.cos(ang).T[i % 32].astype(np.float32), np.sin(ang).T[i % 32].astype(np.float32)
    qc, kc = (i % 64)[:, None], np.arange(64)[None, :]
    w0 = np.clip(qc - WIN_COLS // 2, 0, GRID_W - WIN_COLS)
    win = np.where((kc >= w0) & (kc < w0 + WIN_COLS), 0.0, NEG).astype(np.float32)
    flip2 = np.zeros((P, P), np.float32)
    flip2[i, (i // 64) * 64 + 63 - i % 64] = 1.0
    attn = np.concatenate([rot, cos, sin, win, flip2], axis=1)
    s, t = i[:, None], i[None, :]
    hg = []
    for b in LEVELS:
        pair = (s // (2 * b) == t // (2 * b)) & (s // b != t // b)
        hg += [pair & (s < t), pair & (s > t)]
    hg = np.stack(hg, 1).astype(np.float32).reshape(P, -1)
    moe = np.zeros((P, 2 * P + SLOTS_E + S // SLOTS_E), np.float32)
    moe[:, 0:P] = i[:, None] < i[None, :]
    moe[:, P:2 * P] = 1.0
    moe[:, 2 * P:2 * P + SLOTS_E] = np.arange(SLOTS_E)
    moe[:, 2 * P + SLOTS_E:] = SLOTS_E * np.arange(S // SLOTS_E)
    return {"c2_base": base, "c2_attn": attn, "c2_levels": hg, "c2_moe": moe}


class Area:
    pass


class Chain:

    def __init__(self, eng, sem):
        self.eng, self.sem, self.base, self.n = eng, sem, 0, 0

    def __call__(self, ins):
        self.n += 1
        ins.then_inc(self.sem, 1)
        self.eng.wait_ge(self.sem, self.base + self.n)


DVE_CHAIN, POOL_CHAIN, MOE_CHAIN = 36, 17, 4


def build(nc, d, out):
    ctx = ExitStack()
    with ctx:
        def sb(name, shape, dt=F32):
            return ctx.enter_context(nc.sbuf_tensor(name, shape, dt))

        def sem(name):
            return ctx.enter_context(nc.semaphore(name))

        def rounded_views(*pieces):
            with ExitStack() as over:
                return [over.enter_context(nc.sbuf_tensor(name, shape, F32R if name[:3] != "gap" else F32))
                        for name, shape in pieces]

        F32R = mybir.dt.float32r
        [w_low] = rounded_views(("w_low", [P, SLOTS, BLOCK]))
        wring = sb("wring", [P, SLOTS, BLOCK])
        h = sb("h", [P, ST, D])
        [x_high_r] = rounded_views(("x_high", [P, KT, S]))
        xs = sb("xs", [P, ST, D])
        ident = sb("ident", [P, P])
        stats = sb("stats", [P, 16])
        _, a_low, _, a_high0, w_high_r, a_high1, x_low_r = rounded_views(
            ("gap0", [P, Q_AT]), ("a_low", [P, FT, S]), ("gap1", [P, 2 * N_HEADS * S - FT * S]),
            ("a_high0", [P, N_HEADS, S]), ("w_high", [P, 2, KT, HALF]), ("a_high1", [P, FT - N_HEADS, S]),
            ("x_low", [P, KT, S]))
        R = sb("R", [P, R_SIZE])

        at = [0]

        def part(*shape):
            n = int(np.prod(shape))
            v = R[:, at[0]:at[0] + n]
            at[0] += n
            if len(shape) == 1:
                return v
            names = "abcd"[:len(shape)]
            return v.rearrange(f"p ({' '.join(names)}) -> p {' '.join(names)}", **dict(zip(names, shape)))

        xT = part(KT, S)
        bias = part(N_HEADS, 384)
        upad = part(KT, UW)
        poolT = part(KT, S)
        mark = at[0]
        qT = part(N_HEADS, S)
        kT = part(N_HEADS, S)
        vtok = part(ST, AW)
        assert at[0] == GATE_AT
        gate = part(2 * KT, S)
        attnT = part(HEADS_PER_GROUP, S)
        logit = part(2, NG * S)
        assert at[0] == PROB_AT
        probT = part(2, NG * ST, S)
        poolA = part(2, UW)
        poolB = part(2, UW)
        inv = part(len(POOL_WINDOWS), S)
        cols = part(VEC_ROWS)
        rows = part(P)
        assert at[0] <= R_SIZE, at[0]
        mT = poolT
        poT = xs[:, :, :].rearrange("p t (a s) -> p (t a) s", s=S)
        act = R[:, mark:mark + FT * S].rearrange("p (f s) -> p f s", s=S)
        junk = vtok[:, 0, 0:D]
        hankel = R[:, mark:mark + N_HEADS * 384].rearrange("p (h j) -> p h j", j=384)
        hot = R[0:N_BUCKETS + 1, mark + 4608:mark + 4608 + NG * 512].rearrange("p (g j) -> p g j", j=512)
        relb = R[0:N_BUCKETS + 1, mark + 6144:mark + 6144 + N_HEADS]
        flip = R[:, mark + 6200:mark + 6328]
        tab = R[0:HEADS_PER_GROUP, mark + 6400:mark + 6400 + NG * 512].rearrange("p (g j) -> p g j", j=512)

        bank = [ctx.enter_context(nc.psum_tensor(f"bank{i}", [P, 512], F32)) for i in range(4)]
        ps_s = ctx.enter_context(nc.psum_tensor("ps_s", [P, 1024], F32))
        ps_t = ctx.enter_context(nc.psum_tensor("ps_t", [P, 1024], F32))

        tab_dram = nc.dram_tensor("bias_table", (N_HEADS, 512), F32, kind="Internal").ap()

        loaded = [sem(f"block_loaded{i}") for i in range(SLOTS)]
        const_in = sem("const_in")
        h_in = sem("h_in")
        tab_out = sem("tab_out")
        hankel_in = sem("hankel_in")
        rows_in = sem("rows_in")
        bank_full = sem("bank_full")
        down_used = sem("down_used")
        scores_full = sem("scores_full")
        probT_full = sem("probT_full")
        tab_full = sem("tab_full")
        bias_full = sem("bias_full")
        cols_full = sem("cols_full")
        act_emptied = sem("act_emptied")
        sumsq = sem("sumsq")
        rms_ready = sem("rms_ready")
        probs_ready = sem("probs_ready")
        exp_done = sem("exp_done")
        conv_mid = sem("conv_mid")
        gelu_ready = sem("gelu_ready")
        cols_ready = sem("cols_ready")
        w_high_ready, x_high_ready, a_high_ready = sem("w_high_ready"), sem("x_high_ready"), sem("a_high_ready")
        bias_ready = sem("bias_ready")
        dve_emptied = sem("dve_emptied")
        ms_ready = sem("ms_ready")
        xs_ready = sem("xs_ready")
        neg_max = sem("neg_max")
        rsum_ready = sem("rsum_ready")
        logits_taken = sem("logits_taken")
        probT_ready = sem("probT_ready")
        layer_done = sem("layer_done")
        tab_ready = sem("tab_ready")
        relb_set = sem("relb_set")
        dve_chain = sem("dve_chain")
        w_low_ready, x_low_ready, a_low_ready = sem("w_low_ready"), sem("x_low_ready"), sem("a_low_ready")
        pads_zero = sem("pads_zero")
        pooled = sem("pooled")
        pool_chain = sem("pool_chain")

        def slot_of(name, j):
            return BLK[(name, j)] % SLOTS

        def wait_block(eng, l, name, j):
            n = BLK[(name, j)]
            eng.wait_ge(loaded[n % SLOTS], l * (16 * NB // SLOTS) + 16 * (n // SLOTS + 1))

        def wait_full(eng, l, job):
            eng.wait_ge(bank_full, l * NJ + JOB[job] + 1)

        def a_high(f):
            return a_high0[:, f:f + 2, :] if f < N_HEADS else a_high1[:, f - N_HEADS:f - N_HEADS + 2, :]

        def down_rows(i, ring):
            return ring[:, slot_of("down", i // 2), (i % 2) * 2 * D:(i % 2 + 1) * 2 * D]

        def down_high(i):
            return w_high_r[:, SPLIT[("down", i)] % 2, :, :].rearrange("p k n -> p (k n)")

        def half_block(job, ring):
            name, j = job
            c = (j % 2) * HALF
            return ring[:, slot_of(name, j // 2), :].rearrange("p (k n) -> p k n", k=KT)[:, :, c:c + HALF]

        def wait_emptied(eng, l, job):
            who, n = EMPTIED[job]
            if who == "act":
                eng.wait_ge(act_emptied, l * N_ACT + n)
            else:
                eng.wait_ge(dve_emptied, l * N_DVE + n)

        at[0] = 0
        base = part(P + 64 + 18 * 64)
        ones_blk, id64 = base[:, 0:P], base[:, P:P + 64]
        rw_mask = base[:, P + 64:P + 64 + 18 * 64].rearrange("p (m t) -> p m t", t=64)
        cols2 = part(N_VEC2)
        gmul = part(2, D)
        lng = part(2, 64)
        lnb = part(2, 64)
        hgain = part(A_W)
        rbias = part(40)
        modT = part(32, 2)
        mulT = part(3, KT)
        csil = part(KT, 2)
        wr = part(KT, 36)
        wup = part(B_W)
        aup = part(B_W)
        gup = part(B_W)
        mixtok = part(ST, 768)
        st = part(64)
        lb = part(6, 4)
        mu2 = part(2, 9)
        kam = part(2)
        pB_r, pB_k, pB_v = part(2, S), part(2, T2), part(2, T2)
        pB_w, pB_a, pB_g = part(T2), part(T2), part(S)
        rstage = R[0:C_HEADS, at[0] - 896:at[0]].rearrange("p (r c) -> p r c", c=P)
        x_area = at[0]
        cq, ck, cv = part(4, S), part(4, T2), part(4, 512)
        mod_rows = R[0:2, x_area:x_area + 32 * P]
        attn_c = part(P + 2 * S + 64 + P)
        rot, cos, sin = attn_c[:, 0:P], attn_c[:, P:P + S], attn_c[:, P + S:P + 2 * S]
        win, flip2 = attn_c[:, P + 2 * S:P + 2 * S + 64], attn_c[:, P + 2 * S + 64:]
        a_area = at[0]
        aq = part(2, S)
        fF, fB, kF, kB = part(2, T2), part(2, T2), part(2, T2), part(2, T2)
        ai, ag = part(4, A_W), part(2, A_W)
        hg_mask = part(len(LEVELS) * 2 * P // 4).bitcast(mybir.dt.uint8).rearrange("p (m t) -> p m t", t=P)
        n = len(LEVELS) * 2 * P
        mask_stage = R[:, a_area + 2 * S:a_area + 2 * S + n]
        w_area = at[0]
        hT = part(KT, T2)
        ctxb, csb, normf, vrows = part(ST, D), part(KT, P), part(D), part(P)
        assert at[0] <= R_SIZE, at[0]
        mixT = xs[:, :, :].rearrange("p t (a s) -> p (t a) s", s=S)
        at[0] = w_area
        XS, XP = part(2, S), part(2, S)
        Qd, Kd = part(2, 2, S), part(2, 2, S)
        Ksum = part(2, S)
        AT, ATx = part(2, ST, 2, P), part(2, 2, 2, P)
        kcT, hst = part(2, ST, A_W), part(2, 2, P)
        zeros = part(S)
        ho, hsq = part(ST, A_W), part(ST, A_W)
        assert at[0] <= R_SIZE, at[0]
        IP, IS = fF[:, :, 0:S], fB[:, :, 0:S]
        ring_at = [2 * BLOCK]

        def ring_part(*shape):
            n = int(np.prod(shape))
            v = wring[:, :, :].rearrange("p s n -> p (s n)")[:, ring_at[0]:ring_at[0] + n]
            ring_at[0] += n
            if len(shape) == 1:
                return v
            names = "abcd"[:len(shape)]
            return v.rearrange(f"p ({' '.join(names)}) -> p {' '.join(names)}", **dict(zip(names, shape)))

        at[0] = a_area
        nbias = ring_part(C_HEADS, 6, 64)
        hank_at = ring_at[0]
        nhank = ring_part(C_HEADS, 6, 64)
        ring_at[0] = hank_at
        nsq = ring_part(4, T2)
        nrs = part(4, T2)
        nrot = ring_part(4, S)
        nL, nPT = part(2, T2), part(2, 4, P)
        assert at[0] <= R_SIZE, at[0]
        at[0] = x_area
        reset = xs[:, 0, :].rearrange("p (d t) -> p d t", d=2)
        PhiT, Psi = part(4, NCH, 64), part(4, NCH, 64)
        NN = part(4, 2, LCH, 64)
        GT, Hn = part(4, LCH, 64), part(4, LCH, 64)
        rh = part(4, S)
        states = part(NCH, 4, 64)
        vtk = part(2, NCH, 64)
        kunit = part(2, T2)
        ksum = part(2, S)

        def group_area(take, decay_end):
            w = Area()
            w.sw, w.aa, w.cc, w.tmp1, w.tmp2 = take(T2), take(T2), take(T2), take(T2), take(T2)
            w.kap, w.alp, w.kh = take(T2), take(T2), take(T2)
            w.LT, w.MT = take(NCH, 64), take(NCH, 64)
            w.kapt, w.alpt, w.kht = take(NCH, 64), take(NCH, 64), take(NCH, 64)
            w.X, w.XT, w.T1, w.M2T, w.Hfull = (x.rearrange("p (c t) -> p c t", t=64)
                                               for x in (w.aa, w.tmp1, w.tmp2, w.sw, w.cc))
            w.G, w.W2 = w.T1, w.MT
            w.dend = decay_end
            return w

        ring_at[0] = 2 * BLOCK
        work = [group_area(part, st[:, 40:48]), group_area(ring_part, st[:, 48:56])]
        assert at[0] <= R_SIZE and ring_at[0] <= SLOTS * BLOCK
        kk_sq = (work[0].tmp1, work[0].tmp2)
        at[0] = x_area
        yb, ysq, nSA, bo, gg = part(8, 64), part(8, 64), part(4, LCH, 64), part(8), part(8, 64)
        at[0] = x_area
        h2T = part(KT, S)
        rl = part(ST, 36)
        comb = part(ST, N_EXP)
        gsel, ge, gmx = part(ST, MG), part(ST, MG), part(ST)
        esel, eg, ee, emx = part(ST, MG, PER_GROUP), part(ST, PER_GROUP), part(ST, PER_GROUP), part(ST)
        sel1, sel2, m2, order = part(ST, PER_GROUP), part(ST, PER_GROUP), part(ST), part(PER_GROUP)
        sel, posm = part(ST, N_EXP), part(ST, N_EXP)
        counts, over = part(N_EXP), part(S // SLOTS_E)
        most, sweeps_f = part(1), part(1)
        sweeps_i = part(1).bitcast(mybir.dt.int32)
        moe_c = part(2 * P + SLOTS_E + S // SLOTS_E)
        earlier, all_ones, slot_no = moe_c[:, 0:P], moe_c[:, P:2 * P], moe_c[:, 2 * P:2 * P + SLOTS_E]
        sweep_from = moe_c[:, 2 * P + SLOTS_E:]
        pcol, ccol = part(ST, QUAD), part(ST, QUAD)
        pick, put = part(ST, P), part(ST, P)
        putT = part(ST, P)
        xg = part(KT, P)
        sg, hid = part(D_EXP), part(D_EXP)
        hidT = part(D_EXP // P, P)
        yg = part(D)
        y = part(ST, D)
        ob = part(ST, D)
        assert at[0] <= R_SIZE, (at[0], "experts")

        rpb_dram = nc.dram_tensor("window_bias", (C_HEADS, 7, P), F32, kind="Internal").ap()
        banks8 = [b[:, :] for b in bank] + [ps_s[:, 0:512], ps_s[:, 512:1024], ps_t[:, 0:512], ps_t[:, 512:1024]]
        vec_in, early_in, base_in = sem("vec_in"), sem("early_in"), sem("base_in")
        rpb_in, rpb_out, nhank_in, moe_c_in, stored = sem("rpb_in"), sem("rpb_out"), sem("nhank_in"), sem("moe_c_in"), sem("stored")
        full2, moe_full, moe_used = sem("full2"), sem("moe_full"), sem("moe_used")
        act_emptied2 = sem("act_emptied2")
        csil_ready, sumsq2, rms2, shift_mid = sem("csil_ready"), sem("sumsq2"), sem("rms2"), sem("shift_mid")
        hsq_ready, hroot_ready, nsq_ready = sem("hsq_ready"), sem("hroot_ready"), sem("nsq_ready")
        nroot_ready, nprob_ready, th_ready = sem("nroot_ready"), sem("nprob_ready"), sem("th_ready")
        kroot_ready, exp_out, ysq_ready, yroot_ready = sem("kroot_ready"), sem("exp_out"), sem("ysq_ready"), sem("yroot_ready")
        gexp_out, moe_sg = sem("gexp_out"), sem("moe_sg")
        xg_act, hidT_ready, yg_act = sem("xg_act"), sem("hidT_ready"), sem("yg_act")
        dve_emptied2 = sem("dve_emptied2")
        csb_ready, lb_ready, ms2, xl_ready = sem("csb_ready"), sem("lb_ready"), sem("ms2"), sem("xl_ready")
        ctx_ready, xs2_ready, mul_ready = sem("ctx_ready"), sem("xs2_ready"), sem("mul_ready")
        kc_ready, ksum_ready, xp_ready, lev_f = sem("kc_ready"), sem("ksum_ready"), sem("xp_ready"), sem("lev_f")
        hms_ready, mixa_ready, nms_ready = sem("hms_ready"), sem("mixa_ready"), sem("nms_ready")
        qk_normed, qk_turned, nneg_ready = sem("qk_normed"), sem("qk_turned"), sem("nneg_ready")
        reset_ready, kksq_ready, kn_ready, exp_in, group_ready = sem("reset_ready"), sem("kksq_ready"), sem("kn_ready"), sem("exp_in"), sem("group_ready")
        m0_done, mt_ready, state_ready = sem("m0_done"), sem("mt_ready"), sem("state_ready")
        bonus_in, ycent_ready, yms_ready, yb_ready = sem("bonus_in"), sem("ycent_ready"), sem("yms_ready"), sem("yb_ready")
        h2_ready, xs3_ready, gexp_in, rt_done = sem("h2_ready"), sem("xs3_ready"), sem("gexp_in"), sem("rt_done")
        moe_hid, out_ready, sel_ready = sem("moe_hid"), sem("out_ready"), sem("sel_ready")
        disp_ready, xg_dve, yg_dve = sem("disp_ready"), sem("xg_dve"), sem("yg_dve")
        rstage_zero, fk_ready, lev_b, mask_ready = sem("rstage_zero"), sem("fk_ready"), sem("lev_b"), sem("mask_ready")

        def bank2(name, j):
            return banks8[JOB2[(name, j)] % 8]

        def wait_full2(eng, job):
            eng.wait_ge(full2, JOB2[job] + 1)

        def wait_emptied2(eng, job):
            who, n = EMPTIED2[job]
            eng.wait_ge(act_emptied2 if who == "act" else dve_emptied2, n)

        def wait_block2(eng, n):
            eng.wait_ge(loaded[n % SLOTS], 16 * (DEPTH * NB // SLOTS + n // SLOTS + 1))

        def expert_loads(sw_, tn, m):
            each = 16 * TURN_BLOCKS // SLOTS
            return sw_ * (TURNS * each) + tn * each + 16 * (DEPTH * NB // SLOTS + (len(BLOCKS2) + m) // SLOTS + 1)

        def used_by(sw_, tn, m):
            return sw_ * (TURNS * TURN_BLOCKS) + tn * TURN_BLOCKS + (SLOTS + m)

        def turn(sw_, tn, n, of):
            return sw_ * (TURNS * of) + tn * of + n

        def shift_parts(j):
            if j == 0:
                return [(pB_r[:, 0, :], 0, S, 0), (pB_r[:, 1, :], S, S, 1)]
            if j < 5:
                return [((pB_k, pB_v)[(j - 1) // 2][:, (j - 1) % 2, :], 0, T2, 1 + j)]
            return [((pB_w, pB_a, pB_g)[j - 5], 0, (T2, T2, S)[j - 5], 1 + j)]

        block = ctx.enter_context(nc.Block())

        @block.sync
        def _(sp):
            def source(l, name, j):
                w_in = d["w_in"][l].rearrange("(k p) n -> p k n", p=P)
                col = {"u": 0, "q": QCOL, "k": KCOL, "v": VCOL, "gate": GCOL}
                if name in col:
                    c = col[name] + 512 * j
                    return w_in[:, :, c:c + 512], KT
                if name == "pool":
                    return d["w_pool"][l, 2 * j:2 * j + 2].rearrange("g (k p) n -> p (g k) n", p=P), 4
                if name == "wb":
                    return d["w_b"][l].rearrange("(k p) n -> p k n", p=P)[:, :, 512 * j:512 * j + 512], 4
                if name == "down":
                    k = 4 if j < 5 else 2
                    return d["w_down"][l, 4 * j * P:(4 * j + k) * P].rearrange("(k p) n -> p k n", p=P), k
                w = {"wa": "w_a", "wo": "w_o", "up": "w_up"}[name]
                return d[w][l].rearrange("(k p) n -> p k n", p=P)[:, :, 512 * j:512 * j + 512], KT

            sp.dma_start(h[:, :, :], d["x"][0].rearrange("(t p) n -> p t n", p=P)).then_inc(h_in, 16)
            with sp.Fori(0, DEPTH) as l:
                for n, (name, j, _) in enumerate(LAYER_BLOCKS):
                    if n < 3:
                        sp.wait_ge(down_used, l * (N_DOWN - 1) + 2 * (3 + n))
                    elif n == 3:
                        sp.wait_ge(layer_done, l + 1)
                    else:
                        job = LAYER_BLOCKS[n - SLOTS][2]
                        if job is None:
                            sp.wait_ge(down_used, l * (N_DOWN - 1) + (N_DOWN - 1) + 2 * (LAYER_BLOCKS[n - SLOTS][1] + 1))
                        else:
                            wait_full(sp, l, job)
                    src, k = source(l, name, j)
                    size = src.shape[2] * k
                    dst = wring[:, n % SLOTS, 0:size].rearrange("p (k n) -> p k n", k=k)
                    sp.dma_start(dst, src).then_inc(loaded[n % SLOTS], 16)


            def load2(n):
                name, c, width = BLOCKS2[n]
                dst = wring[:, n % SLOTS, 0:KT * width].rearrange("p (k n) -> p k n", k=KT)
                sp.dma_start(dst, d[name][0].rearrange("(k p) n -> p k n", p=P)[:, :, c:c + width])\
                    .then_inc(loaded[n % SLOTS], 16)

            for n in range(len(BLOCKS2)):
                if n < 3:
                    sp.wait_ge(down_used, DEPTH * (N_DOWN - 1) + 2 * (3 + n))
                elif n == 3:
                    sp.wait_ge(layer_done, DEPTH + 1)
                else:
                    wait_full2(sp, USED2[n - SLOTS])
                load2(n)

            gates_d = [d[x].rearrange("a g e k n -> (a g e) k n") for x in ("w_exp_gate_2", "w_exp_up_2", "w_exp_down_2")]

            for n in range(len(BLOCKS2) - SLOTS, len(BLOCKS2)):
                wait_full2(sp, USED2[n])

            def load_turn(sw_, tn):
                for m in range(TURN_BLOCKS):
                    u, which = (m // 2, m % 2) if m < 2 * QUAD else (m - 2 * QUAD, 2)
                    s = (len(BLOCKS2) + m) % SLOTS
                    sp.wait_ge(moe_used, used_by(sw_, tn, m - SLOTS + 1))
                    sp.dma_start(wring[:, s, :].rearrange("p (k n) -> p k n", k=(KT, KT, D_EXP // P)[which]),
                                 gates_d[which][tn * QUAD + u].rearrange("(k p) n -> p k n", p=P)).then_inc(loaded[s], 16)

            with sp.Fori(0, TURNS) as tn:
                load_turn(0, tn)
            sp.wait_ge(rt_done, 1)
            n = sp.value_load(sweeps_i[0:1, 0:1], min_val=1, max_val=S // SLOTS_E)
            with sp.If(n > 1):
                with sp.Fori(1, n) as sw_:
                    with sp.Fori(0, TURNS) as tn:
                        load_turn(sw_, tn)
            for t in range(ST):
                sp.wait_ge(out_ready, t + 1)
                sp.dma_start(out[0, t * P:(t + 1) * P, :], ob[:, t, :]).then_inc(stored, 16)
            sp.wait_ge(stored, 16 * ST)

        @block.tensor
        def _(pe):
            def w(name, j, k, n):
                return wring[:, slot_of(name, j), 0:k * n].rearrange("p (k n) -> p k n", k=k)

            pe.wait_ge(const_in, 80)
            pe.wait_ge(relb_set, 2)
            for g in range(NG):
                mm = pe.matmul(bank[g][0:HEADS_PER_GROUP, :], relb[:, 4 * g:4 * g + 4], hot[:, g, :],
                               start=True, stop=True)
            mm.then_inc(tab_full, 1)
            pe.wait_ge(hankel_in, 16)
            pe.wait_ge(tab_ready, 1)
            for i in range(N_HEADS):
                if i >= 4:
                    pe.wait_ge(bias_ready, i - 3)
                pe.matmul(bank[i % 4][:, 0:384], flip, hankel[:, i, :], start=True, stop=True).then_inc(bias_full, 1)
            pe.wait_ge(bias_ready, N_HEADS)
            pe.nop().then_inc(down_used, N_DOWN - 1)

            with pe.Fori(0, DEPTH) as l:
                def begin(name, j):
                    n = JOB[(name, j)]
                    if n >= 4:
                        wait_emptied(pe, l, JOBS[n - 4][:2])
                    return bank[n % 4]

                def x_job(name, j):
                    b = begin(name, j)
                    for kk in range(2):
                        for t in range(ST):
                            mm = pe.transpose(b[:, kk * S + t * P:kk * S + t * P + P],
                                              xs[:, t, (2 * j + kk) * P:(2 * j + kk + 1) * P], ident[:, :])
                    mm.then_inc(bank_full, 1)

                def rows_of(name, j, c0, c1, blk, k, n, rhs, rk0=0, wk0=0):
                    b = begin(name, j)
                    ww = w(blk[0], blk[1], k, n)
                    for i, c in enumerate((c0, c1)):
                        for kk in range(rhs[1]):
                            mm = pe.matmul(b[:, i * S:(i + 1) * S], ww[:, wk0 + kk, c:c + P],
                                           rhs[0][:, rk0 + kk, :], start=kk == 0, stop=kk == rhs[1] - 1)
                    mm.then_inc(bank_full, 1)

                def split_rows(name, j, tokens_out=False):
                    b = begin(name, j)
                    n = SPLIT[(name, j)]
                    pe.wait_ge(w_low_ready, l * len(SPLIT) + n + 1)
                    high, low = w_high_r[:, n % 2, :, :], half_block((name, j), w_low)
                    xh, xl = x_high_r, x_low_r
                    for i in range(2):
                        for k in range(KT):
                            for m, (ww, xx) in enumerate(((high, xh), (high, xl), (low, xh))):
                                part_of = slice(i * P, (i + 1) * P)
                                left, right = (xx[:, k, part_of], ww[:, k, :]) if tokens_out else \
                                    (ww[:, k, part_of], xx[:, k, :])
                                mm = pe.matmul(b[:, i * S:(i + 1) * S], left, right, start=k == 0 and m == 0,
                                               stop=k == KT - 1 and m == 2)
                    mm.then_inc(bank_full, 1)

                def scores(i):
                    hh, t = i // 2, i % 2
                    if i:
                        pe.wait_ge(logits_taken, l * 8 + i)
                    for g in range(NG):
                        hd = g * HEADS_PER_GROUP + hh
                        mm = pe.matmul(ps_s[:, g * S:(g + 1) * S], qT[:, hd, t * P:(t + 1) * P], kT[:, hd, :],
                                       start=True, stop=True)
                    mm.then_inc(scores_full, 1)

                def turn_probs(i):
                    pe.wait_ge(probs_ready, l * 8 + i + 1)
                    if i:
                        pe.wait_ge(probT_ready, l * 8 + i)
                    for k in range(NG * ST):
                        mm = pe.transpose(ps_t[:, k * P:(k + 1) * P], logit[:, i % 2, k * P:(k + 1) * P], ident[:, :])
                    mm.then_inc(probT_full, 1)

                def pv(hh):
                    pe.wait_ge(probT_ready, l * 8 + 2 * hh + 2)
                    b = begin("pv", hh)
                    for g in range(NG):
                        hd = g * HEADS_PER_GROUP + hh
                        for t in range(ST):
                            mm = pe.matmul(b[:, 0:S], vtok[:, t, hd * HD:(hd + 1) * HD], probT[:, hh % 2, g * ST + t, :],
                                           start=g == 0 and t == 0, stop=g == NG - 1 and t == ST - 1)
                    mm.then_inc(bank_full, 1)

                pe.wait_ge(rows_in, l * 80 + 80)
                pe.transpose(ps_t[:, 0:VEC_ROWS], rows[0:VEC_ROWS, :], ident[0:VEC_ROWS, 0:VEC_ROWS]).then_inc(cols_full, 1)

                pe.wait_ge(xs_ready, l * 4 + 2)
                for j in range(4):
                    x_job("x1", j)
                wait_emptied(pe, l, ("x1", 2))
                wait_emptied(pe, l, ("x1", 3))
                pe.wait_ge(x_low_ready, l * 2 + 1)
                for name, n in (("u", 4), ("q", 6), ("k", 6)):
                    for j in range(n):
                        split_rows(name, j)
                for j in range(6):
                    split_rows("v", j, tokens_out=True)
                wait_emptied(pe, l, ("v", 5))
                for i in range(8):
                    scores(i)
                    if i % 2 == 0:
                        wait_block(pe, l, "gate", i // 2)
                    rows_of("gate", i, (i % 2) * S, (i % 2) * S + P, ("gate", i // 2), KT, 512, (xT, KT))
                    if i:
                        turn_probs(i - 1)
                    if i % 2 == 1 and i >= 3:
                        pv((i - 3) // 2)
                turn_probs(7)
                pe.wait_ge(pooled, l + 1)
                for g in range(4):
                    if g % 2 == 0:
                        wait_block(pe, l, "pool", g // 2)
                    rows_of("pool", g, 0, P, ("pool", g // 2), 4, S, (poolT, 2), rk0=2 * g, wk0=2 * (g % 2))
                pv(3)
                wait_emptied(pe, l, ("pool", 3))
                for j in range(4):
                    if j % 2 == 0:
                        wait_block(pe, l, "wa", j // 2)
                    rows_of("wa", j, (j % 2) * S, (j % 2) * S + P, ("wa", j // 2), KT, 512, (poT, KT))
                wait_emptied(pe, l, ("pv", 3))
                for j in range(4):
                    if j % 2 == 0:
                        wait_block(pe, l, "wb", j // 2)
                    rows_of("wb", j, (j % 2) * S, (j % 2) * S + P, ("wb", j // 2), 4, 512, (attnT, HEADS_PER_GROUP))
                wait_emptied(pe, l, ("wb", 3))
                for j in range(4):
                    half, t = j // 2, j % 2
                    if t == 0:
                        wait_block(pe, l, "wo", half)
                    b = begin("wo", j)
                    for k in range(KT):
                        mm = pe.matmul(b[:, :], mT[:, k, t * P:(t + 1) * P], w("wo", half, KT, 512)[:, k, :],
                                       start=k == 0, stop=k == KT - 1)
                    mm.then_inc(bank_full, 1)
                pe.wait_ge(xs_ready, l * 4 + 4)
                for j in range(4):
                    x_job("x2", j)
                wait_emptied(pe, l, ("x2", 2))
                wait_emptied(pe, l, ("x2", 3))
                pe.wait_ge(x_low_ready, l * 2 + 2)
                for j in range(FT):
                    split_rows("up", j)
                wait_emptied(pe, l, ("up", FT - 1))
                for i in range(N_DOWN):
                    pe.wait_ge(w_low_ready, l * len(SPLIT) + SPLIT[("down", i)] + 1)
                    pe.wait_ge(a_low_ready, l * N_DOWN + i + 1)
                    high = down_high(i).rearrange("p (k n) -> p k n", k=2)
                    low = down_rows(i, w_low).rearrange("p (k n) -> p k n", k=2)
                    for j in range(4):
                        half, t = j // 2, j % 2
                        for kk in range(2):
                            ah, al = a_high(2 * i)[:, kk, t * P:(t + 1) * P], a_low[:, 2 * i + kk, t * P:(t + 1) * P]
                            for m, (left, ww) in enumerate(((ah, high), (al, high), (ah, low))):
                                mm = pe.matmul(bank[JOB[("down", j)] % 4][:, :], left, ww[:, kk, half * 512:(half + 1) * 512],
                                               start=i == 0 and kk == 0 and m == 0,
                                               stop=i == N_DOWN - 1 and kk == 1 and m == 2)
                        if i == N_DOWN - 1:
                            mm.then_inc(bank_full, 1)
                        elif j == 3:
                            mm.then_inc(down_used, 1)

            def fill(name, j):
                n = JOB2[(name, j)]
                assert n == done2[0], (name, j, JOBS2[done2[0]])
                done2[0] += 1
                if n >= 8:
                    wait_emptied2(pe, JOBS2[n - 8][:2])
                return bank2(name, j)

            done2 = [0]

            def w2(n, c0=0, c1=512):
                cols_n = BLOCKS2[n][2]
                return wring[:, n % SLOTS, 0:KT * cols_n].rearrange("p (k n) -> p k n", k=KT)[:, :, c0:c1]

            def channels(name, j, n, tiles, width, o=0):
                b = fill(name, j)
                for i, c in enumerate(tiles):
                    for k in range(KT):
                        mm = pe.matmul(b[:, i * width:(i + 1) * width], w2(n)[:, k, c:c + P] if BLOCKS2[n][2] == 512 else
                                       w2(n, 0, 384)[:, k, c:c + P], hT[:, k, o:o + width], start=k == 0, stop=k == KT - 1)
                mm.then_inc(full2, 1)

            def tokens(name, j, n, toks, c0, c1):
                b = fill(name, j)
                width = c1 - c0
                for i, t in enumerate(toks):
                    for k in range(KT):
                        mm = pe.matmul(b[:, i * width:(i + 1) * width], hT[:, k, t * P:(t + 1) * P],
                                       w2(n)[:, k, c0:c1], start=k == 0, stop=k == KT - 1)
                mm.then_inc(full2, 1)

            def turn4(name, j, src):
                b = fill(name, j)
                for kk_ in range(2):
                    for t in range(ST):
                        mm = pe.transpose(b[:, kk_ * S + t * P:kk_ * S + t * P + P], src(2 * j + kk_, t), ident[:, :])
                mm.then_inc(full2, 1)

            def heads64(b, chunks, lhs, rhs, start=True, stop=True, out=None, skip=False):
                for c in chunks:
                    for hd in range(2):
                        q = slice(64 * hd, 64 * hd + 64)
                        o = c if out is None else out(c)
                        mm = pe.matmul(b[q, 64 * o:64 * o + 64], lhs(q, c), rhs(q, c), start=start, stop=stop,
                                       skip_group_check=skip)
                return mm

            pe.wait_ge(vec_in, 16 * N_VEC2_DMA)
            b = fill("vec", 0)
            pe.transpose(b[:, 0:N_VEC2], vrows[0:N_VEC2, :], ident[0:N_VEC2, 0:N_VEC2]).then_inc(full2, 1)
            pe.wait_ge(csb_ready, 1)
            for n in range(12):
                wait_block2(pe, n)
                b = fill("ada", n)
                rows_out = P if n in ADA_ROWS else 2
                for k in range(KT):
                    mm = pe.matmul(b[0:rows_out, :], csb[:, k, :] if n in ADA_ROWS else csil[:, k, :], w2(n)[:, k, :],
                                   start=k == 0, stop=k == KT - 1)
                mm.then_inc(full2, 1)
            wait_emptied2(pe, ("ada", 9))
            b = fill("adaT", 0)
            for m in range(32):
                mm = pe.transpose(b[:, 2 * m:2 * m + 2], mod_rows[:, m * P:(m + 1) * P], ident[0:2, 0:2])
            mm.then_inc(full2, 1)
            pe.wait_ge(xs2_ready, 2)
            for j in range(4):
                turn4("xl", j, lambda k, t: xs[:, t, k * P:(k + 1) * P])
            pe.wait_ge(ctx_ready, 2)
            for j in range(4):
                turn4("xc", j, lambda k, t: ctxb[:, t, k * P:(k + 1) * P])
            wait_emptied2(pe, ("xc", 2))
            wait_emptied2(pe, ("xc", 3))
            wait_block2(pe, 12)
            channels("aq", 0, 12, (0, P), S)
            channels("ff", 0, 12, (2 * P,), T2)
            channels("ff", 1, 12, (3 * P,), T2)
            wait_block2(pe, 13)
            channels("fb", 0, 13, (0,), T2)
            channels("fb", 1, 13, (P,), T2)
            for j in range(2):
                tokens("ai", j, 13, (2 * j, 2 * j + 1), 2 * P, 4 * P)
            wait_block2(pe, 14)
            tokens("ag", 0, 14, (0, 1), 0, 2 * P)
            channels("b", 0, 14, (2 * P, 3 * P), S)
            wait_block2(pe, 15)
            for j in range(4):
                channels("b", 1 + j, 15, (j * P,), T2)
            wait_block2(pe, 16)
            channels("b", 5, 16, (0,), T2)
            channels("b", 6, 16, (P,), T2)
            channels("b", 7, 16, (2 * P,), S)
            wait_block2(pe, 17)
            channels("cq", 0, 17, (0, P), S)
            channels("cq", 1, 17, (2 * P, 3 * P), S)
            wait_block2(pe, 18)
            for j in range(4):
                channels("ck", j, 18, (j * P,), T2)
            wait_block2(pe, 19)
            for j in range(4):
                tokens("cv", j, 19, (j,), 0, 512)

            pe.wait_ge(kc_ready, 2)
            for dr in range(2):
                b = fill("kcT", dr)
                for t in range(ST):
                    for pr in range(2):
                        mm = pe.transpose(b[:, t * A_W + pr * P:t * A_W + (pr + 1) * P], Kd[:, dr, pr, t * P:(t + 1) * P],
                                          ident[:, :])
                mm.then_inc(full2, 1)
            for dr in range(2):
                wait_emptied2(pe, ("kcT", dr))
                b = fill("hs", dr)
                for pr in range(2):
                    for t in range(ST):
                        mm = pe.matmul(b[:, pr * P:(pr + 1) * P], kcT[:, dr, t, pr * P:(pr + 1) * P],
                                       ai[:, 2 + t, pr * P:(pr + 1) * P], start=t == 0, stop=t == ST - 1)
                mm.then_inc(full2, 1)

            def level(name, j, par, parts):
                b = fill(name, j)
                q = slice(64 * par, 64 * par + 64)
                for i, (q_of, k_of, pr, ts, tq) in enumerate(parts):
                    mm = pe.matmul(b[:, i * P:(i + 1) * P], k_of[q, pr, ts * P:(ts + 1) * P],
                                   q_of[q, pr, tq * P:(tq + 1) * P], start=True, stop=True)
                mm.then_inc(full2, 1)

            pe.wait_ge(ksum_ready, 1)
            for par in range(2):
                level("diag", par, par, [(aq, Ksum, pr, t, t) for t in range(ST) for pr in range(2)])
            for n in range(len(LEVELS)):
                for dr in range(2):
                    pe.wait_ge((lev_f, lev_b)[dr], n + 1)
                    for par in range(2):
                        level("lev", 4 * n + 2 * dr + par, par,
                              [(Qd[:, dr, :, :], Kd[:, dr, :, :], pr, t, t) for t in range(ST) for pr in range(2)])
            pe.wait_ge(nhank_in, 16 * 12)
            for j in range(C_HEADS):
                b = fill("nb", j)
                pe.matmul(b[:, 0:384], flip2, nhank[:, j, :, :].rearrange("p r c -> p (r c)"), start=True, stop=True)\
                    .then_inc(full2, 1)
            for dr in range(2):
                pe.wait_ge((lev_f, lev_b)[dr], len(LEVELS) + 1)
            for par in range(2):
                level("cross", par, par, [(Qd[:, dr, :, :], Kd[:, dr, :, :], pr, dr, 1 - dr)
                                          for dr in range(2) for pr in range(2)])
            for dr in range(2):
                pe.wait_ge((lev_f, lev_b)[dr], len(LEVELS) + 2)
            wait_emptied2(pe, ("hs", 1))
            wait_emptied2(pe, ("lev", 4 * len(LEVELS) - 1))
            wait_emptied2(pe, ("cross", 1))
            for t in range(ST):
                b = fill("ho", t)
                for pr in range(2):
                    for dr in range(2):
                        pe.matmul(b[:, pr * P:(pr + 1) * P], Qd[:, dr, pr, t * P:(t + 1) * P], hst[:, dr, pr, :],
                                  start=dr == 0, stop=False, skip_group_check=True)
                    for hd in (2 * pr, 2 * pr + 1):
                        o = b[:, hd * 64:hd * 64 + 64]
                        pe.matmul(o, AT[:, hd % 2, t, pr, :], ai[:, t, hd * 64:hd * 64 + 64], start=False, stop=False,
                                  skip_group_check=True)
                        mm = pe.matmul(o, ATx[:, hd % 2, 1 - t, pr, :], ai[:, 1 - t, hd * 64:hd * 64 + 64], start=False,
                                       stop=True, skip_group_check=True)
                mm.then_inc(full2, 1)

            pe.wait_ge(nsq_ready, 1)
            for j in range(2):
                b = fill("qs", j)
                pe.matmul(b[:, :], ones_blk, nrot[:, 2 * j:2 * j + 2, :], start=True, stop=True).then_inc(full2, 1)
            wait_emptied2(pe, ("qs", 1))
            pe.wait_ge(nsq_ready, 2)
            for j in range(4):
                b = fill("qs", 2 + j)
                pe.matmul(b[:, :], ones_blk, nsq[:, j, :], start=True, stop=True).then_inc(full2, 1)
            pe.wait_ge(qk_normed, 2)
            for j in range(4):
                src = (cq, cq, ck, ck)[j]
                b = fill("rope", j)
                for i in range(2):
                    mm = pe.matmul(b[:, i * S:(i + 1) * S], rot, src[:, 2 * (j % 2) + i, 0:S], start=True, stop=True)
                mm.then_inc(full2, 1)
            pe.wait_ge(qk_turned, 1)
            for i in range(18):
                if i < 16:
                    hd, t = i // 2, i % 2
                    q = slice(64 * (hd % 2), 64 * (hd % 2) + 64)
                    b = fill("ns", i)
                    pe.matmul(b[:, :], cq[q, hd // 2, t * P:(t + 1) * P], ck[q, hd // 2, :], start=True, stop=True)\
                        .then_inc(full2, 1)
                if 1 <= i < 17:
                    b = fill("nt", i - 1)
                    pe.wait_ge(nprob_ready, i)
                    for k in range(4):
                        mm = pe.transpose(b[:, k * P:(k + 1) * P], nL[:, (i - 1) % 2, k * P:(k + 1) * P], ident[:, :])
                    mm.then_inc(full2, 1)
                if i >= 2:
                    hd = (i - 2) // 2
                    b = fill("no", i - 2)
                    wait_emptied2(pe, ("nt", i - 2))
                    for k in range(4):
                        mm = pe.matmul(b[:, 0:64], nPT[:, i % 2, k, :], cv[:, k, hd * 64:hd * 64 + 64],
                                       start=k == 0, stop=k == 3)
                    mm.then_inc(full2, 1)

            idn = lambda q, c: ident[q, q]
            ck_ = lambda v: lambda q, c: v[q, 64 * c:64 * c + 64]
            cc_ = lambda v: lambda q, c: v[q, c, :]
            every, lat = range(NCH), range(LCH)
            pe.wait_ge(kksq_ready, 1)
            for pr in range(2):
                b = fill("kn", pr)
                pe.matmul(b[:, :], ones_blk, kk_sq[pr], start=True, stop=True).then_inc(full2, 1)
            for pr in range(2):
                b = fill("vt", pr)
                heads64(b, every, lambda q, c: pB_v[q, pr, 64 * c:64 * c + 64], idn).then_inc(full2, 1)
            pe.wait_ge(th_ready, 1)
            for stage, g in GROUP_STEPS:
                dr, pr = g // 2, g % 2
                w = work[pr]
                if stage == "gates":
                    q = slice(64 * dr, 64 * dr + 64)
                    b = fill("wz", g)
                    pe.matmul(b[:, :], wup[q, pr * P:(pr + 1) * P], pB_w[q, :], start=True, stop=True).then_inc(full2, 1)
                    b = fill("az", g)
                    pe.matmul(b[:, :], aup[q, pr * P:(pr + 1) * P], pB_a[q, :], start=True, stop=True).then_inc(full2, 1)
                elif stage == "products":
                    pe.wait_ge(group_ready, g + 1)
                    for name, src in (("tk", w.kap), ("ta", w.aa), ("tkk", w.tmp1)):
                        b = fill(name, g)
                        heads64(b, every, ck_(src), idn).then_inc(full2, 1)
                    b = fill("LT", g)
                    heads64(b, every, ck_(w.alp), ck_(w.kap)).then_inc(full2, 1)
                    b = fill("L1", g)
                    heads64(b, every, ck_(w.kap), ck_(w.alp)).then_inc(full2, 1)
                    b = fill("M2T", g)
                    heads64(b, every, ck_(w.kh), ck_(w.kap)).then_inc(full2, 1)
                    b = fill("NN", g)
                    rg = rh[:, g, :]
                    heads64(b, lat, ck_(w.alp), ck_(rg))
                    heads64(b, lat, ck_(w.kh), ck_(rg), out=lambda c: c + LCH).then_inc(full2, 1)
                elif stage == "G":
                    wait_emptied2(pe, ("M2T", g))
                    b = fill("W2", g)
                    heads64(b, every, cc_(w.M2T), cc_(vtk[:, pr, :, :])).then_inc(full2, 1)
                    wait_emptied2(pe, ("XTU", 8 * g + 5))
                    b = fill("G", g)
                    heads64(b, every, cc_(w.XT), cc_(w.kapt)).then_inc(full2, 1)
                elif stage == "H":
                    wait_emptied2(pe, ("W2", g))
                    b = fill("H", g)
                    heads64(b, every, cc_(w.XT), cc_(w.W2)).then_inc(full2, 1)
                    wait_emptied2(pe, ("G", g))
                    b = fill("PH", g)
                    heads64(b, every, cc_(w.G), cc_(w.alpt)).then_inc(full2, 1)
                elif stage == "Psi":
                    wait_emptied2(pe, ("H", g))
                    b = fill("PS", g)
                    for c in every:
                        for hd in range(2):
                            q = slice(64 * hd, 64 * hd + 64)
                            pe.matmul(b[q, 64 * c:64 * c + 64], w.kht[q, c, :], vtk[q, pr, c, :], start=True, stop=False)
                            mm = pe.matmul(b[q, 64 * c:64 * c + 64], w.alpt[q, c, :], w.Hfull[q, c, :], start=False, stop=True)
                    mm.then_inc(full2, 1)
                    b = fill("GT", g)
                    heads64(b, lat, cc_(w.kapt), cc_(w.XT)).then_inc(full2, 1)
                elif stage[0] == "M":
                    n = int(stage[-1])
                    pe.wait_ge(mt_ready, inverse_inputs(g, n))
                    b = fill("T1", 8 * g + n)
                    heads64(b, every, cc_(w.MT), cc_(w.X)).then_inc(full2, 1)
                else:
                    n = int(stage[-1])
                    wait_emptied2(pe, ("T1", 8 * g + n))
                    if n < 5:
                        b = fill("XU", 8 * g + n)
                        heads64(b, every, cc_(w.XT), cc_(w.T1)).then_inc(full2, 1)
                    b = fill("XTU", 8 * g + n)
                    heads64(b, every, cc_(w.T1), cc_(w.XT)).then_inc(full2, 1)
            wait_emptied2(pe, ("GT", 3))
            pe.wait_ge(state_ready, 1)
            for i in range(1, 7):
                b = fill("st", i)
                for g in range(4):
                    c = step_chunks(i)[g // 2]
                    for hd in range(2):
                        q = slice(64 * hd, 64 * hd + 64)
                        mm = pe.matmul(b[q, 64 * g:64 * g + 64], PhiT[q, g, c, :], states[q, i, g, :], start=True, stop=True)
                mm.then_inc(full2, 1)
                wait_emptied2(pe, ("st", i))
            for dr in range(2):
                b = fill("sa", dr)
                for pr in range(2):
                    g = 2 * dr + pr
                    for c in lat:
                        i = 4 + (c if dr == 0 else 3 - c)
                        for hd in range(2):
                            q = slice(64 * hd, 64 * hd + 64)
                            o = 64 * (LCH * pr + c)
                            mm = pe.matmul(b[q, o:o + 64], GT[q, g, c, :], states[q, i, g, :], start=True, stop=True)
                mm.then_inc(full2, 1)
            wait_emptied2(pe, ("sa", 1))
            b = fill("y", 0)
            for pr in range(2):
                for c in lat:
                    for hd in range(2):
                        q = slice(64 * hd, 64 * hd + 64)
                        o = b[q, 64 * (LCH * pr + c):64 * (LCH * pr + c) + 64]
                        for dr in range(2):
                            g = 2 * dr + pr
                            i = 4 + (c if dr == 0 else 3 - c)
                            pe.matmul(o, rh[q, g, 64 * c:64 * c + 64], states[q, i, g, :], start=dr == 0, stop=False)
                            pe.matmul(o, NN[q, g, 1, c, :], vtk[q, pr, c, :], start=False, stop=False)
                            mm = pe.matmul(o, NN[q, g, 0, c, :], nSA[q, g, c, :], start=False, stop=dr == 1)
            mm.then_inc(full2, 1)
            pe.wait_ge(bonus_in, 1)
            b = fill("bon", 0)
            for pr in range(2):
                for c in lat:
                    for hd in range(2):
                        q = slice(64 * hd, 64 * hd + 64)
                        o = LCH * pr + c
                        mm = pe.matmul(b[q, o:o + 1], ksum[q, pr, 64 * c:64 * c + 64], ones_blk[q, 64 * hd:64 * hd + 1],
                                       start=True, stop=True)
            mm.then_inc(full2, 1)
            b = fill("gg", 0)
            for pr in range(2):
                for c in lat:
                    for hd in range(2):
                        q = slice(64 * hd, 64 * hd + 64)
                        o = 64 * (LCH * pr + c)
                        mm = pe.matmul(b[q, o:o + 64], pB_g[:, 64 * c:64 * c + 64],
                                       gup[:, (2 * pr + hd) * 64:(2 * pr + hd) * 64 + 64], start=True, stop=True)
            mm.then_inc(full2, 1)
            pe.wait_ge(yb_ready, 1)
            b = fill("bT", 0)
            heads64(b, range(2 * LCH), lambda q, c: yb[q, c, :], idn).then_inc(full2, 1)

            pe.wait_ge(mixa_ready, 1)
            wait_emptied2(pe, ("no", 15))
            for j in range(3):
                turn4("mt", j, lambda k, t: mixtok[:, t, k * P:(k + 1) * P])
            wait_emptied2(pe, ("mt", 2))
            for j in range(4):
                half, t = j // 2, j % 2
                if t == 0:
                    wait_block2(pe, 20 + half)
                b = fill("wout", j)
                for k in range(KT):
                    mm = pe.matmul(b[:, :], mixT[:, k, t * P:(t + 1) * P], w2(20 + half)[:, k, :],
                                   start=k == 0, stop=k == KT - 1)
                mm.then_inc(full2, 1)
            pe.wait_ge(xs3_ready, 2)
            for j in range(4):
                turn4("x3", j, lambda k, t: xs[:, t, k * P:(k + 1) * P])
            wait_emptied2(pe, ("x3", 2))
            wait_emptied2(pe, ("x3", 3))
            b = fill("rt", 0)
            for t in range(ST):
                for k in range(KT):
                    mm = pe.matmul(b[:, t * 36:(t + 1) * 36], h2T[:, k, t * P:(t + 1) * P], wr[:, k, :],
                                   start=k == 0, stop=k == KT - 1)
            mm.then_inc(full2, 1)
            pe.wait_ge(sel_ready, 1)
            pe.wait_ge(moe_c_in, 16)
            b = fill("pos", 0)
            pe.matmul(b[:, 0:N_EXP], earlier, sel[:, 0, :], start=True, stop=True)
            pe.matmul(b[:, N_EXP:2 * N_EXP], all_ones, sel[:, 0, :], start=True, stop=False)
            pe.matmul(b[:, N_EXP:2 * N_EXP], earlier, sel[:, 1, :], start=False, stop=True)
            pe.matmul(b[:, 2 * N_EXP:3 * N_EXP], all_ones, sel[:, 0, :], start=True, stop=False)
            pe.matmul(b[:, 2 * N_EXP:3 * N_EXP], all_ones, sel[:, 1, :], start=False, stop=True).then_inc(full2, 1)
            assert done2[0] == len(JOBS2)
            pe.wait_ge(rt_done, 1)
            sweeps = pe.value_load(sweeps_i[0:1, 0:1], min_val=1, max_val=S // SLOTS_E)

            with pe.Fori(0, sweeps) as sw_:
                with pe.Fori(0, TURNS) as tn:
                    pe.wait_ge(disp_ready, turn(sw_, tn, 1, 1))
                    for j in range(2):
                        for i in range(4):
                            k = 4 * j + i
                            for t in range(ST):
                                mm = pe.matmul(banks8[j][:, i * P:(i + 1) * P], xs[:, t, k * P:(k + 1) * P], pick[:, t, :],
                                               start=t == 0, stop=t == ST - 1)
                        mm.then_inc(moe_full, 1)
                    for t in range(ST):
                        mm = pe.transpose(banks8[7][:, t * P:(t + 1) * P], put[:, t, :], ident[:, :])
                    mm.then_inc(moe_full, 1)
                    pe.wait_ge(xg_act, turn(sw_, tn, 1, 1))
                    pe.wait_ge(xg_dve, turn(sw_, tn, 1, 1))
                    for m in range(2 * QUAD):
                        u, which = m // 2, m % 2
                        s = (len(BLOCKS2) + m) % SLOTS
                        pe.wait_ge(loaded[s], expert_loads(sw_, tn, m))
                        ww = wring[:, s, :].rearrange("p (k n) -> p k n", k=KT)
                        q = slice(SLOTS_E * u, SLOTS_E * (u + 1))
                        for k in range(KT):
                            mm = pe.matmul(banks8[2 + which][q, :], xg[:, k, q], ww[:, k, :], start=k == 0, stop=k == KT - 1)
                        mm.then_inc(moe_used, 1)
                    pe.wait_ge(moe_hid, turn(sw_, tn, 1, 1))
                    for k in range(D_EXP // P):
                        mm = pe.transpose(banks8[4][:, k * P:(k + 1) * P], hid[:, k * P:(k + 1) * P], ident[:, :])
                    mm.then_inc(moe_full, 1)
                    pe.wait_ge(hidT_ready, turn(sw_, tn, 1, 1))
                    for u in range(QUAD):
                        m = 2 * QUAD + u
                        s = (len(BLOCKS2) + m) % SLOTS
                        pe.wait_ge(loaded[s], expert_loads(sw_, tn, m))
                        ww = wring[:, s, :].rearrange("p (k n) -> p k n", k=D_EXP // P)
                        q = slice(SLOTS_E * u, SLOTS_E * (u + 1))
                        for half in range(2):
                            for k in range(D_EXP // P):
                                mm = pe.matmul(banks8[5 + half][q, :], hidT[:, k, q], ww[:, k, half * 512:(half + 1) * 512],
                                               start=k == 0, stop=k == D_EXP // P - 1)
                        mm.then_inc(moe_used, 1)
                    pe.wait_ge(yg_act, turn(sw_, tn, 1, 1))
                    pe.wait_ge(yg_dve, turn(sw_, tn, 1, 1))
                    for j in range(4):
                        half, t = j // 2, j % 2
                        pe.matmul(banks8[BACK[j]], putT[:, t, :], yg[:, half * 512:(half + 1) * 512], start=True, stop=True)\
                            .then_inc(moe_full, 1)

        @block.scalar
        def _(act_eng):
            a = act_eng
            a.dma_start(hot[:, :, :], d["c_hot"].rearrange("b (g j) -> b g j", g=NG)).then_inc(const_in, 16)
            a.dma_start(ident[:, :], d["c_ident"]).then_inc(const_in, 16)
            a.dma_start(flip, d["c_flip"]).then_inc(const_in, 16)
            a.dma_start(inv[:, :, :], d["c_inv"].unsqueeze(0).broadcast_to([P, 4, S])).then_inc(const_in, 16)
            a.wait_ge(relb_set, 1)
            a.dma_start(relb[0:N_BUCKETS, :], d["rel_bias"]).then_inc(const_in, 16)
            a.wait_ge(tab_ready, 1)
            a.dma_start(tab_dram.rearrange("(g h) j -> h g j", h=4), tab[:, :, :]).then_inc(tab_out, 16)
            a.wait_ge(tab_out, 16)
            a.dma_start(hankel[:, :, :], bass.AP(tensor=tab_dram.tensor, offset=0,
                                                 ap=[[1, P], [512, N_HEADS], [1, 384]])).then_inc(hankel_in, 16)
            for i in range(N_HEADS):
                a.wait_ge(bias_full, i + 1)
                a.activation(bias[:, i, :], bank[i % 4][:, 0:384], ACT.Copy).then_inc(bias_ready, 1)

            with a.Fori(0, DEPTH) as l:
                a.wait_ge(layer_done, l + 1)
                for name, row, n in (("norm1", V_N1, 8), ("norm2", V_N2, 8), ("pool_scale", V_PS, 8),
                                     ("conv_b", V_CB, FT)):
                    a.dma_start(rows[row:row + n, :], d[name][l].rearrange("(r p) -> r p", p=P)).then_inc(rows_in, 16)
                a.dma_start(rows[V_CW:V_CW + 3 * FT, :],
                            d["conv_w"][l].rearrange("c (r p) -> (c r) p", p=P)).then_inc(rows_in, 16)

                def squares(n):
                    for t in range(ST):
                        a.activation(junk, h[:, t, :], ACT.Square, accum_out=stats[:, t:t + 1]).then_inc(sumsq, 1)
                        a.wait_ge(sumsq, l * 4 + 2 * n + t + 1)
                    a.wait_ge(ms_ready, l * 2 + n + 1)
                    a.activation(stats[:, 4:6], stats[:, 2:4], ACT.Sqrt).then_inc(rms_ready, 1)

                def x_evac(name, vec):
                    for j in (0, 2):
                        b = bank[JOB[(name, j)] % 4]
                        wait_full(a, l, (name, j))
                        for kk in range(2):
                            k = 2 * j + kk
                            ins = a.activation(xT[:, k, :], b[:, kk * S:(kk + 1) * S], ACT.Copy,
                                               scale=cols[:, vec + k:vec + k + 1])
                        ins.then_inc(act_emptied, 1)

                def evac(name, j, dst, func=ACT.Copy, scale=1.0, n=512):
                    wait_full(a, l, (name, j))
                    b = bank[JOB[(name, j)] % 4]
                    a.activation(dst, b[:, 0:n] if len(dst.shape) == 2 else
                                 b[:, 0:n].rearrange("p (c s) -> p c s", s=S), func, scale=scale).then_inc(act_emptied, 1)

                def split_weights(jobs, i):
                    if i >= len(jobs):
                        return
                    if i >= 2:
                        wait_full(a, l, jobs[i - 2])
                    name, j = jobs[i]
                    wait_block(a, l, name, j // 2)
                    n = SPLIT[jobs[i]]
                    a.activation(w_high_r[:, n % 2, :, :], half_block(jobs[i], wring), ACT.Copy)\
                        .then_inc(w_high_ready, 1)

                def split_x(name, n):
                    wait_full(a, l, (name, 3))
                    wait_emptied(a, l, (name, 2))
                    wait_emptied(a, l, (name, 3))
                    a.activation(x_high_r[:, :, :], xT[:, :, :], ACT.Copy).then_inc(x_high_ready, 1)

                squares(0)
                a.wait_ge(cols_full, l + 1)
                a.activation(cols, ps_t[:, 0:VEC_ROWS], ACT.Copy).then_inc(cols_ready, 1)
                a.wait_ge(cols_ready, l + 1)
                for i in range(2):
                    split_weights(SPLIT_IN, i)
                x_evac("x1", V_N1)
                split_x("x1", 0)
                a.wait_ge(pads_zero, 1)
                for i, (name, j) in enumerate(SPLIT_IN):
                    split_weights(SPLIT_IN, i + 2)
                    evac(name, j, {"u": upad[:, 2 * (j % 4):2 * (j % 4) + 2, PAD:PAD + S], "q": qT[:, 2 * j:2 * j + 2, :],
                                   "k": kT[:, 2 * j:2 * j + 2, :], "v": vtok[:, :, j * HALF:(j + 1) * HALF]}[name])

                def softmax(i):
                    a.wait_ge(neg_max, l * 8 + i + 1)
                    L = logit[:, i % 2, :]
                    o = 6 + 3 * (i % 2)
                    a.activation(L, L, ACT.Exp, bias=stats[:, o:o + 1], accum_out=stats[:, o + 1:o + 2])\
                        .then_inc(exp_done, 1)
                    a.wait_ge(exp_done, l * 8 + i + 1)
                    a.wait_ge(rsum_ready, l * 8 + i + 1)
                    a.activation(L, L, ACT.Copy, scale=stats[:, o + 2:o + 3]).then_inc(probs_ready, 1)

                for i in range(8):
                    softmax(i)
                    evac("gate", i, gate[:, 2 * i:2 * i + 2, :], ACT.Tanh, 0.5)
                    if i % 2 == 1 and i >= 3:
                        evac("pv", (i - 3) // 2, attnT[:, (i - 3) // 2, :], n=S)
                for g in range(4):
                    b = bank[JOB[("pool", g)] % 4]
                    wait_full(a, l, ("pool", g))
                    for kk in range(2):
                        k = 2 * g + kk
                        ins = a.activation(poT[:, k, :], b[:, kk * S:(kk + 1) * S], ACT.Copy,
                                           scale=cols[:, V_PS + k:V_PS + k + 1])
                    ins.then_inc(act_emptied, 1)
                evac("pv", 3, attnT[:, 3, :], n=S)

                wait_emptied(a, l, ("wo", 3))
                squares(1)
                for i in range(2):
                    split_weights(SPLIT_UP, i)
                x_evac("x2", V_N2)
                split_x("x2", 1)
                for j in range(11):
                    wait_full(a, l, ("up", j))
                    split_weights(SPLIT_UP, j + 2)
                    b = bank[JOB[("up", j)] % 4]
                    for kk in range(2):
                        f = 2 * j + kk
                        a.activation(act[:, f, :], b[:, kk * S:(kk + 1) * S], ACT.Identity,
                                     scale=cols[:, V_CW + FT + f:V_CW + FT + f + 1],
                                     bias=cols[:, V_CB + f:V_CB + f + 1]).then_inc(conv_mid, 1)
                    if j:
                        wait_emptied(a, l, ("up", j - 1))
                        a.activation(act[:, 2 * j - 2:2 * j, :], act[:, 2 * j - 2:2 * j, :],
                                     ACT.Gelu_apprx_tanh).then_inc(gelu_ready, 1)
                wait_emptied(a, l, ("up", 10))
                a.activation(act[:, 20:22, :], act[:, 20:22, :], ACT.Gelu_apprx_tanh).then_inc(gelu_ready, 1)

                def split_down(i):
                    if i < 2:
                        wait_full(a, l, SPLIT_UP[i - 2])
                    else:
                        a.wait_ge(down_used, l * (N_DOWN - 1) + N_DOWN - 1 + i - 1)
                    wait_block(a, l, "down", i // 2)
                    a.activation(down_high(i), down_rows(i, wring), ACT.Copy).then_inc(w_high_ready, 1)

                def split_act(i):
                    wait_emptied(a, l, ("up", 11 + i))
                    a.activation(a_high(2 * i), act[:, 2 * i:2 * i + 2, :], ACT.Copy).then_inc(a_high_ready, 1)

                for j in range(11, FT):
                    if j + 2 < FT:
                        split_weights(SPLIT_UP, j + 2)
                    else:
                        split_down(j + 2 - FT)
                    if j > 11:
                        split_act(j - 12)
                split_act(N_DOWN - 1)
                for i in range(2, N_DOWN):
                    split_down(i)


            a.wait_ge(layer_done, DEPTH + 1)

            def flat(name, off, n, m):
                return bass.AP(tensor=d[name].tensor, offset=off, ap=[[m, n], [1, m]])

            for name, (row, n) in VEC2.items():
                if n == 1:
                    for q in range(2):
                        a.dma_start(vrows[row:row + 1, 64 * q:64 * q + 64], flat(name, 0, 1, 64)).then_inc(vec_in, 16)
                else:
                    a.dma_start(vrows[row:row + n, :], flat(name, 0, n, P)).then_inc(vec_in, 16)

            def spread(name, off, n, parts=P):
                return bass.AP(tensor=d[name].tensor, offset=off, ap=[[0, parts], [1, n]])

            a.dma_start(ctxb[:, :, :], d["ctx_2"][0].rearrange("(t p) n -> p t n", p=P)).then_inc(early_in, 16)
            a.dma_start(normf, spread("norm_f", 0, D)).then_inc(early_in, 16)
            for i in range(2):
                a.dma_start(gmul[:, i, :], spread("b_ada_2", (2 + 3 * i) * D, D)).then_inc(early_in, 16)
            a.dma_start(base, d["c2_base"]).then_inc(base_in, 16)
            a.dma_start(attn_c, d["c2_attn"]).then_inc(base_in, 16)
            a.dma_start(mask_stage, d["c2_levels"]).then_inc(base_in, 16)
            for hd in range(2):
                for dst, name in ((lng, "rwkv_ln_gain_2"), (lnb, "rwkv_ln_bias_2")):
                    a.dma_start(dst[64 * hd:64 * hd + 64, :, :],
                                bass.AP(tensor=d[name].tensor, offset=64 * hd, ap=[[0, 64], [P, 2], [1, 64]]))\
                        .then_inc(base_in, 16)
            a.dma_start(hgain, spread("hgrn_gn_gain_2", 0, A_W)).then_inc(base_in, 16)
            a.dma_start(rbias[:, 0:4], spread("b_router_group_2", 0, 4)).then_inc(base_in, 16)
            a.dma_start(rbias[:, 4:36], spread("b_router_expert_2", 0, 32)).then_inc(base_in, 16)
            a.dma_start(wr[:, :, 0:4], d["w_router_group_2"][0].rearrange("(k p) n -> p k n", p=P)).then_inc(base_in, 16)
            a.dma_start(wr[:, :, 4:36], d["w_router_expert_2"][0].rearrange("(k p) n -> p k n", p=P)).then_inc(base_in, 16)
            a.dma_start(wup, d["rwkv_w_up_2"][0].rearrange("e r n -> (e r) n")).then_inc(base_in, 16)
            a.dma_start(aup, d["rwkv_a_up_2"][0].rearrange("e r n -> (e r) n")).then_inc(base_in, 16)
            a.dma_start(gup, d["rwkv_g_up_2"][0]).then_inc(base_in, 16)
            a.wait_ge(rstage_zero, 1)
            a.dma_start(rstage[:, :, 48:48 + RPB_C], d["na_rpb_2"][0, :, 4:11, :]).then_inc(rpb_in, 16)
            a.wait_ge(rpb_in, 16)
            a.dma_start(rpb_dram, rstage[:, :, :]).then_inc(rpb_out, 16)

            wait_emptied2(a, ("vec", 0))
            rc = VEC2["c_2"][0]
            a.activation(csil[:, :, :].rearrange("p k c -> p c k"), cols2[:, rc:rc + 16].rearrange("p (c k) -> p c k", c=2),
                         ACT.Silu).then_inc(csil_ready, 1)

            def squares2(n, src):
                for t in range(ST):
                    a.activation(mixtok[:, :, :].rearrange("p t n -> p (t n)")[:, 0:D], src[:, t, :], ACT.Square,
                                 accum_out=st[:, 4 * n + t:4 * n + t + 1]).then_inc(sumsq2, 1)
                    a.wait_ge(sumsq2, 2 * n + t + 1)

            def root2(n):
                a.wait_ge(ms2, n + 1)
                a.activation(st[:, 16 + 2 * n:18 + 2 * n], st[:, 4 * n + 2:4 * n + 4], ACT.Sqrt).then_inc(rms2, 1)

            squares2(0, h)
            a.wait_ge(early_in, 64)
            squares2(1, ctxb)
            root2(0)
            root2(1)
            a.wait_ge(xl_ready, 2)
            squares2(2, h)
            root2(2)

            def full_bank(job):
                wait_full2(a, job)
                return bank2(*job)

            def x2_evac(name, dst, w, mul, add):
                for j in (0, 2):
                    b = full_bank((name, j))
                    for kk_ in range(2):
                        k = 2 * j + kk_
                        ins = a.activation(dst(k), b[:, kk_ * S:(kk_ + 1) * S], ACT.Identity,
                                           scale=mul(k), bias=add(k))
                    ins.then_inc(act_emptied2, 1)

            def take(job, dst, func=ACT.Copy, scale=1.0, n=512, split=None):
                b = full_bank(job)[:, 0:n]
                if split:
                    b = b.rearrange("p (c s) -> p c s", c=split)
                a.activation(dst, b, func, scale=scale).then_inc(act_emptied2, 1)

            a.wait_ge(mul_ready, 1)
            x2_evac("xl", lambda k: hT[:, k, 0:S], S, lambda k: mulT[:, 0, k:k + 1], lambda k: modT[:, k, 0:1])
            x2_evac("xc", lambda k: hT[:, k, S:T2], S, lambda k: mulT[:, 1, k:k + 1], lambda k: modT[:, k, 1:2])
            take(("aq", 0), aq[:, :, :], split=2)
            a.wait_ge(mask_ready, 1)
            for name, f, kx in (("ff", fF, kF), ("fb", fB, kB)):
                for j in range(2):
                    b = full_bank((name, j))
                    a.activation(kx[:, j, :], b, ACT.Sigmoid, scale=-1.0)
                    a.activation(f[:, j, :], b, ACT.Sigmoid).then_inc(act_emptied2, 1)
            for j in range(2):
                take(("ai", j), ai[:, 2 * j:2 * j + 2, :], split=2)
            take(("ag", 0), ag[:, :, :], ACT.Silu, split=2)
            a.wait_ge(base_in, 16 * N_BASE_DMA)
            a.wait_ge(rpb_out, 16)
            for j in range(8):
                b = full_bank(("b", j))
                for dst, o, n, m in shift_parts(j):
                    ins = a.activation(dst, b[:, o:o + n], ACT.Copy, scale=mu2[:, 0, m:m + 1])
                ins.then_inc(shift_mid, 1)
            for j in range(2):
                take(("cq", j), cq[:, 2 * j:2 * j + 2, :], split=2)
            for j in range(4):
                take(("ck", j), ck[:, j, :])
            for j in range(4):
                take(("cv", j), cv[:, j, :])
            for q in range(2):
                for r in range(6):
                    src = bass.AP(tensor=rpb_dram.tensor, offset=(1 - q + r) * P, ap=[[1, 64], [7 * P, C_HEADS], [1, 64]])
                    a.dma_start(nhank[64 * q:64 * q + 64, :, r, :], src).then_inc(nhank_in, 16)
            for j in range(2):
                take(("kcT", j), kcT[:, j, :, :], split=2)
            wait_full2(a, ("nb", C_HEADS - 1))
            a.activation(nrot[:, :, :], cq[:, :, :], ACT.Square).then_inc(nsq_ready, 1)
            a.activation(nsq[:, :, :], ck[:, :, :], ACT.Square).then_inc(nsq_ready, 1)
            for j in range(2):
                take(("cross", j), ATx[:, j, :, :, :].rearrange("p d r s -> p (d r) s"), split=4)
            for t in range(2):
                take(("ho", t), ho[:, t, :], n=A_W)
                wait_emptied2(a, ("ho", t))
            a.activation(hsq[:, :, :], ho[:, :, :], ACT.Square).then_inc(hsq_ready, 1)
            a.wait_ge(hms_ready, 1)
            a.activation(st[:, 32:40], st[:, 32:40], ACT.Sqrt).then_inc(hroot_ready, 1)
            a.wait_ge(nms_ready, 1)
            a.activation(nL[:, :, :], nL[:, :, :], ACT.Sqrt).then_inc(nroot_ready, 1)
            a.activation(nrs[:, :, :], nrs[:, :, :], ACT.Sqrt).then_inc(nroot_ready, 1)
            for i in range(18):
                if i < 16:
                    o = 48 + 3 * (i % 4)
                    L = nL[:, i % 2, :]
                    a.wait_ge(nneg_ready, i + 1)
                    a.activation(L, L, ACT.Exp, bias=st[:, o:o + 1], accum_out=st[:, o + 1:o + 2]).then_inc(nprob_ready, 1)
                if 1 <= i < 17:
                    if i >= 3:
                        wait_full2(a, ("no", i - 3))
                    take(("nt", i - 1), nPT[:, (i - 1) % 2, :, :], split=4)
            a.activation(pB_w, pB_w, ACT.Tanh)
            a.activation(pB_g, pB_g, ACT.Sigmoid).then_inc(th_ready, 1)
            a.wait_ge(kn_ready, 1)
            a.activation(kk_sq[0], kk_sq[0], ACT.Sqrt)
            a.activation(kk_sq[1], kk_sq[1], ACT.Sqrt).then_inc(kroot_ready, 1)
            for pr in range(2):
                take(("vt", pr), vtk[:, pr, :, :], split=NCH)
            for stage, g in GROUP_STEPS:
                dr, pr = g // 2, g % 2
                w = work[pr]
                if stage == "gates":
                    for name, dst, vec in (("wz", w.sw, "rwkv_w0_2"), ("az", w.aa, "rwkv_a0_2")):
                        c = VEC2[vec][0] + g
                        b = full_bank((name, g))
                        a.activation(dst, b, ACT.Sigmoid, bias=cols2[:, c:c + 1]).then_inc(act_emptied2, 1)
                    if pr == 0:
                        continue
                    for i in range(2):
                        w = work[i]
                        a.wait_ge(exp_in, 2 * (2 * dr + i) + 1)
                        a.activation(w.tmp2[:, 0:S], w.cc[:, 0:S], ACT.Exp, scale=-DECAY)
                        a.activation(w.alp, w.cc, ACT.Exp, scale=DECAY)
                        a.activation(w.dend, w.cc[:, (CH - 1 if dr == 0 else 0)::CH], ACT.Exp, scale=-DECAY).then_inc(exp_out, 1)
                        a.wait_ge(exp_in, 2 * (2 * dr + i) + 2)
                        a.activation(w.kap, w.kap, ACT.Exp, scale=-DECAY)
                        kx = w.kapt[:, :, :].rearrange("p c t -> p (c t)")
                        a.activation(kx, kx, ACT.Exp, scale=DECAY).then_inc(exp_out, 1)
                elif stage == "products":
                    take(("tk", g), w.kapt[:, :, :], split=NCH)
                    take(("ta", g), w.alpt[:, :, :], split=NCH)
                    take(("tkk", g), w.kht[:, :, :], split=NCH)
                elif stage == "G":
                    take(("W2", g), w.W2[:, :, :], split=NCH)
                    take(("G", g), w.G[:, :, :], split=NCH)
                elif stage == "H":
                    b = full_bank(("H", g))
                    a.activation(Hn[:, g, :, :], b[:, 0:S].rearrange("p (c s) -> p c s", c=LCH), ACT.Copy, scale=-1.0)
                    take(("H", g), w.Hfull[:, :, :], scale=-1.0, split=NCH)
                elif stage == "Psi":
                    take(("PS", g), Psi[:, g, :, :], split=NCH)
                    take(("GT", g), GT[:, g, :, :], n=S, split=LCH)
                elif stage[0] == "M":
                    take(("T1", 8 * g + int(stage[-1])), w.T1[:, :, :], split=NCH)
            take(("y", 0), yb[:, :, :], split=8)
            take(("bon", 0), bo, n=8)
            take(("gg", 0), gg[:, :, :], split=8)
            wait_emptied2(a, ("y", 0))
            a.wait_ge(ycent_ready, 1)
            a.activation(ysq[:, :, :], yb[:, :, :], ACT.Square).then_inc(ysq_ready, 1)
            a.wait_ge(yms_ready, 1)
            a.activation(st[:, 32:40], st[:, 32:40], ACT.Sqrt).then_inc(yroot_ready, 1)
            take(("bT", 0), mixT[:, 2:4, :], split=2)
            for j in range(3):
                c = (0, 4, 6)[j]
                take(("mt", j), mixT[:, c:c + 2, :], split=2)
            a.wait_ge(h2_ready, 1)
            a.dma_start(moe_c, d["c2_moe"]).then_inc(moe_c_in, 16)
            squares2(3, h)
            root2(3)
            x2_evac("x3", lambda k: h2T[:, k, :], S, lambda k: mulT[:, 2, k:k + 1], lambda k: modT[:, 16 + k, 0:1])
            a.wait_ge(gexp_in, 1)
            a.activation(ge, ge, ACT.Exp)
            a.activation(ee, ee, ACT.Exp).then_inc(gexp_out, 1)
            a.wait_ge(rt_done, 1)
            sweeps = a.value_load(sweeps_i[0:1, 0:1], min_val=1, max_val=S // SLOTS_E)
            with a.Fori(0, sweeps) as sw_:
                with a.Fori(0, TURNS) as tn:
                    a.wait_ge(moe_full, turn(sw_, tn, 1, 8))
                    for i in range(4):
                        ins = a.activation(xg[:, i, :], banks8[0][:, i * P:(i + 1) * P], ACT.Identity,
                                           scale=mulT[:, 2, i:i + 1], bias=modT[:, 16 + i, 0:1])
                    ins.then_inc(xg_act, 1)
                    a.wait_ge(moe_full, turn(sw_, tn, 3, 8))
                    a.activation(putT[:, :, :].rearrange("p t s -> p (t s)"), banks8[7][:, 0:ST * P], ACT.Copy)
                    a.wait_ge(moe_used, used_by(sw_, tn, 2 * QUAD - 1))
                    a.activation(sg, banks8[2], ACT.Silu).then_inc(moe_sg, 1)
                    a.wait_ge(moe_full, turn(sw_, tn, 4, 8))
                    a.activation(hidT[:, :, :].rearrange("p k s -> p (k s)"), banks8[4], ACT.Copy).then_inc(hidT_ready, 1)
                    a.wait_ge(moe_used, used_by(sw_, tn, TURN_BLOCKS))
                    a.activation(yg[:, 0:512], banks8[5], ACT.Copy).then_inc(yg_act, 1)

        @block.vector
        def _(v):
            chain = Chain(v, dve_chain)
            v.memset(relb, NEG).then_inc(relb_set, 1)
            v.wait_ge(const_in, 80)
            v.memset(stats[:, :], 0.0).then_inc(relb_set, 1)
            v.wait_ge(tab_full, 1)
            for g in range(NG):
                ins = v.tensor_copy(tab[:, g, :], bank[g][0:HEADS_PER_GROUP, :])
                if g < NG - 1:
                    chain(ins)
            ins.then_inc(tab_ready, 1)
            v.wait_ge(h_in, 16)
            v.wait_ge(bias_ready, N_HEADS)
            v.memset(stats[:, 15:16], 0.0).then_inc(layer_done, 1)
            first = chain.n

            with v.Fori(0, DEPTH) as l:
                chain.base, chain.n = l * DVE_CHAIN + first, 0

                def norm(n):
                    v.wait_ge(sumsq, l * 4 + 2 * n + 2)
                    v.tensor_scalar(stats[:, 2:4], stats[:, 0:2], 1.0 / D, EPS, ALU.mult, ALU.add).then_inc(ms_ready, 1)
                    v.wait_ge(rms_ready, l * 2 + n + 1)
                    chain(v.reciprocal(stats[:, 12:14], stats[:, 4:6]))
                    for t in range(ST):
                        v.tensor_scalar(xs[:, t, :], h[:, t, :], stats[:, 12 + t:13 + t], None, ALU.mult)\
                            .then_inc(xs_ready, 1)

                def x_evac(name, vec):
                    for j in (1, 3):
                        b = bank[JOB[(name, j)] % 4]
                        wait_full(v, l, (name, j))
                        for kk in range(2):
                            k = 2 * j + kk
                            ins = v.tensor_scalar(xT[:, k, :], b[:, kk * S:(kk + 1) * S],
                                                  cols[:, vec + k:vec + k + 1], None, ALU.mult)
                        ins.then_inc(dve_emptied, 1)

                def split_weights(jobs, i):
                    if i >= len(jobs):
                        return
                    n = SPLIT[jobs[i]]
                    wait_block(v, l, jobs[i][0], jobs[i][1] // 2)
                    v.wait_ge(w_high_ready, l * len(SPLIT) + n + 1)
                    v.tensor_tensor(half_block(jobs[i], w_low), half_block(jobs[i], wring), w_high_r[:, n % 2, :, :].bitcast(F32),
                                    ALU.subtract).then_inc(w_low_ready, 1)

                def split_x(n):
                    v.wait_ge(x_high_ready, l * 2 + n + 1)
                    v.tensor_tensor(x_low_r[:, :, :], xT[:, :, :], x_high_r[:, :, :].bitcast(F32), ALU.subtract).then_inc(x_low_ready, 1)

                norm(0)
                for i in range(2):
                    split_weights(SPLIT_IN, i)
                v.wait_ge(cols_ready, l + 1)
                x_evac("x1", V_N1)
                wait_emptied(v, l, ("x1", 3))
                split_x(0)
                for i in range(2, len(SPLIT_IN)):
                    split_weights(SPLIT_IN, i)

                def logits(i):
                    hh, t = i // 2, i % 2
                    L = logit[:, i % 2, :]
                    o = 6 + 3 * (i % 2)
                    v.wait_ge(scores_full, l * 8 + i + 1)
                    if i >= 2:
                        v.wait_ge(probT_full, l * 8 + i - 1)
                    v.scalar_tensor_tensor(
                        L.rearrange("p (g s) -> p g s", s=S), ps_s[:, 0:NG * S].rearrange("p (g s) -> p g s", s=S),
                        HD ** -0.5, bias[:, hh::HEADS_PER_GROUP, P * (1 - t):P * (1 - t) + S],
                        ALU.mult, ALU.add).then_inc(logits_taken, 1)
                    v.wait_ge(logits_taken, l * 8 + i + 1)
                    chain(v.tensor_reduce(stats[:, 14:15], L, AX_X, ALU.max))
                    v.tensor_scalar(stats[:, o:o + 1], stats[:, 14:15], -1.0, None, ALU.mult).then_inc(neg_max, 1)
                    v.wait_ge(exp_done, l * 8 + i + 1)
                    v.reciprocal(stats[:, o + 2:o + 3], stats[:, o + 1:o + 2]).then_inc(rsum_ready, 1)

                def take_probT(i):
                    hh, t = i // 2, i % 2
                    v.wait_ge(probT_full, l * 8 + i + 1)
                    if hh >= 2 and t == 0:
                        wait_full(v, l, ("pv", hh - 2))
                    v.tensor_copy(probT[:, hh % 2, :, t * P:(t + 1) * P],
                                  ps_t[:, 0:NG * S].rearrange("p (k q) -> p k q", q=P)).then_inc(probT_ready, 1)

                for i in range(8):
                    logits(i)
                    if i:
                        take_probT(i - 1)
                take_probT(7)
                for j in range(4):
                    wait_full(v, l, ("wa", j))
                    v.scalar_tensor_tensor(mT[:, 2 * j:2 * j + 2, :].rearrange("p c s -> p (c s)"),
                                           gate[:, 2 * j:2 * j + 2, :].rearrange("p c s -> p (c s)"), 1.0,
                                           bank[JOB[("wa", j)] % 4][:, :], ALU.add, ALU.mult).then_inc(dve_emptied, 1)
                for j in range(4):
                    wait_full(v, l, ("wb", j))
                    tmp = logit[:, 0, 0:512]
                    chain(v.scalar_tensor_tensor(tmp, gate[:, KT + 2 * j:KT + 2 * j + 2, :].rearrange("p c s -> p (c s)"),
                                                 1.0, bank[JOB[("wb", j)] % 4][:, :], ALU.add, ALU.mult))
                    m = mT[:, 2 * j:2 * j + 2, :].rearrange("p c s -> p (c s)")
                    wait_emptied(v, l, ("wa", j))
                    v.tensor_tensor(m, m, tmp, ALU.add).then_inc(dve_emptied, 1)
                    wait_emptied(v, l, ("wb", j))
                for j in range(4):
                    half, t = j // 2, j % 2
                    wait_full(v, l, ("wo", j))
                    hv = h[:, t, half * 512:(half + 1) * 512]
                    v.scalar_tensor_tensor(hv, bank[JOB[("wo", j)] % 4][:, :], 0.5, hv, ALU.mult, ALU.add)\
                        .then_inc(dve_emptied, 1)
                norm(1)
                for i in range(2):
                    split_weights(SPLIT_UP, i)
                x_evac("x2", V_N2)
                wait_emptied(v, l, ("x2", 3))
                split_x(1)
                for j in range(11):
                    wait_full(v, l, ("up", j))
                    split_weights(SPLIT_UP, j + 2)
                    b = bank[JOB[("up", j)] % 4]
                    v.wait_ge(conv_mid, l * FT + 2 * j + 2)
                    for kk in range(2):
                        f = 2 * j + kk
                        c = V_CW + f
                        o = kk * S
                        chain(v.scalar_tensor_tensor(act[:, f, 1:S], b[:, o:o + S - 1], cols[:, c:c + 1],
                                                     act[:, f, 1:S], ALU.mult, ALU.add))
                        ins = v.scalar_tensor_tensor(act[:, f, 0:S - 1], b[:, o + 1:o + S],
                                                     cols[:, c + 2 * FT:c + 2 * FT + 1],
                                                     act[:, f, 0:S - 1], ALU.mult, ALU.add)
                    ins.then_inc(dve_emptied, 1)
                def split_down(i):
                    wait_block(v, l, "down", i // 2)
                    v.wait_ge(w_high_ready, l * len(SPLIT) + SPLIT[("down", i)] + 1)
                    v.tensor_tensor(down_rows(i, w_low), down_rows(i, wring), down_high(i).bitcast(F32), ALU.subtract)\
                        .then_inc(w_low_ready, 1)

                def split_act(i):
                    v.wait_ge(a_high_ready, l * N_DOWN + i + 1)
                    v.tensor_tensor(a_low[:, 2 * i:2 * i + 2, :], act[:, 2 * i:2 * i + 2, :], a_high(2 * i).bitcast(F32),
                                    ALU.subtract).then_inc(a_low_ready, 1)

                for j in range(11, FT):
                    wait_full(v, l, ("up", j))
                    if j + 2 < FT:
                        split_weights(SPLIT_UP, j + 2)
                    else:
                        split_down(j + 2 - FT)
                    v.wait_ge(gelu_ready, l * 11 + j - 10)
                    f = 2 * (j - 11)
                    av = act[:, f:f + 2, :].rearrange("p c s -> p (c s)")
                    v.tensor_tensor(av, bank[JOB[("up", j)] % 4][:, :], av, ALU.mult).then_inc(dve_emptied, 1)
                    if j > 11:
                        split_act(j - 12)
                split_act(N_DOWN - 1)
                for i in range(2, N_DOWN):
                    split_down(i)
                for j in range(4):
                    half, t = j // 2, j % 2
                    wait_full(v, l, ("down", j))
                    hv = h[:, t, half * 512:(half + 1) * 512]
                    v.tensor_tensor(hv, bank[JOB[("down", j)] % 4][:, :], hv, ALU.add).then_inc(dve_emptied, 1)
                wait_emptied(v, l, ("down", 3))
                v.memset(stats[:, 15:16], 0.0).then_inc(layer_done, 1)
                assert chain.n == DVE_CHAIN, chain.n


            chain.base, chain.n = first + DEPTH * DVE_CHAIN, 0

            def full_bank(job):
                wait_full2(v, job)
                return bank2(*job)

            def col(name, i, n=1):
                c = VEC2[name][0] + i
                return cols2[:, c:c + n]

            v.tensor_copy(cols2, full_bank(("vec", 0))[:, 0:N_VEC2]).then_inc(dve_emptied2, 1)
            wait_emptied2(v, ("vec", 0))
            v.wait_ge(csil_ready, 1)
            v.tensor_copy(csb[:, :, :], csil[:, :, 0:1].broadcast_to([P, KT, P])).then_inc(csb_ready, 1)
            chain(v.tensor_scalar(mu2[:, 0, :], col("rwkv_mu_2", 0, 9), -1.0, 1.0, ALU.mult, ALU.add))
            chain(v.tensor_scalar(mu2[:, 1, :], col("rwkv_mu_2", 0, 9), 0.5, None, ALU.mult))
            lg = col("hgrn_lb_logits_2", 0, 4)
            chain(v.tensor_tensor(lb[:, 0, :], lg, lg, ALU.subtract))
            v.wait_ge(base_in, 16 * N_BASE_DMA)
            chain(v.tensor_tensor(lb[:, 1, :], lb[:, 0, :], lb[:, 0, :], ALU.is_equal))
            chain(v.reciprocal(lb[:, 2, :], lb[:, 1, :]))
            chain(v.tensor_tensor(lb[:, 3, :], lb[:, 1, :], lb[:, 2, :], ALU.mult))
            chain(v.tensor_tensor(lb[:, 4, :], lb[:, 3, :], lb[:, 3, :], ALU.subtract))
            v.tensor_scalar(lb[:, 5, :], lb[:, 4, :], -1.0, 1.0, ALU.mult, ALU.add).then_inc(lb_ready, 1)
            chain(v.tensor_scalar(kam[:, 0:2], col("rwkv_k_a_2", 0, 2), -1.0, 1.0, ALU.mult, ALU.add))

            def inverse_rms(n, width=D):
                v.wait_ge(sumsq2, 2 * n + 2)
                v.tensor_scalar(st[:, 4 * n + 2:4 * n + 4], st[:, 4 * n:4 * n + 2], 1.0 / width, EPS, ALU.mult, ALU.add)\
                    .then_inc(ms2, 1)
                v.wait_ge(rms2, n + 1)
                chain(v.reciprocal(st[:, 24 + 2 * n:26 + 2 * n], st[:, 16 + 2 * n:18 + 2 * n]))

            def rs(n, t):
                return st[:, 24 + 2 * n + t:25 + 2 * n + t]

            inverse_rms(0)
            v.wait_ge(early_in, 64)
            for t in range(ST):
                v.scalar_tensor_tensor(h[:, t, :], h[:, t, :], rs(0, t), normf, ALU.mult, ALU.mult).then_inc(xl_ready, 1)
            inverse_rms(1)
            for t in range(ST):
                v.tensor_scalar(ctxb[:, t, :], ctxb[:, t, :], rs(1, t), None, ALU.mult).then_inc(ctx_ready, 1)
            inverse_rms(2)
            for t in range(ST):
                v.tensor_scalar(xs[:, t, :], h[:, t, :], rs(2, t), None, ALU.mult).then_inc(xs2_ready, 1)
            for n in range(12):
                b = full_bank(("ada", n))
                if n in ADA_ROWS:
                    g = gmul[:, n // 6, (n % 2) * 512:(n % 2) * 512 + 512]
                    v.tensor_tensor(g, b, g, ALU.add).then_inc(dve_emptied2, 1)
                else:
                    m = 4 * n if n < 4 else 4 * n - 8
                    v.tensor_copy(mod_rows[:, m * P:(m + 4) * P], b[0:2, :]).then_inc(dve_emptied2, 1)
            b = full_bank(("adaT", 0))[:, 0:64].rearrange("p (m c) -> p m c", c=2)
            for m, r in ((0, 0), (16, 24)):
                ins = v.tensor_tensor(modT[:, m:m + 16, :], b[:, m:m + 16, :],
                                      col("b_ada_2", r, 16).unsqueeze(2).broadcast_to([P, 16, 2]), ALU.add)
            ins.then_inc(dve_emptied2, 1)
            wait_emptied2(v, ("adaT", 0))
            for i, (m, c, name) in enumerate(((8, 0, "norm1_gain_2"), (8, 1, "norm1_gain_2"), (24, 0, "norm2_gain_2"))):
                ins = v.scalar_tensor_tensor(mulT[:, i, :], modT[:, m:m + 8, c], 1.0, col(name, 0, 8), ALU.add, ALU.mult)
                if i < 2:
                    chain(ins)
            ins.then_inc(mul_ready, 1)
            v.wait_ge(mul_ready, 1)

            def x2_evac(name, dst, mul, add):
                for j in (1, 3):
                    b = full_bank((name, j))
                    for kk_ in range(2):
                        k = 2 * j + kk_
                        ins = v.tensor_scalar(dst(k), b[:, kk_ * S:(kk_ + 1) * S], mul(k), add(k), ALU.mult, ALU.add)
                    ins.then_inc(dve_emptied2, 1)

            x2_evac("xl", lambda k: hT[:, k, 0:S], lambda k: mulT[:, 0, k:k + 1], lambda k: modT[:, k, 0:1])
            x2_evac("xc", lambda k: hT[:, k, S:T2], lambda k: mulT[:, 1, k:k + 1], lambda k: modT[:, k, 1:2])
            for j in range(8):
                b = full_bank(("b", j))
                v.wait_ge(shift_mid, j + 1)
                parts = shift_parts(j)
                for i, (dst, o, n, m) in enumerate(parts):
                    segs = n // S
                    dv = dst.rearrange("p (s t) -> p s t", t=S)
                    bv = b[:, o:o + n].rearrange("p (s t) -> p s t", t=S)
                    hm = mu2[:, 1, m:m + 1]
                    chain(v.scalar_tensor_tensor(dv[:, :, 1:S], bv[:, :, 0:S - 1], hm, dv[:, :, 1:S], ALU.mult, ALU.add))
                    ins = v.scalar_tensor_tensor(dv[:, :, 0:S - 1], bv[:, :, 1:S], hm, dv[:, :, 0:S - 1],
                                                 ALU.mult, ALU.add)
                    if i < len(parts) - 1:
                        chain(ins)
                ins.then_inc(dve_emptied2, 1)

            wait_full2(v, ("cv", 3))
            chain(v.memset(zeros, 0.0))
            v.memset(XS[:, :, CTX - 1:CTX], 1.0)
            chain(v.memset(XP[:, :, 0:1], 1.0))
            v.wait_ge(fk_ready, 1)
            for pr in range(2):
                chain(v.tensor_tensor_scan(XS[:, pr, 0:CTX - 1][:, ::-1], fF[:, pr, S + 1:T2][:, ::-1],
                                           zeros[:, 0:CTX - 1], 1.0, ALU.mult, ALU.add))
                chain(v.tensor_tensor_scan(XP[:, pr, 1:CTX], fB[:, pr, S:T2 - 1], zeros[:, 0:CTX - 1], 1.0,
                                           ALU.mult, ALU.add))
            v.tensor_tensor(Kd[:, 0, :, :], kF[:, :, S:T2], XS[:, :, :], ALU.mult).then_inc(kc_ready, 1)
            v.tensor_tensor(Kd[:, 1, :, :], kB[:, :, S:T2], XP[:, :, :], ALU.mult).then_inc(kc_ready, 1)
            v.tensor_tensor(Ksum[:, :, :], kF[:, :, 0:S], kB[:, :, 0:S], ALU.add).then_inc(ksum_ready, 1)
            v.wait_ge(kc_ready, 2)
            v.memset(XS[:, :, :], 1.0)
            v.memset(XP[:, :, :], 1.0).then_inc(xp_ready, 1)
            v.wait_ge(xp_ready, 1)
            wait_full2(v, ("kcT", 1))

            def level_f(n):
                if n:
                    wait_full2(v, ("lev", 4 * (n - 1) + 1) if n <= len(LEVELS) else ("cross", 1))
                if n <= len(LEVELS):
                    chain(v.tensor_tensor(Kd[:, 0, :, :], kF[:, :, 0:S], XS[:, :, :], ALU.mult))
                v.tensor_tensor(Qd[:, 0, :, :], aq[:, :, :], IP, ALU.mult).then_inc(lev_f, 1)
                v.wait_ge(lev_f, n + 1)
                if n <= len(LEVELS):
                    bw = 1 << n
                    x = XS[:, :, :].rearrange("p r (n h b) -> p r n h b", h=2, b=bw)
                    ip = IP.rearrange("p r (n h b) -> p r n h b", h=2, b=bw)
                    for r in range(2):
                        shape = [P, S // (2 * bw), bw]
                        chain(v.tensor_tensor(x[:, r, :, 0, :], x[:, r, :, 0, :],
                                              ip[:, r, :, 1, bw - 1:bw].broadcast_to(shape), ALU.mult))
                        chain(v.tensor_tensor(ip[:, r, :, 1, :], ip[:, r, :, 1, :],
                                              ip[:, r, :, 0, bw - 1:bw].broadcast_to(shape), ALU.mult))

            level_f(0)
            for j in range(2):
                b = full_bank(("hs", j))
                v.tensor_tensor(hst[:, j, :, :], b[:, 0:A_W].rearrange("p (r m) -> p r m", r=2),
                                ones_blk.unsqueeze(1).broadcast_to([P, 2, P]), ALU.mult).then_inc(dve_emptied2, 1)
            at3 = [AT[:, par, :, :, :].rearrange("p t r s -> p (t r) s") for par in range(2)]
            for par in range(2):
                b = full_bank(("diag", par))
                v.tensor_copy(at3[par], b.rearrange("p (h s) -> p h s", h=4)).then_inc(dve_emptied2, 1)
            wait_emptied2(v, ("diag", 1))
            for n in range(len(LEVELS)):
                level_f(n + 1)
                for j in range(4):
                    dr, par = j // 2, j % 2
                    job = ("lev", 4 * n + j)
                    if j >= 2 or n:
                        wait_emptied2(v, ("lev", 4 * n + j - 2) if j >= 2 else ("lev", 4 * (n - 1) + j + 2))
                    b = full_bank(job)
                    v.copy_predicated(at3[par], hg_mask[:, 2 * n + dr:2 * n + dr + 1, :].broadcast_to([P, 4, P]),
                                      b.rearrange("p (h s) -> p h s", h=4)).then_inc(dve_emptied2, 1)
            for j in range(C_HEADS):
                b = full_bank(("nb", j))
                v.tensor_tensor(nbias[:, j, :, :], b[:, 0:384].rearrange("p (r c) -> p r c", r=6),
                                win.unsqueeze(1).broadcast_to([P, 6, 64]), ALU.add).then_inc(dve_emptied2, 1)
            level_f(len(LEVELS) + 1)
            v.wait_ge(hsq_ready, 1)
            chain(v.tensor_reduce(st[:, 32:40], hsq[:, :, :].rearrange("p t (h d) -> p (t h) d", d=64), AX_X, ALU.add))
            v.tensor_scalar(st[:, 32:40], st[:, 32:40], 1.0 / 64, EPS, ALU.mult, ALU.add).then_inc(hms_ready, 1)
            v.wait_ge(hroot_ready, 1)
            chain(v.reciprocal(st[:, 32:40], st[:, 32:40]))
            hv = ho[:, :, :].rearrange("p t (h d) -> p (t h) d", d=64)
            chain(v.tensor_tensor(hv, hv, st[:, 32:40].unsqueeze(2).broadcast_to([P, 8, 64]), ALU.mult))
            chain(v.tensor_tensor(ho[:, :, :], ho[:, :, :], hgain.unsqueeze(1).broadcast_to([P, ST, A_W]), ALU.mult))
            v.tensor_tensor(mixtok[:, :, 0:A_W], ho[:, :, :], ag[:, :, :], ALU.mult).then_inc(mixa_ready, 1)
            v.wait_ge(mixa_ready, 1)

            for j in range(6):
                b = full_bank(("qs", j))
                dst = nL[:, j, :] if j < 2 else nrs[:, j - 2, :]
                v.tensor_scalar(dst, b, 1.0 / 64, EPS, ALU.mult, ALU.add).then_inc(dve_emptied2, 1)
            wait_emptied2(v, ("qs", 5))
            v.memset(st[:, 63:64], 0.0).then_inc(nms_ready, 1)
            for i, (x, r, name, n) in enumerate(((cq, nL, "na_q_gain_2", 1024), (ck, nrs, "na_k_gain_2", 2048))):
                v.wait_ge(nroot_ready, i + 1)
                rf = r[:, :, :].rearrange("p a b -> p (a b)")
                xf = x[:, :, :].rearrange("p a b -> p (a b)")
                chain(v.reciprocal(rf, rf))
                v.scalar_tensor_tensor(xf, xf, col(name, 0), rf, ALU.mult, ALU.mult).then_inc(qk_normed, 1)
            v.wait_ge(qk_normed, 2)
            for j in range(4):
                x = (cq, cq, ck, ck)[j][:, 2 * (j % 2):2 * (j % 2) + 2, 0:S]
                tr = nrot[:, 0:2, :]
                b = full_bank(("rope", j)).rearrange("p (i s) -> p i s", i=2)
                chain(v.tensor_tensor(tr, b, sin.unsqueeze(1).broadcast_to([P, 2, S]), ALU.mult))
                chain(v.tensor_tensor(x, x, cos.unsqueeze(1).broadcast_to([P, 2, S]), ALU.mult))
                v.tensor_tensor(x, x, tr, ALU.add).then_inc(dve_emptied2, 1)
                wait_emptied2(v, ("rope", j))
            v.memset(st[:, 63:64], 0.0).then_inc(qk_turned, 1)
            for i in range(18):
                if i < 16:
                    hd, t = i // 2, i % 2
                    o = 48 + 3 * (i % 4)
                    b = full_bank(("ns", i))
                    if i >= 2:
                        wait_full2(v, ("nt", i - 2))
                    L = nL[:, i % 2, :]
                    r0 = 2 * (1 - t)
                    chain(v.scalar_tensor_tensor(L[:, 0:S], b[:, 0:S], H2 ** -0.5,
                                                 nbias[:, hd, r0:r0 + 4, :].rearrange("p r c -> p (r c)"),
                                                 ALU.mult, ALU.add))
                    v.tensor_scalar(L[:, S:T2], b[:, S:T2], H2 ** -0.5, None, ALU.mult).then_inc(dve_emptied2, 1)
                    wait_emptied2(v, ("ns", i))
                    chain(v.tensor_reduce(st[:, o + 2:o + 3], L, AX_X, ALU.max))
                    v.tensor_scalar(st[:, o:o + 1], st[:, o + 2:o + 3], -1.0, None, ALU.mult).then_inc(nneg_ready, 1)
                if i >= 2:
                    hd, t = (i - 2) // 2, i % 2
                    o = 48 + 3 * ((i - 2) % 4)
                    v.wait_ge(nprob_ready, i - 1)
                    chain(v.reciprocal(st[:, o + 2:o + 3], st[:, o + 1:o + 2]))
                    b = full_bank(("no", i - 2))
                    v.tensor_scalar(mixtok[:, t, A_W + 64 * hd:A_W + 64 * hd + 64], b[:, 0:64], st[:, o + 2:o + 3], None,
                                    ALU.mult).then_inc(dve_emptied2, 1)
            for pr in range(2):
                chain(v.tensor_scalar(kunit[:, pr, :], pB_k[:, pr, :], col("rwkv_kk_scale_2", pr), None, ALU.mult))
                chain(v.tensor_tensor(kk_sq[pr], kunit[:, pr, :], kunit[:, pr, :], ALU.mult))
            v.memset(st[:, 63:64], 0.0).then_inc(kksq_ready, 1)
            for pr in range(2):
                v.tensor_scalar(kk_sq[pr], full_bank(("kn", pr)), 1e-24, None, ALU.max).then_inc(dve_emptied2, 1)
            wait_emptied2(v, ("kn", 1))
            v.memset(st[:, 63:64], 0.0).then_inc(kn_ready, 1)
            v.memset(reset[:, :, :], 1.0)
            chain(v.memset(states[:, 0, :, :], 0.0))
            v.memset(st[:, 63:64], 0.0).then_inc(reset_ready, 1)
            v.wait_ge(reset_ready, 1)
            rv = reset.rearrange("p d (c t) -> p d c t", t=CH)
            chain(v.memset(rv[:, 0, :, 0:1], 0.0))
            chain(v.memset(rv[:, 1, :, CH - 1:CH], 0.0))
            v.wait_ge(kroot_ready, 1)
            for pr in range(2):
                t_ = kk_sq[pr]
                chain(v.reciprocal(t_, t_))
                chain(v.tensor_tensor(kunit[:, pr, :], kunit[:, pr, :], t_, ALU.mult))
            def mask(m, dr, n=NCH):
                return rw_mask[:, 9 * dr + m:9 * dr + m + 1, :].broadcast_to([P, n, 64])

            def b3(job):
                return full_bank(job).rearrange("p (c t) -> p c t", t=64)

            idb = id64.unsqueeze(1).broadcast_to([P, NCH, 64])
            for stage, g in GROUP_STEPS:
                dr, pr = g // 2, g % 2
                w = work[pr]
                if stage == "gates":
                    wait_emptied2(v, ("az", g))
                    rm, cc3 = reset[:, dr, :], w.cc.rearrange("p (c t) -> p c t", t=CH)
                    if dr == 0:
                        v.tensor_tensor_scan(w.cc, rm, w.sw, 0.0, ALU.mult, ALU.add).then_inc(exp_in, 1)
                    else:
                        v.tensor_tensor_scan(w.cc[:, ::-1], rm[:, ::-1], w.sw[:, ::-1], 0.0, ALU.mult, ALU.add)\
                            .then_inc(exp_in, 1)
                    v.wait_ge(exp_in, 2 * g + 1)
                    chain(v.tensor_tensor(w.kap, w.cc, w.sw, ALU.subtract))
                    e = CH - 1 if dr == 0 else 0
                    v.tensor_tensor(w.kapt[:, :, :], cc3, cc3[:, :, e:e + 1].broadcast_to([P, NCH, CH]), ALU.subtract)\
                        .then_inc(exp_in, 1)
                    chain(v.tensor_scalar(w.tmp1, w.aa, col("rwkv_k_a_2", pr), kam[:, pr:pr + 1], ALU.mult, ALU.add))
                    chain(v.tensor_tensor(w.tmp1, w.tmp1, pB_k[:, pr, :], ALU.mult))
                    if dr == 0:
                        chain(v.tensor_copy(ksum[:, pr, :], w.tmp1[:, 0:S]))
                    else:
                        chain(v.tensor_tensor(ksum[:, pr, :], ksum[:, pr, :], w.tmp1[:, 0:S], ALU.add))
                    chain(v.tensor_tensor(w.aa, w.aa, kunit[:, pr, :], ALU.mult))
                    if pr == 0:
                        continue
                    for i in range(2):
                        w, gi = work[i], 2 * dr + i
                        v.wait_ge(exp_out, 2 * gi + 1)
                        chain(v.tensor_tensor(rh[:, gi, :], pB_r[:, i, :], w.tmp2[:, 0:S], ALU.mult))
                        chain(v.tensor_tensor(w.kh, w.tmp1, w.alp, ALU.mult))
                        chain(v.tensor_tensor(w.alp, w.aa, w.alp, ALU.mult))
                        v.wait_ge(exp_out, 2 * gi + 2)
                        chain(v.tensor_tensor(w.kap, w.kap, kunit[:, i, :], ALU.mult))
                        kx = w.kapt[:, :, :].rearrange("p c t -> p (c t)")
                        chain(v.tensor_tensor(w.aa, w.aa, kx, ALU.mult))
                        v.tensor_tensor(w.tmp1, w.tmp1, kx, ALU.mult).then_inc(group_ready, 1)
                elif stage == "products":
                    v.tensor_tensor(w.LT[:, :, :], b3(("LT", g)), mask(0, dr), ALU.mult).then_inc(dve_emptied2, 1)
                    wait_emptied2(v, ("LT", g))
                    v.tensor_tensor(w.MT[:, :, :], w.LT[:, :, :], mask(2, dr), ALU.mult).then_inc(m0_done, 1)
                    chain(v.tensor_tensor(w.X[:, :, :], b3(("L1", g)), mask(8, dr), ALU.mult))
                    v.wait_ge(m0_done, g + 1)
                    chain(v.tensor_tensor(w.XT[:, :, :], idb, w.MT[:, :, :], ALU.subtract))
                    v.tensor_tensor(w.X[:, :, :], idb, w.X[:, :, :], ALU.subtract).then_inc(dve_emptied2, 1)
                    wait_emptied2(v, ("L1", g))
                    v.tensor_tensor(w.MT[:, :, :], w.LT[:, :, :], mask(3, dr), ALU.mult).then_inc(mt_ready, 1)
                    v.tensor_tensor(w.M2T[:, :, :], b3(("M2T", g)), mask(0, dr), ALU.mult).then_inc(dve_emptied2, 1)
                    v.tensor_tensor(NN[:, g, :, :, :].rearrange("p a c t -> p (a c) t"), b3(("NN", g)), mask(1, dr), ALU.mult)\
                        .then_inc(dve_emptied2, 1)
                elif stage == "H":
                    chain(v.tensor_tensor(PhiT[:, g, :, :], idb, w.dend.unsqueeze(2).broadcast_to([P, NCH, 64]), ALU.mult))
                    v.tensor_tensor(PhiT[:, g, :, :], PhiT[:, g, :, :], b3(("PH", g)), ALU.subtract)\
                        .then_inc(dve_emptied2, 1)
                    wait_emptied2(v, ("PH", g))
                elif stage[0] == "M" and stage != "MX5":
                    n = int(stage[-1])
                    wait_full2(v, ("T1", 8 * g + n))
                    v.tensor_tensor(w.MT[:, :, :], w.LT[:, :, :], mask(3 + n, dr), ALU.mult)
                elif stage[0] == "X":
                    n = int(stage[-1])
                    if n < 5:
                        v.tensor_tensor(w.X[:, :, :], w.X[:, :, :], b3(("XU", 8 * g + n)), ALU.subtract)\
                            .then_inc(dve_emptied2, 1)
                    v.tensor_tensor(w.XT[:, :, :], w.XT[:, :, :], b3(("XTU", 8 * g + n)), ALU.subtract)\
                        .then_inc(dve_emptied2, 1)
                    wait_emptied2(v, ("XTU", 8 * g + n))
                    if n < 5:
                        v.memset(st[:, 63:64], 0.0).then_inc(mt_ready, 1)
            wait_emptied2(v, ("GT", 3))
            for dr in range(2):
                c = step_chunks(0)[dr]
                ins = v.tensor_copy(states[:, 1, 2 * dr:2 * dr + 2, :], Psi[:, 2 * dr:2 * dr + 2, c, :])
                if dr == 0:
                    chain(ins)
            ins.then_inc(state_ready, 1)
            for i in range(1, 7):
                b = full_bank(("st", i))[:, 0:256].rearrange("p (g t) -> p g t", g=4)
                for dr in range(2):
                    c = step_chunks(i)[dr]
                    ins = v.tensor_tensor(states[:, i + 1, 2 * dr:2 * dr + 2, :], b[:, 2 * dr:2 * dr + 2, :],
                                          Psi[:, 2 * dr:2 * dr + 2, c, :], ALU.add)
                    if dr == 0:
                        chain(ins)
                ins.then_inc(dve_emptied2, 1)
            for dr in range(2):
                v.tensor_tensor(nSA[:, 2 * dr:2 * dr + 2, :, :], Hn[:, 2 * dr:2 * dr + 2, :, :],
                                full_bank(("sa", dr)).rearrange("p (g c t) -> p g c t", g=2, c=LCH), ALU.subtract)\
                    .then_inc(dve_emptied2, 1)
            for pr in range(2):
                chain(v.scalar_tensor_tensor(ksum[:, pr, :], ksum[:, pr, :], col("rwkv_r_k_2", pr), pB_r[:, pr, :],
                                             ALU.mult, ALU.mult))
            v.memset(st[:, 63:64], 0.0).then_inc(bonus_in, 1)
            yv = yb[:, :, :]
            s8 = lambda x: x.unsqueeze(2).broadcast_to([P, 8, 64])
            g4 = lambda x: x.unsqueeze(2).broadcast_to([P, 2, LCH, 64])
            y4 = yv.rearrange("p (r c) t -> p r c t", r=2)
            wait_emptied2(v, ("gg", 0))
            chain(v.tensor_reduce(st[:, 48:56], yv, AX_X, ALU.add))
            chain(v.tensor_scalar(st[:, 48:56], st[:, 48:56], 1.0 / 64, None, ALU.mult))
            v.tensor_tensor(yv, yv, s8(st[:, 48:56]), ALU.subtract).then_inc(ycent_ready, 1)
            v.wait_ge(ysq_ready, 1)
            chain(v.tensor_reduce(st[:, 32:40], ysq[:, :, :], AX_X, ALU.add))
            v.tensor_scalar(st[:, 32:40], st[:, 32:40], 1.0 / 64, LN_EPS, ALU.mult, ALU.add).then_inc(yms_ready, 1)
            v.wait_ge(yroot_ready, 1)
            chain(v.reciprocal(st[:, 32:40], st[:, 32:40]))
            chain(v.tensor_tensor(yv, yv, s8(st[:, 32:40]), ALU.mult))
            for r in range(2):
                chain(v.tensor_tensor(y4[:, r, :, :], y4[:, r, :, :], lng[:, r:r + 1, :].broadcast_to([P, LCH, 64]), ALU.mult))
                chain(v.tensor_tensor(y4[:, r, :, :], y4[:, r, :, :], lnb[:, r:r + 1, :].broadcast_to([P, LCH, 64]), ALU.add))
                chain(v.tensor_tensor(ysq[:, 4 * r:4 * r + 4, :], vtk[:, r, 0:LCH, :],
                                      bo[:, 4 * r:4 * r + 4].unsqueeze(2).broadcast_to([P, LCH, 64]), ALU.mult))
            chain(v.tensor_tensor(yv, yv, ysq[:, :, :], ALU.add))
            v.tensor_tensor(yv, yv, gg[:, :, :], ALU.mult).then_inc(yb_ready, 1)

            for j in range(4):
                half, t = j // 2, j % 2
                tm = mixtok[:, :, :].rearrange("p t n -> p (t n)")[:, 0:512]
                c = slice(half * 512, half * 512 + 512)
                chain(v.tensor_tensor(tm, full_bank(("wout", j)), gmul[:, 0, c], ALU.mult))
                v.tensor_tensor(h[:, t, c], h[:, t, c], tm, ALU.add).then_inc(dve_emptied2, 1)
                wait_emptied2(v, ("wout", j))
            v.memset(st[:, 63:64], 0.0).then_inc(h2_ready, 1)
            inverse_rms(3)
            for t in range(ST):
                v.tensor_scalar(xs[:, t, :], h[:, t, :], rs(3, t), None, ALU.mult).then_inc(xs3_ready, 1)
            x2_evac("x3", lambda k: h2T[:, k, :], lambda k: mulT[:, 2, k:k + 1], lambda k: modT[:, 16 + k, 0:1])
            v.tensor_tensor(rl[:, :, :], full_bank(("rt", 0))[:, 0:72].rearrange("p (t n) -> p t n", t=2),
                            rbias[:, 0:36].unsqueeze(1).broadcast_to([P, ST, 36]), ALU.add).then_inc(dve_emptied2, 1)
            wait_emptied2(v, ("rt", 0))
            gl, el = rl[:, :, 0:MG], rl[:, :, MG:36].rearrange("p t (g e) -> p t g e", g=MG)

            def b2(x, n):
                return x.unsqueeze(2).broadcast_to([P, ST, n])

            def first_max(dst, src, mx, n):
                chain(v.tensor_reduce(mx, src, AX_X, ALU.max))
                chain(v.tensor_tensor(dst, src, b2(mx, n), ALU.is_equal))
                chain(v.tensor_tensor(dst, dst, order[:, 8 - n:8].unsqueeze(1).broadcast_to([P, ST, n]), ALU.mult))
                chain(v.tensor_reduce(m2, dst, AX_X, ALU.max))
                chain(v.tensor_tensor(dst, dst, b2(m2, n), ALU.is_equal))

            for i in range(8):
                chain(v.memset(order[:, i:i + 1], float(8 - i)))
            first_max(gsel, gl, gmx, MG)
            chain(v.tensor_tensor(ge, gl, b2(gmx, MG), ALU.subtract))
            for t in range(ST):
                chain(v.tensor_tensor(esel[:, t, :, :], el[:, t, :, :],
                                      gsel[:, t, :].unsqueeze(2).broadcast_to([P, MG, PER_GROUP]), ALU.mult))
            chain(v.tensor_reduce(eg, esel[:, :, :, :].rearrange("p t g e -> p t e g"), AX_X, ALU.add))
            first_max(sel1, eg, emx, PER_GROUP)
            chain(v.tensor_tensor(ee, eg, b2(emx, PER_GROUP), ALU.subtract))
            v.scalar_tensor_tensor(eg, sel1, NEG, eg, ALU.mult, ALU.add).then_inc(gexp_in, 1)
            v.wait_ge(gexp_in, 1)
            first_max(sel2, eg, emx, PER_GROUP)
            chain(v.tensor_tensor(sel1, sel1, sel2, ALU.add))
            v.wait_ge(gexp_out, 1)
            chain(v.tensor_reduce(gmx, ge, AX_X, ALU.add))
            chain(v.reciprocal(gmx, gmx))
            chain(v.tensor_reduce(emx, ee, AX_X, ALU.add))
            chain(v.reciprocal(emx, emx))
            chain(v.tensor_tensor(ee, ee, b2(emx, PER_GROUP), ALU.mult))
            chain(v.tensor_tensor(ee, ee, sel1, ALU.mult))
            chain(v.tensor_reduce(emx, ee, AX_X, ALU.add))
            chain(v.reciprocal(emx, emx))
            chain(v.tensor_tensor(emx, emx, gmx, ALU.mult))
            chain(v.tensor_tensor(ee, ee, b2(emx, PER_GROUP), ALU.mult))
            for t in range(ST):
                chain(v.tensor_tensor(comb[:, t, :].rearrange("p (g e) -> p g e", g=MG),
                                      gsel[:, t, :].unsqueeze(2).broadcast_to([P, MG, PER_GROUP]),
                                      ee[:, t, :].unsqueeze(1).broadcast_to([P, MG, PER_GROUP]), ALU.mult))
            v.tensor_scalar(sel[:, :, :], comb[:, :, :], 0.0, None, ALU.is_gt).then_inc(sel_ready, 1)
            v.wait_ge(sel_ready, 1)
            b = full_bank(("pos", 0))
            chain(v.scalar_tensor_tensor(posm[:, :, :], b[:, 0:2 * N_EXP].rearrange("p (t e) -> p t e", t=ST), 1.0,
                                         sel[:, :, :], ALU.add, ALU.mult))
            chain(v.tensor_scalar(posm[:, :, :], posm[:, :, :], -1.0, None, ALU.add))
            v.tensor_copy(counts, b[:, 2 * N_EXP:3 * N_EXP]).then_inc(dve_emptied2, 1)
            wait_emptied2(v, ("pos", 0))
            chain(v.tensor_reduce(most, counts, AX_X, ALU.max))
            chain(v.tensor_scalar(over, sweep_from, most, None, ALU.is_lt))
            chain(v.tensor_reduce(sweeps_f, over, AX_X, ALU.add))
            chain(v.tensor_copy(sweeps_i, sweeps_f))
            v.memset(y[:, :, :], 0.0).then_inc(rt_done, 1)
            v.wait_ge(rt_done, 1)
            second = chain.base + chain.n
            sweeps = v.value_load(sweeps_i[0:1, 0:1], min_val=1, max_val=S // SLOTS_E)
            per_sweep = TURNS * MOE_CHAIN + 1

            def of_quad(x):
                return x.unsqueeze(2).broadcast_to([P, QUAD, SLOTS_E])

            slots = slot_no.unsqueeze(1).broadcast_to([P, QUAD, SLOTS_E])
            with v.Fori(0, sweeps) as sw_:
                with v.Fori(0, TURNS) as tn:
                    chain.base, chain.n = sw_ * per_sweep + tn * MOE_CHAIN + second, 0
                    chain(v.tensor_copy(ccol[:, :, :], comb[:, :, bass.ds(tn * QUAD, QUAD)]))
                    chain(v.tensor_copy(pcol[:, :, :], posm[:, :, bass.ds(tn * QUAD, QUAD)]))
                    for t in range(ST):
                        ins = v.tensor_tensor(pick[:, t, :].rearrange("p (u s) -> p u s", u=QUAD), slots,
                                              of_quad(pcol[:, t, :]), ALU.is_equal)
                    chain(ins)
                    for t in range(ST):
                        ins = v.tensor_tensor(put[:, t, :].rearrange("p (u s) -> p u s", u=QUAD),
                                              pick[:, t, :].rearrange("p (u s) -> p u s", u=QUAD),
                                              of_quad(ccol[:, t, :]), ALU.mult)
                    ins.then_inc(disp_ready, 1)
                    v.wait_ge(moe_full, turn(sw_, tn, 2, 8))
                    for i in range(4):
                        ins = v.tensor_scalar(xg[:, 4 + i, :], banks8[1][:, i * P:(i + 1) * P], mulT[:, 2, 4 + i:5 + i],
                                              modT[:, 20 + i, 0:1], ALU.mult, ALU.add)
                    ins.then_inc(xg_dve, 1)
                    v.wait_ge(moe_used, used_by(sw_, tn, 2 * QUAD))
                    v.wait_ge(moe_sg, turn(sw_, tn, 1, 1))
                    v.tensor_tensor(hid, banks8[3], sg, ALU.mult).then_inc(moe_hid, 1)
                    v.wait_ge(moe_used, used_by(sw_, tn, TURN_BLOCKS))
                    v.tensor_copy(yg[:, 512:1024], banks8[6]).then_inc(yg_dve, 1)
                    for j in range(4):
                        half, t = j // 2, j % 2
                        yv = y[:, t, half * 512:half * 512 + 512]
                        v.wait_ge(moe_full, turn(sw_, tn, 5 + j, 8))
                        ins = v.tensor_tensor(yv, yv, banks8[BACK[j]], ALU.add)
                    chain(ins)
                    assert chain.n == MOE_CHAIN
                chain.base, chain.n = sw_ * per_sweep + TURNS * MOE_CHAIN + second, 0
                chain(v.tensor_scalar(posm[:, :, :], posm[:, :, :], -float(SLOTS_E), None, ALU.add))
            for t in range(ST):
                chain.base, chain.n = sweeps * per_sweep + second, t
                chain(v.tensor_tensor(ob[:, t, :], y[:, t, :], gmul[:, 1, :], ALU.mult))
                v.tensor_tensor(ob[:, t, :], ob[:, t, :], h[:, t, :], ALU.add).then_inc(out_ready, 1)

        @block.gpsimd
        def _(g_eng):
            g_eng.memset(upad[:, :, :], 0.0).then_inc(pads_zero, 1)
            chain = Chain(g_eng, pool_chain)
            g_eng.wait_ge(const_in, 80)
            with g_eng.Fori(0, DEPTH) as l:
                chain.base, chain.n = l * POOL_CHAIN, 0
                wait_emptied(g_eng, l, ("u", 3))
                for g, window in enumerate(POOL_WINDOWS):
                    u = upad[:, 2 * g:2 * g + 2, :]
                    src, w, n = u, 1, 0
                    while w < window:
                        dst = (poolA, poolB)[n % 2]
                        m = UW - 2 * w + 1
                        chain(g_eng.tensor_tensor(dst[:, :, 0:m], src[:, :, 0:m], src[:, :, w:w + m], ALU.add))
                        src, w, n = dst, 2 * w, n + 1
                    o = PAD - window // 2
                    dst = (poolA, poolB)[n % 2]
                    chain(g_eng.tensor_tensor(dst[:, :, 0:S], src[:, :, o:o + S],
                                              inv[:, g:g + 1, :].broadcast_to([P, 2, S]), ALU.mult))
                    ins = g_eng.tensor_tensor(poolT[:, 2 * g:2 * g + 2, :], dst[:, :, 0:S], u[:, :, PAD:PAD + S],
                                              ALU.subtract)
                    if g < 3:
                        chain(ins)
                ins.then_inc(pooled, 1)
                assert chain.n == POOL_CHAIN, chain.n

            g_eng.wait_ge(layer_done, DEPTH + 1)
            g_eng.memset(rstage[:, :, :], 0.0).then_inc(rstage_zero, 1)
            g_eng.memset(st[:, 61:62], 0.0).then_inc(moe_used, SLOTS)
            chain.base, chain.n = DEPTH * POOL_CHAIN, 0
            g_eng.wait_ge(base_in, 16 * N_BASE_DMA)
            g_eng.tensor_copy(hg_mask.rearrange("p m t -> p (m t)"), mask_stage).then_inc(mask_ready, 1)
            g_eng.wait_ge(lb_ready, 1)
            for dr, (name, f, kx) in enumerate((("ff", fF, kF), ("fb", fB, kB))):
                for j in range(2):
                    wait_emptied2(g_eng, (name, j))
                    low, rest = lb[:, 4, 2 * dr + j:2 * dr + j + 1], lb[:, 5, 2 * dr + j:2 * dr + j + 1]
                    chain(g_eng.tensor_scalar(f[:, j, :], f[:, j, :], rest, low, ALU.mult, ALU.add))
                    chain(g_eng.tensor_scalar(f[:, j, :], f[:, j, :], F_FLOOR, None, ALU.max))
                    ins = g_eng.tensor_scalar(kx[:, j, :], kx[:, j, :], rest, None, ALU.mult)
                    if (dr, j) != (1, 1):
                        chain(ins)
            ins.then_inc(fk_ready, 1)
            g_eng.wait_ge(fk_ready, 1)
            g_eng.wait_ge(xp_ready, 1)
            wait_full2(g_eng, ("kcT", 1))
            for n in range(len(LEVELS) + 2):
                if n:
                    wait_full2(g_eng, ("lev", 4 * (n - 1) + 3) if n <= len(LEVELS) else ("cross", 1))
                if n <= len(LEVELS):
                    chain(g_eng.tensor_tensor(Kd[:, 1, :, :], kB[:, :, 0:S], XP[:, :, :], ALU.mult))
                g_eng.tensor_tensor(Qd[:, 1, :, :], aq[:, :, :], IS, ALU.mult).then_inc(lev_b, 1)
                g_eng.wait_ge(lev_b, n + 1)
                if n <= len(LEVELS):
                    bw = 1 << n
                    x = XP[:, :, :].rearrange("p r (n h b) -> p r n h b", h=2, b=bw)
                    ip = IS.rearrange("p r (n h b) -> p r n h b", h=2, b=bw)
                    for r in range(2):
                        shape = [P, S // (2 * bw), bw]
                        chain(g_eng.tensor_tensor(x[:, r, :, 1, :], x[:, r, :, 1, :],
                                                  ip[:, r, :, 0, 0:1].broadcast_to(shape), ALU.mult))
                        chain(g_eng.tensor_tensor(ip[:, r, :, 0, :], ip[:, r, :, 0, :],
                                                  ip[:, r, :, 1, 0:1].broadcast_to(shape), ALU.mult))


INPUTS = ["x", "w_in", "w_pool", "pool_scale", "w_a", "w_b", "w_o", "norm1", "norm2", "w_up", "conv_w", "conv_b", "w_down",
          "rel_bias", "norm_f", "c_2", "ctx_2", "c_ctx_2", "norm1_gain_2", "norm2_gain_2", "w_ada_2", "b_ada_2", "w_in_2",
          "w_out_2", "hgrn_lb_logits_2", "hgrn_gn_gain_2", "rwkv_mu_2", "rwkv_w0_2", "rwkv_w_up_2", "rwkv_a0_2",
          "rwkv_a_up_2", "rwkv_g_up_2", "rwkv_kk_scale_2", "rwkv_k_a_2", "rwkv_r_k_2", "rwkv_ln_gain_2",
          "rwkv_ln_bias_2", "na_q_gain_2", "na_k_gain_2", "na_rpb_2", "w_router_group_2", "b_router_group_2",
          "w_router_expert_2", "b_router_expert_2", "w_exp_gate_2", "w_exp_up_2", "w_exp_down_2"]


def kernel(**inputs):
    import concourse.bacc as bacc
    from concourse.bass_utils import run_bass_kernel_spmd

    nc = bacc.Bacc("TRN2", target_bir_lowering=False, num_devices=1)
    arrays = {name: np.ascontiguousarray(inputs[name]) for name in INPUTS}
    arrays.update(first_constants())
    arrays.update(second_constants())
    views = {name: nc.dram_tensor(name, a.shape, mybir.dt.from_np(a.dtype), kind="ExternalInput").ap()
             for name, a in arrays.items()}
    out = nc.dram_tensor("out", (1, S, D), F32, kind="ExternalOutput").ap()
    build(nc, views, out)
    result = run_bass_kernel_spmd(nc, [arrays], core_ids=[0])
    return result.results[0]["out"]
```
